# Optimizing a Trainium2 kernel written in Bass

```python
import jax, jax.numpy as jnp
from jax import lax
import numpy as np

D_MODEL = 1024
BATCH = 1
SEQ = 1024
DEPTH = 2

HG_WIDTH = D_MODEL // 2
HG_DK = 128
HG_HEADS = HG_WIDTH // HG_DK
HG_CHUNK = 64
RW_WIDTH = D_MODEL // 2
RW_HEAD = 64
RW_HEADS = RW_WIDTH // RW_HEAD
RW_DECAY_RANK = 64
RW_ICL_RANK = 64
RW_VRES_RANK = 32
N_BRANCH = 2
HG_COLS = 4 * HG_WIDTH
RW_COLS = 4 * RW_WIDTH + RW_DECAY_RANK + RW_ICL_RANK
GATE_COLS = N_BRANCH * D_MODEL
N_IN = HG_COLS + RW_COLS + GATE_COLS
DN_ALPHA = (2 * DEPTH) ** 0.25
DN_BETA = (8 * DEPTH) ** -0.25
LN_EPS = 1e-5
RMS_EPS = 1e-6
GN_EPS = 64e-5
L2_EPS = 1e-12
LB_FLOOR = 1e-30


def layer_norm(x, g, b):
    xf = x.astype(jnp.float32)
    mu = xf.mean(-1, keepdims=True)
    var = jnp.mean(jnp.square(xf - mu), -1, keepdims=True)
    return ((xf - mu) * lax.rsqrt(var + LN_EPS)).astype(x.dtype) * g + b

def heads(t, n):
    return t.reshape(t.shape[:-1] + (-1, n))

def token_shift(p, mu):
    prev = jnp.pad(p[:, :-1], ((0, 0), (1, 0), (0, 0)))
    return p + (prev - p) * mu

def hgrn2_chunked(q, k, v, log_f):
    B, T, H, K = q.shape
    V = v.shape[-1]
    C = HG_CHUNK
    N = T // C

    def to_chunks(a):
        return a.reshape(B, N, C, H, a.shape[-1]).transpose(1, 0, 3, 2, 4)

    qc, kc, vc, gc = (to_chunks(a) for a in (q, k, v, log_f))
    causal = jnp.tril(jnp.ones((C, C), dtype=bool))[:, :, None]

    def step(S, inp):
        qi, ki, vi, gi = inp
        b = jnp.cumsum(gi, axis=2)
        diff = b[:, :, :, None, :] - b[:, :, None, :, :]
        decay = jnp.where(causal, jnp.exp(jnp.where(causal, diff, 0.0)), 0.0)
        scores = jnp.einsum('bhtk,bhtsk,bhsk->bhts', qi, decay, ki)
        o = (jnp.einsum('bhts,bhsv->bhtv', scores, vi)
             + jnp.einsum('bhtk,bhkv->bhtv', qi * jnp.exp(b), S))
        b_last = b[:, :, -1:, :]
        S = (jnp.exp(b_last[:, :, 0, :])[..., None] * S
             + jnp.einsum('bhsk,bhsv->bhkv', ki * jnp.exp(b_last - b), vi))
        return S, o

    S0 = jnp.zeros((B, H, K, V), q.dtype)
    _, o = lax.scan(step, S0, (qc, kc, vc, gc))
    return o.transpose(1, 0, 3, 2, 4).reshape(B, T, H, V)

def rwkv7_scan(r, w, k, v, kk, a):
    B, T, H, N = r.shape

    def step(S, inp):
        r_t, w_t, k_t, v_t, kk_t, a_t = inp
        sa = jnp.einsum('bhvk,bhk->bhv', S, -kk_t)
        S = (S * w_t[:, :, None, :] + sa[..., None] * (kk_t * a_t)[:, :, None, :]
             + v_t[..., None] * k_t[:, :, None, :])
        y = jnp.einsum('bhvk,bhk->bhv', S, r_t)
        return S, y

    xs = tuple(jnp.moveaxis(t, 1, 0) for t in (r, w, k, v, kk, a))
    S0 = jnp.zeros((B, H, N, N), r.dtype)
    _, y = lax.scan(step, S0, xs)
    return jnp.moveaxis(y, 0, 1)

def first_inputs(seed: int = 0) -> dict:
    key = jax.random.key(seed)
    ks = iter(jax.random.split(key, 32))
    nrm = lambda shape, s: jax.random.normal(next(ks), shape, jnp.float32) * s
    uni = lambda shape, lo, hi: jax.random.uniform(next(ks), shape, jnp.float32, lo, hi)
    return {
        "x": nrm((BATCH, SEQ, D_MODEL), 1.0),
        "c": nrm((BATCH, D_MODEL), 1.0),
        "w_ada": nrm((DEPTH, D_MODEL, 3 * D_MODEL), 0.1 * D_MODEL ** -0.5),
        "b_ada": nrm((DEPTH, 3 * D_MODEL), 0.01),
        "w_in": nrm((DEPTH, D_MODEL, N_IN), D_MODEL ** -0.5),
        "hg_lower_bounds": nrm((DEPTH, HG_WIDTH), 0.5),
        "hg_norm_g": 1.0 + nrm((DEPTH, HG_WIDTH), 0.01),
        "rw_mu": uni((DEPTH, RW_COLS), 0.0, 1.0),
        "rw_w0": uni((DEPTH, RW_WIDTH), -6.0, 0.0),
        "rw_w_up": nrm((DEPTH, RW_DECAY_RANK, RW_WIDTH), 0.1 * RW_DECAY_RANK ** -0.5),
        "rw_a0": nrm((DEPTH, RW_WIDTH), 0.1),
        "rw_a_up": nrm((DEPTH, RW_ICL_RANK, RW_WIDTH), 0.1 * RW_ICL_RANK ** -0.5),
        "rw_k_k": 0.85 + nrm((DEPTH, RW_WIDTH), 0.02),
        "rw_k_a": 1.0 + nrm((DEPTH, RW_WIDTH), 0.02),
        "rw_r_k": nrm((DEPTH, RW_HEADS, RW_HEAD), 0.1),
        "rw_v0": 1.0 + nrm((DEPTH - 1, RW_WIDTH), 0.1),
        "rw_v_down": nrm((DEPTH - 1, D_MODEL, RW_VRES_RANK), D_MODEL ** -0.5),
        "rw_v_up": nrm((DEPTH - 1, RW_VRES_RANK, RW_WIDTH), 0.1 * RW_VRES_RANK ** -0.5),
        "rw_gn_g": 1.0 + nrm((DEPTH, RW_WIDTH), 0.01),
        "rw_gn_b": nrm((DEPTH, RW_WIDTH), 0.01),
        "w_branch_hg": nrm((DEPTH, HG_WIDTH, D_MODEL), DN_BETA * HG_WIDTH ** -0.5),
        "w_branch_rw": nrm((DEPTH, RW_WIDTH, D_MODEL), DN_BETA * RW_WIDTH ** -0.5),
        "w_out": nrm((DEPTH, D_MODEL, D_MODEL), DN_BETA * D_MODEL ** -0.5),
        "ln_g": 1.0 + nrm((DEPTH, D_MODEL), 0.01),
        "ln_b": nrm((DEPTH, D_MODEL), 0.01),
    }

def first_block(x, c, w_ada, b_ada, w_in, hg_lower_bounds, hg_norm_g, rw_mu, rw_w0, rw_w_up,
              rw_a0, rw_a_up, rw_k_k, rw_k_a, rw_r_k, rw_v0, rw_v_down, rw_v_up, rw_gn_g, rw_gn_b,
              w_branch_hg, w_branch_rw, w_out, ln_g, ln_b):
    f32 = jnp.float32
    B, T, _ = x.shape
    lb_soft = jax.nn.softmax(hg_lower_bounds.astype(f32), axis=0)
    lower_bounds = jnp.cumsum(lb_soft, axis=0) - lb_soft[0]
    v_first = None
    for l in range(DEPTH):
        cond = jax.nn.silu(c) @ w_ada[l] + b_ada[l]
        shift, scale, gate_raw = jnp.split(cond, 3, axis=-1)
        h = x * (1.0 + scale[:, None]) + shift[:, None]
        proj = h @ w_in[l]
        p_hg, p_rw, p_gate = jnp.split(proj, [HG_COLS, HG_COLS + RW_COLS], axis=-1)

        p_hg = p_hg.astype(f32)
        q, f_pre, i_val, z_hg = jnp.split(p_hg, 4, axis=-1)
        lb = lower_bounds[l]
        log_f = jnp.logaddexp(jnp.log(jnp.maximum(lb, LB_FLOOR)),
                              jnp.log1p(-lb) + jax.nn.log_sigmoid(f_pre))
        k_hg = (1.0 - lb) * jax.nn.sigmoid(-f_pre)
        o_hg = hgrn2_chunked(heads(q, HG_DK), heads(k_hg, HG_DK), heads(i_val, HG_DK), heads(log_f, HG_DK))
        o_hg = o_hg * lax.rsqrt(jnp.mean(jnp.square(o_hg), -1, keepdims=True) + RMS_EPS)
        o_hg = o_hg.reshape(B, T, HG_WIDTH) * hg_norm_g[l] * jax.nn.silu(z_hg)
        y_hg = o_hg.astype(x.dtype) @ w_branch_hg[l]

        p_rw = token_shift(p_rw.astype(f32), rw_mu[l])
        r, k, v, z_rw, w_down, a_down = jnp.split(
            p_rw, [RW_WIDTH, 2 * RW_WIDTH, 3 * RW_WIDTH, 4 * RW_WIDTH, 4 * RW_WIDTH + RW_DECAY_RANK], axis=-1)
        w_raw = -jax.nn.softplus(-(rw_w0[l] + jnp.tanh(w_down) @ rw_w_up[l])) - 0.5
        decay = jnp.exp(-jnp.exp(w_raw))
        if l == 0:
            v_first = v
        else:
            v_mix = jax.nn.sigmoid(rw_v0[l - 1] + (h.astype(f32) @ rw_v_down[l - 1]) @ rw_v_up[l - 1])
            v = v + (v_first - v) * v_mix
        a = jax.nn.sigmoid(rw_a0[l] + a_down @ rw_a_up[l])
        kk = heads(k * rw_k_k[l], RW_HEAD)
        kk = kk / jnp.maximum(jnp.sqrt(jnp.sum(jnp.square(kk), -1, keepdims=True)), L2_EPS)
        k = k * (1.0 + (a - 1.0) * rw_k_a[l])
        r_h, k_h, v_h = heads(r, RW_HEAD), heads(k, RW_HEAD), heads(v, RW_HEAD)
        y_rw = rwkv7_scan(r_h, heads(decay, RW_HEAD), k_h, v_h, kk, heads(a, RW_HEAD))
        mu = y_rw.mean(-1, keepdims=True)
        var = jnp.mean(jnp.square(y_rw - mu), -1, keepdims=True)
        y_rw = ((y_rw - mu) * lax.rsqrt(var + GN_EPS)).reshape(B, T, RW_WIDTH) * rw_gn_g[l] + rw_gn_b[l]
        bonus = jnp.sum(r_h * k_h * rw_r_k[l], -1, keepdims=True) * v_h
        y_rw = (y_rw + bonus.reshape(B, T, RW_WIDTH)) * jax.nn.silu(z_rw)
        y_rw = y_rw.astype(x.dtype) @ w_branch_rw[l]

        g_hg, g_rw = jnp.split(p_gate, N_BRANCH, axis=-1)
        merged = jax.nn.sigmoid(g_hg) * y_hg + jax.nn.sigmoid(g_rw) * y_rw
        out = merged @ w_out[l]
        x = layer_norm(DN_ALPHA * x + (1.0 + gate_raw[:, None]) * out, ln_g[l], ln_b[l])
    return x


DEPTH_2 = 1

GRID_W = 64
CTX_LEN = 256
N_HEADS = 8
N_KV_HEADS = 2
HEAD_DIM = 64
KV_GROUP = N_HEADS // N_KV_HEADS
ATTN_WIDTH = N_HEADS * HEAD_DIM
KV_WIDTH = N_KV_HEADS * HEAD_DIM
WINDOW = 128
BLOCK = 128
ROPE_THETA = 10000.0
POOL_WINDOWS = (2, 4, 8, 16)
N_POOL_GROUPS = 4
POOL_WIDTH = D_MODEL - ATTN_WIDTH
POOL_GROUP_DIM = POOL_WIDTH // N_POOL_GROUPS
MIX_WIDTH = ATTN_WIDTH + POOL_WIDTH
IN_COLS = ATTN_WIDTH + 2 * KV_WIDTH + POOL_WIDTH
N_EXPERTS = 64
TOP_K = 8
N_EXPERT_GROUPS = 8
EXPERTS_PER_GROUP = N_EXPERTS // N_EXPERT_GROUPS
TOPK_GROUPS = 4
D_EXPERT = 256
D_SHARED = 256
ROUTED_SCALE = 2.5
EXPERT_BLOCK = 128
EPS = 1e-6


F32 = jnp.float32

def rmsnorm(x, g):
    x32 = x.astype(F32)
    y = x32 * lax.rsqrt(jnp.mean(x32 * x32, axis=-1, keepdims=True) + EPS)
    return (y * g.astype(F32)).astype(x.dtype)

def modulate(h, shift, scale):
    return h * (1 + scale) + shift

def axial_rope_tables(n_tokens):
    rows = n_tokens // GRID_W
    row = jnp.repeat(jnp.arange(rows), GRID_W).astype(F32)
    col = jnp.tile(jnp.arange(GRID_W), rows).astype(F32)
    n_freq = HEAD_DIM // 4
    inv_freq = ROPE_THETA ** (-jnp.arange(n_freq, dtype=F32) / n_freq)
    ang_r = row[:, None] * inv_freq[None, :]
    ang_c = col[:, None] * inv_freq[None, :]
    return jnp.cos(ang_r), jnp.sin(ang_r), jnp.cos(ang_c), jnp.sin(ang_c)

def _rope_half(x, cos, sin):
    x1, x2 = jnp.split(x, 2, axis=-1)
    cos = cos[:, None, :]
    sin = sin[:, None, :]
    return jnp.concatenate([x1 * cos - x2 * sin, x1 * sin + x2 * cos], axis=-1)

def apply_axial_rope(x, tables):
    cos_r, sin_r, cos_c, sin_c = tables
    xr, xc = jnp.split(x.astype(F32), 2, axis=-1)
    return jnp.concatenate([_rope_half(xr, cos_r, sin_r), _rope_half(xc, cos_c, sin_c)], axis=-1).astype(x.dtype)

def split_projection(z):
    B, L = z.shape[:2]
    q = z[..., :ATTN_WIDTH].reshape(B, L, N_HEADS, HEAD_DIM)
    k = z[..., ATTN_WIDTH:ATTN_WIDTH + KV_WIDTH].reshape(B, L, N_KV_HEADS, HEAD_DIM)
    v = z[..., ATTN_WIDTH + KV_WIDTH:ATTN_WIDTH + 2 * KV_WIDTH].reshape(B, L, N_KV_HEADS, HEAD_DIM)
    p = z[..., ATTN_WIDTH + 2 * KV_WIDTH:]
    return q, k, v, p

def split_kv(z):
    B, L = z.shape[:2]
    k = z[..., :KV_WIDTH].reshape(B, L, N_KV_HEADS, HEAD_DIM)
    v = z[..., KV_WIDTH:].reshape(B, L, N_KV_HEADS, HEAD_DIM)
    return k, v

def latent_window_attention(q, k, v, k_ctx, v_ctx, sink):
    B, S = q.shape[:2]
    nb = S // BLOCK
    scale = HEAD_DIM ** -0.5
    qb = q.reshape(B, nb, BLOCK, N_KV_HEADS, KV_GROUP, HEAD_DIM)

    def band(t):
        tp = jnp.pad(t, ((0, 0), (BLOCK, BLOCK), (0, 0), (0, 0))).reshape(B, nb + 2, BLOCK, N_KV_HEADS, HEAD_DIM)
        return jnp.concatenate([tp[:, :-2], tp[:, 1:-1], tp[:, 2:]], axis=2)

    kb, vb = band(k), band(v)
    s_loc = jnp.einsum('bnqkgd,bnjkd->bnkgqj', qb, kb, preferred_element_type=F32) * scale
    s_ctx = jnp.einsum('bnqkgd,bckd->bnkgqc', qb, k_ctx, preferred_element_type=F32) * scale
    q_pos = jnp.arange(nb)[:, None, None] * BLOCK + jnp.arange(BLOCK)[None, :, None]
    k_pos = jnp.arange(nb)[:, None, None] * BLOCK - BLOCK + jnp.arange(3 * BLOCK)[None, None, :]
    allowed = (jnp.abs(q_pos - k_pos) <= WINDOW) & (k_pos >= 0) & (k_pos < S)
    s_loc = jnp.where(allowed[None, :, None, None], s_loc, -jnp.inf)
    sink_l = sink.astype(F32).reshape(1, 1, N_KV_HEADS, KV_GROUP, 1, 1)
    m = jnp.maximum(jnp.maximum(s_loc.max(-1, keepdims=True), s_ctx.max(-1, keepdims=True)), sink_l)
    p_loc = jnp.exp(s_loc - m)
    p_ctx = jnp.exp(s_ctx - m)
    denom = p_loc.sum(-1, keepdims=True) + p_ctx.sum(-1, keepdims=True) + jnp.exp(sink_l - m)
    o = (jnp.einsum('bnkgqj,bnjkd->bnkgqd', p_loc, vb.astype(F32))
         + jnp.einsum('bnkgqc,bckd->bnkgqd', p_ctx, v_ctx.astype(F32))) / denom
    o = o.transpose(0, 1, 4, 2, 3, 5).reshape(B, S, ATTN_WIDTH)
    return o.astype(q.dtype)

def context_attention(q, k, v, sink):
    B, C = q.shape[:2]
    scale = HEAD_DIM ** -0.5
    qc = q.reshape(B, C, N_KV_HEADS, KV_GROUP, HEAD_DIM)
    s = jnp.einsum('bqkgd,bckd->bkgqc', qc, k, preferred_element_type=F32) * scale
    sink_l = sink.astype(F32).reshape(1, N_KV_HEADS, KV_GROUP, 1, 1)
    m = jnp.maximum(s.max(-1, keepdims=True), sink_l)
    p = jnp.exp(s - m)
    denom = p.sum(-1, keepdims=True) + jnp.exp(sink_l - m)
    o = jnp.einsum('bkgqc,bckd->bkgqd', p, v.astype(F32)) / denom
    return o.transpose(0, 3, 1, 2, 4).reshape(B, C, ATTN_WIDTH).astype(q.dtype)

def multiscale_pool(p, pool_w, pool_scale):
    B, L, _ = p.shape
    p32 = p.astype(F32)
    cs = jnp.concatenate([jnp.zeros((B, 1, POOL_WIDTH), F32), jnp.cumsum(p32, axis=1)], axis=1)
    t = jnp.arange(L)
    outs = []
    for g, w in enumerate(POOL_WINDOWS):
        lo = jnp.clip(t - w // 2, 0, L)
        hi = jnp.clip(t - w // 2 + w, 0, L)
        sl = slice(g * POOL_GROUP_DIM, (g + 1) * POOL_GROUP_DIM)
        csg = cs[:, :, sl]
        mean = (csg[:, hi] - csg[:, lo]) / (hi - lo).astype(F32)[None, :, None]
        outs.append(mean - p32[:, :, sl])
    d = jnp.stack(outs, axis=2)
    y = jnp.einsum('blgc,gcd->blgd', d, pool_w.astype(F32)).reshape(B, L, POOL_WIDTH)
    return (y * pool_scale.astype(F32)).astype(p.dtype)

def routed_experts(h, idx, gate, w_gate, w_up, w_down):
    T, D = h.shape
    TK = T * TOP_K
    flat_e = idx.reshape(TK)
    flat_w = gate.reshape(TK)
    order = jnp.argsort(flat_e)
    e_sorted = flat_e[order]
    sizes = jnp.bincount(flat_e, length=N_EXPERTS)
    padded = (sizes + EXPERT_BLOCK - 1) // EXPERT_BLOCK * EXPERT_BLOCK
    pad_end = jnp.cumsum(padded)
    pad_start = pad_end - padded
    start = jnp.cumsum(sizes) - sizes
    dest = pad_start[e_sorted] + (jnp.arange(TK) - start[e_sorted])
    n_rows = -(-(TK + N_EXPERTS * (EXPERT_BLOCK - 1)) // EXPERT_BLOCK) * EXPERT_BLOCK
    n_blocks = n_rows // EXPERT_BLOCK
    row_tok = jnp.zeros((n_rows,), jnp.int32).at[dest].set((order // TOP_K).astype(jnp.int32))
    row_w = jnp.zeros((n_rows,), F32).at[dest].set(flat_w[order])
    block_e = jnp.minimum(jnp.searchsorted(pad_end, jnp.arange(n_blocks) * EXPERT_BLOCK, side='right'),
                          N_EXPERTS - 1)

    def expert_block(args):
        tok_b, w_b, e = args
        xb = h[tok_b]
        y = (jax.nn.silu(xb @ w_gate[e]) * (xb @ w_up[e])) @ w_down[e]
        return y.astype(F32) * w_b[:, None]

    y_rows = lax.map(expert_block, (row_tok.reshape(n_blocks, EXPERT_BLOCK),
                                    row_w.reshape(n_blocks, EXPERT_BLOCK), block_e))
    return jnp.zeros((T, D), F32).at[row_tok].add(y_rows.reshape(n_rows, D))

def moe_ffn(h, w_router, router_bias, w_gate, w_up, w_down, ws_gate, ws_up, ws_down):
    T = h.shape[0]
    scores = jax.nn.sigmoid(jnp.dot(h, w_router, preferred_element_type=F32))
    biased = scores + router_bias.astype(F32)
    grp_score = lax.top_k(biased.reshape(T, N_EXPERT_GROUPS, EXPERTS_PER_GROUP), 2)[0].sum(-1)
    _, top_grp = lax.top_k(grp_score, TOPK_GROUPS)
    grp_mask = jnp.any(top_grp[:, :, None] == jnp.arange(N_EXPERT_GROUPS)[None, None, :], axis=1)
    expert_mask = jnp.repeat(grp_mask, EXPERTS_PER_GROUP, axis=1)
    _, idx = lax.top_k(jnp.where(expert_mask, biased, -jnp.inf), TOP_K)
    gate = jnp.take_along_axis(scores, idx, axis=1)
    gate = gate / jnp.sum(gate, axis=-1, keepdims=True) * ROUTED_SCALE
    routed = routed_experts(h, idx, gate, w_gate, w_up, w_down)
    shared = (jax.nn.silu(h @ ws_gate) * (h @ ws_up)) @ ws_down
    return (routed + shared.astype(F32)).astype(h.dtype)

def second_inputs(seed: int = 0) -> dict:
    key = jax.random.key(seed)
    ks = jax.random.split(key, 24)
    D, L = D_MODEL, DEPTH_2

    def nrm(k, shape, scale):
        return jax.random.normal(k, shape, F32) * scale

    return {
        "x": nrm(ks[0], (BATCH, SEQ, D), 1.0),
        "c": nrm(ks[1], (BATCH, D), 1.0),
        "ctx": nrm(ks[2], (BATCH, CTX_LEN, D), 1.0),
        "c_ctx": nrm(ks[3], (D,), 1.0),
        "w_ada": nrm(ks[4], (L, D, 6 * D), 0.5 * D ** -0.5),
        "b_ada": nrm(ks[5], (L, 6 * D), 0.02),
        "norm1_g": 1.0 + nrm(ks[6], (L, D), 0.05),
        "norm2_g": 1.0 + nrm(ks[7], (L, D), 0.05),
        "w_in": nrm(ks[8], (L, D, IN_COLS), D ** -0.5),
        "attn_sink": nrm(ks[9], (L, N_HEADS), 0.5),
        "pool_w": nrm(ks[10], (L, N_POOL_GROUPS, POOL_GROUP_DIM, POOL_GROUP_DIM), POOL_GROUP_DIM ** -0.5),
        "pool_scale": 1.0 + nrm(ks[11], (L, POOL_WIDTH), 0.1),
        "w_out": nrm(ks[12], (L, MIX_WIDTH, D), MIX_WIDTH ** -0.5),
        "w_router": nrm(ks[13], (L, D, N_EXPERTS), D ** -0.5),
        "router_bias": nrm(ks[14], (L, N_EXPERTS), 0.01),
        "w_gate": nrm(ks[15], (L, N_EXPERTS, D, D_EXPERT), D ** -0.5),
        "w_up": nrm(ks[16], (L, N_EXPERTS, D, D_EXPERT), D ** -0.5),
        "w_down": nrm(ks[17], (L, N_EXPERTS, D_EXPERT, D), D_EXPERT ** -0.5),
        "ws_gate": nrm(ks[18], (L, D, D_SHARED), D ** -0.5),
        "ws_up": nrm(ks[19], (L, D, D_SHARED), D ** -0.5),
        "ws_down": nrm(ks[20], (L, D_SHARED, D), D_SHARED ** -0.5),
        "final_g": 1.0 + nrm(ks[21], (D,), 0.05),
    }

def second_block(x, c, ctx, c_ctx, w_ada, b_ada, norm1_g, norm2_g, w_in, attn_sink, pool_w, pool_scale,
              w_out, w_router, router_bias, w_gate, w_up, w_down, ws_gate, ws_up, ws_down, final_g):
    B, S, D = x.shape
    rope = axial_rope_tables(S)
    silu_c = jax.nn.silu(c)
    silu_cc = jax.nn.silu(c_ctx)
    for l in range(DEPTH_2):
        last = l == DEPTH_2 - 1
        mod = silu_c @ w_ada[l] + b_ada[l]
        mod_c = silu_cc @ w_ada[l] + b_ada[l]
        sh1, sc1, g1, sh2, sc2, g2 = jnp.split(mod[:, None, :], 6, axis=-1)
        sh1c, sc1c, g1c, sh2c, sc2c, g2c = jnp.split(mod_c, 6)

        hx = modulate(rmsnorm(x, norm1_g[l]), sh1, sc1)
        hc = modulate(rmsnorm(ctx, norm1_g[l]), sh1c, sc1c)
        qx, kx, vx, px = split_projection(hx @ w_in[l])
        qx = apply_axial_rope(qx, rope)
        kx = apply_axial_rope(kx, rope)
        if last:
            kc, vc = split_kv(hc @ w_in[l][:, ATTN_WIDTH:ATTN_WIDTH + 2 * KV_WIDTH])
        else:
            qc, kc, vc, pc = split_projection(hc @ w_in[l])
        attn_x = latent_window_attention(qx, kx, vx, kc, vc, attn_sink[l])
        pool_x = multiscale_pool(px, pool_w[l], pool_scale[l])
        x = x + g1 * (jnp.concatenate([attn_x, pool_x], axis=-1) @ w_out[l])
        if not last:
            attn_c = context_attention(qc, kc, vc, attn_sink[l])
            pool_c = multiscale_pool(pc, pool_w[l], pool_scale[l])
            ctx = ctx + g1c * (jnp.concatenate([attn_c, pool_c], axis=-1) @ w_out[l])

        hx2 = modulate(rmsnorm(x, norm2_g[l]), sh2, sc2)
        ffn_x = moe_ffn(hx2.reshape(B * S, D), w_router[l], router_bias[l], w_gate[l], w_up[l], w_down[l],
                        ws_gate[l], ws_up[l], ws_down[l]).reshape(B, S, D)
        x = x + g2 * ffn_x
        if not last:
            Cn = ctx.shape[1]
            hc2 = modulate(rmsnorm(ctx, norm2_g[l]), sh2c, sc2c)
            ffn_c = moe_ffn(hc2.reshape(B * Cn, D), w_router[l], router_bias[l], w_gate[l], w_up[l], w_down[l],
                            ws_gate[l], ws_up[l], ws_down[l]).reshape(B, Cn, D)
            ctx = ctx + g2c * ffn_c
    return rmsnorm(x, final_g)


def setup_inputs(seed=0):
    out = dict(first_inputs(seed))
    for name, value in second_inputs(seed + 1).items():
        if name != "x":
            out[name + "_2"] = value
    return out


def reference(
    x, c, w_ada, b_ada, w_in, hg_lower_bounds, hg_norm_g, rw_mu, rw_w0, rw_w_up, rw_a0, rw_a_up,
    rw_k_k, rw_k_a, rw_r_k, rw_v0, rw_v_down, rw_v_up, rw_gn_g, rw_gn_b, w_branch_hg,
    w_branch_rw, w_out, ln_g, ln_b, c_2, ctx_2, c_ctx_2, w_ada_2, b_ada_2, norm1_g_2, norm2_g_2,
    w_in_2, attn_sink_2, pool_w_2, pool_scale_2, w_out_2, w_router_2, router_bias_2, w_gate_2,
    w_up_2, w_down_2, ws_gate_2, ws_up_2, ws_down_2, final_g_2,
):
    x = first_block(
        x, c, w_ada, b_ada, w_in, hg_lower_bounds, hg_norm_g, rw_mu, rw_w0, rw_w_up, rw_a0,
        rw_a_up, rw_k_k, rw_k_a, rw_r_k, rw_v0, rw_v_down, rw_v_up, rw_gn_g, rw_gn_b,
        w_branch_hg, w_branch_rw, w_out, ln_g, ln_b,
    )
    return second_block(
        x, c_2, ctx_2, c_ctx_2, w_ada_2, b_ada_2, norm1_g_2, norm2_g_2, w_in_2, attn_sink_2,
        pool_w_2, pool_scale_2, w_out_2, w_router_2, router_bias_2, w_gate_2, w_up_2, w_down_2,
        ws_gate_2, ws_up_2, ws_down_2, final_g_2,
    )


_drawn_inputs = setup_inputs


def setup_inputs(seed=0):
    import zlib

    import numpy as np

    out = dict(_drawn_inputs(seed))
    spreads = {}
    factors = {'b_ada': 4.076,
     'hg_norm_g': 24.736,
     'rw_w_up': 8.0,
     'rw_a0': 5.136,
     'rw_a_up': 4.553,
     'rw_k_k': 22.843,
     'rw_k_a': 5.826,
     'rw_v0': 6.39,
     'rw_v_down': 7.797,
     'rw_v_up': 6.493,
     'rw_gn_g': 29.306,
     'rw_gn_b': 27.688,
     'attn_sink_2': 64.0}
    for name, (base, spread) in spreads.items():
        noise = np.random.default_rng([zlib.crc32(name.encode()), seed]).standard_normal(out[name].shape)
        drawn = base * np.exp(spread * noise) if base else spread * noise
        out[name] = __import__('jax').numpy.asarray(drawn.astype(out[name].dtype))
    for name, factor in factors.items():
        out[name] = (out[name] * factor).astype(out[name].dtype)
    return out
```

```python
from contextlib import ExitStack

import numpy as np

import concourse.bass as bass
from concourse import mybir

F32 = mybir.dt.float32
I32 = mybir.dt.int32
ALU = mybir.AluOpType
ACT = mybir.ActivationFunctionType
AX = mybir.AxisListType.X

P = 128
T = 1024
HALF = 512
D = 1024
KT = D // P
CH = 128
NC = T // CH
L = 2
HG = 4
PAIRS = 4
CQ, CF, CI, CZ, CR, CK, CV, CY, CLOW, CG1, CG2 = 0, 4, 8, 12, 16, 20, 24, 28, 32, 33, 41
NSCAN = 33
NIN = 49
NADA1, NADA2 = 24, 48
LN_EPS, RMS_EPS, GN_EPS, L2_EPS, LB_FLOOR, EPS = 1e-5, 1e-6, 64e-5, 1e-12, 1e-30, 1e-6
ALPHA = (2 * L) ** 0.25
E_HALF = 0.6065306597126334
LN2 = 0.6931471805599453
NE_BLOCKS, SLOT_BLOCKS = 64, 128
LEVELS = [64, 32, 16, 8, 4, 2, 1]


def wait(eng, sem, value, unit=1):
    if isinstance(value, int):
        if value > 0:
            eng.wait_ge(sem, value)
        return
    value = eng.snap(value)
    if unit:
        eng.wait_ge(sem, unit)
    eng.wait_ge(sem, value)


def rounds(eng, n):
    yield 0
    if n > 1:
        with eng.Fori(1, n) as i:
            yield i


class Steps:

    def __init__(self, eng, sem):
        self.eng, self.sem, self.base, self.n = eng, sem, 0, 0

    def loop(self, base):
        self.base, self.n = base, 0

    def mark(self, ins):
        ins.then_inc(self.sem, 1)
        self.n += 1
        return ins

    def settle(self):
        wait(self.eng, self.sem, self.base + self.n)

    def do(self, ins):
        self.mark(ins)
        self.settle()


class Kernel:

    def __init__(self, nc, I, out, ctx, scratch):
        self.nc, self.I, self.out, self.ctx = nc, I, out, ctx
        self.scratch = scratch

        def keep(name, shape, dt=F32):
            return ctx.enter_context(nc.sbuf_tensor("keep_" + name, shape, dt))

        self.xT = keep("xT", [P, KT, T])
        self.cond = keep("cond", [P, 2 * NADA1 + NADA2, 3])
        self.ones = keep("ones", [P, P])
        self.eye = keep("eye", [P, P])
        self.mix = keep("mix", [P, KT, T])
        self.yhg = self.mix[:, 0:HG, :]
        self.yrw = self.mix[:, HG:KT, :]
        self.vd = keep("vd", [32, T])
        self.ps = ctx.enter_context(nc.psum_tensor("ps", [P, 8, HALF], F32))
        self.keep = keep

    def second_block(self):
        self.hT2 = self.keep("hT2", [P, KT, T])
        self.idx = self.keep("idx", [P, P], I32)
        self.eb = self.keep("eb", [1, P], I32)
        self.nr = self.keep("nr", [1, 1], I32)
        self.slot = self.keep("slot", [P, KT, KT], I32)
        self.gates = self.keep("gates", [P, KT, KT])


class Stage:

    def __init__(self, k, name):
        self.k, self.name, self.ctx, self.sems = k, name, ExitStack(), []

    def __enter__(self):
        self.ctx.__enter__()
        return self

    def __exit__(self, *a):
        self.ctx.__exit__(*a)
        self.k.nc.clear_and_free_semaphores(self.sems)
        self.k.nc.all_engine_barrier()

    def sb(self, name, shape, dt=F32):
        return self.ctx.enter_context(self.k.nc.sbuf_tensor(f"s_{self.name}_{name}", shape, dt))

    def sem(self, name):
        self.sems.append(self.k.nc.alloc_semaphore(f"{self.name}_{name}"))
        return self.sems[-1]

    def block(self):
        return self.ctx.enter_context(self.k.nc.Block())


def modulation(k):
    nc, I = k.nc, k.I
    GRP, NT = 4, 2 * NADA1 + NADA2
    NG = NT // GRP
    with Stage(k, "ada") as s:
        w = s.sb("w", [P, 2, GRP, KT, P])
        c3 = s.sb("c3", [P, KT, 3])
        e3 = s.sb("e3", [P, KT, 3])
        bias = s.sb("bias", [P, NT])
        ld_w, ld_c = [s.sem("ld_w0"), s.sem("ld_w1")], s.sem("ld_c")
        exp_ready, silu_ready = s.sem("exp_ready"), s.sem("silu_ready")
        tiles_ready, tiles_taken, own = s.sem("tiles_ready"), s.sem("tiles_taken"), s.sem("own")
        cst, eye_clear = s.sem("cst"), s.sem("eye_clear")
        block = s.block()

        @block.sync
        def _(sp):
            sp.dma_start(c3[:], I["c3"]).then_inc(ld_c, 16)
            sp.dma_start(bias[:], I["b_ada"]).then_inc(ld_c, 16)
            for b in range(2):
                sp.dma_start(w[:, b], I["w_ada"][b]).then_inc(ld_w[b], 16)
            with sp.Fori(1, NG // 2) as i:
                for b in range(2):
                    wait(sp, tiles_ready, i * 2 + (b - 1))
                    sp.dma_start(w[:, b], I["w_ada"][i * 2 + b]).then_inc(ld_w[b], 16)

        @block.gpsimd
        def _(pool):
            pool.memset(k.ones[:], 1.0).then_inc(cst, 1)
            pool.memset(k.eye[:], 0.0).then_inc(eye_clear, 1)
            pool.wait_ge(eye_clear, 1)
            pool.affine_select(out=k.eye[:], in_=k.eye[:], compare_op=ALU.not_equal, fill=1.0, base=0,
                               pattern=[[-1, P]], channel_multiplier=1).then_inc(cst, 1)

        @block.scalar
        def _(act):
            act.wait_ge(ld_c, 32)
            act.activation(e3[:], c3[:], ACT.Exp, scale=-1.0).then_inc(exp_ready, 1)
            for t in range(KT):
                act.dma_start(k.xT[:, t], I["xT"][t]).then_inc(ld_c, 16)

        @block.vector
        def _(dve):
            own_steps = Steps(dve, own)
            dve.wait_ge(exp_ready, 1)
            own_steps.do(dve.tensor_scalar(e3[:], e3[:], 1.0, None, ALU.add))
            own_steps.do(dve.reciprocal(e3[:], e3[:]))
            dve.tensor_tensor(e3[:], e3[:], c3[:], ALU.mult).then_inc(silu_ready, 1)
            for i in rounds(dve, NG):
                wait(dve, tiles_ready, i + 1)
                dve.tensor_copy(k.cond[:, bass.ds(i * GRP, GRP), :],
                                k.ps[:, 0, 0:3 * GRP].rearrange("p (g v) -> p g v", g=GRP)).then_inc(tiles_taken, 1)
            dve.wait_ge(tiles_taken, NG)
            dve.wait_ge(ld_c, 32 + 16 * KT)
            dve.tensor_tensor(k.cond[:], k.cond[:], bias[:].unsqueeze(2).to_broadcast([P, NT, 3]), ALU.add).then_inc(own, 1)

        @block.tensor
        def _(pe):
            pe.wait_ge(silu_ready, 1)
            for i in rounds(pe, NG // 2):
                for b in range(2):
                    wait(pe, ld_w[b], i * 16 + 16, 16)
                    wait(pe, tiles_taken, i * 2 + b)
                    for g in range(GRP):
                        for t in range(KT):
                            mm = pe.matmul(k.ps[:, 0, 3 * g:3 * g + 3], w[:, b, g, t, :], e3[:, t, :],
                                           start=(t == 0), stop=(t == KT - 1))
                    mm.then_inc(tiles_ready, 1)


def modulate(eng, steps, k, hT, l, sc1):
    c = l * NADA1
    steps.do(eng.tensor_scalar(sc1[:], k.cond[:, c + KT:c + 2 * KT, 0], 1.0, None, ALU.add))
    for t in range(KT):
        steps.mark(eng.tensor_scalar(hT[:, t], k.xT[:, t], sc1[:, t:t + 1], k.cond[:, c + t, 0:1],
                                     ALU.mult, ALU.add))


def projection(k, l):
    nc, I = k.nc, k.I
    NB = 3
    with Stage(k, f"proj{l}") as s:
        hT = s.sb("hT", [P, KT, T])
        sc1 = s.sb("sc1", [P, KT])
        w = s.sb("w", [P, NB, KT, P])
        o = s.sb("o", [P, NB, T])
        ld_w = [s.sem(f"ld_w{b}") for b in range(NB)]
        st_o = [s.sem(f"st_o{b}") for b in range(NB)]
        h_ready, half_ready = s.sem("h_ready"), s.sem("half_ready")
        taken_a, taken_v = s.sem("taken_a"), s.sem("taken_v")
        if l:
            wv = s.sb("wv", [P, KT, 32])
            ld_v, vd_ready, vd_taken = s.sem("ld_v"), s.sem("vd_ready"), s.sem("vd_taken")
        block = s.block()

        @block.sync
        def _(sp):
            for b in range(NB):
                sp.dma_start(w[:, b], I["w_in"][l, b]).then_inc(ld_w[b], 16)
            if l:
                sp.dma_start(wv[:], I["v_down"]).then_inc(ld_v, 16)
            with sp.Fori(1, NSCAN // NB) as i:
                for b in range(NB):
                    wait(sp, half_ready, i * 2 * NB + 2 * (b + 1 - NB))
                    sp.dma_start(w[:, b], I["w_in"][l, i * NB + b]).then_inc(ld_w[b], 16)

        @block.vector
        def _(dve):
            modulate(dve, Steps(dve, h_ready), k, hT, l, sc1)
            for i in rounds(dve, NSCAN // NB):
                for b in range(NB):
                    wait(dve, half_ready, i * 2 * NB + 2 * b + 2)
                    wait(dve, st_o[b], i * 16, 16)
                    dve.tensor_copy(o[:, b, HALF:T], k.ps[:, 2 * b + 1, :]).then_inc(taken_v, 1)
            if l:
                dve.wait_ge(vd_ready, 1)
                dve.tensor_copy(k.vd[:], k.ps[0:32, 6:8, :].rearrange("p a n -> p (a n)")).then_inc(vd_taken, 1)

        @block.scalar
        def _(act):
            for i in rounds(act, NSCAN // NB):
                for b in range(NB):
                    wait(act, half_ready, i * 2 * NB + 2 * b + 1)
                    wait(act, st_o[b], i * 16, 16)
                    act.activation(o[:, b, 0:HALF], k.ps[:, 2 * b, :], ACT.Copy).then_inc(taken_a, 1)
                    wait(act, taken_a, i * NB + b + 1)
                    wait(act, taken_v, i * NB + b + 1)
                    act.dma_start(k.scratch["proj"][i * NB + b], o[:, b, :]).then_inc(st_o[b], 16)
            for b in range(NB):
                act.wait_ge(st_o[b], 16 * (NSCAN // NB))

        @block.tensor
        def _(pe):
            for i in rounds(pe, NSCAN // NB):
                for b in range(NB):
                    wait(pe, ld_w[b], i * 16 + 16, 16)
                    wait(pe, taken_a, (i - 1) * NB + b + 1)
                    wait(pe, taken_v, (i - 1) * NB + b + 1)
                    for half in range(2):
                        for t in range(KT):
                            if isinstance(i, int) and b == 0 and half == 0:
                                pe.wait_ge(h_ready, t + 2)
                            mm = pe.matmul(k.ps[:, 2 * b + half, :], w[:, b, t, :],
                                           hT[:, t, half * HALF:(half + 1) * HALF], start=(t == 0), stop=(t == KT - 1))
                        mm.then_inc(half_ready, 1)
            if l:
                pe.wait_ge(ld_v, 16)
                for half in range(2):
                    for t in range(KT):
                        mm = pe.matmul(k.ps[0:32, 6 + half, :], wv[:, t, :], hT[:, t, half * HALF:(half + 1) * HALF],
                                       start=(t == 0), stop=(t == KT - 1))
                mm.then_inc(vd_ready, 1)


def chunks(ap):
    return ap.rearrange("p (c n) -> p c n", c=NC)


def halves(ap, m, h):
    return ap.rearrange("p (b h m) -> p b h m", h=2, m=m)[:, :, h, :]


def banks(k, a, n=2):
    return k.ps[:, a:a + n, :].rearrange("p a n -> p (a n)")


def hgrn(k, l):
    nc, I = k.nc, k.I
    NL = len(LEVELS) + 1
    with Stage(k, f"hg{l}") as s:
        q, f, iv, z = (s.sb(n, [P, T]) for n in ("q", "f", "iv", "z"))
        par = s.sb("par", [P, HG, 8])
        cur = s.sb("cur", [P, 8])
        tmp = s.sb("tmp", [P, HG, 4])
        t1, t2, b = s.sb("t1", [P, T]), s.sb("t2", [P, T]), s.sb("b", [P, T])
        kk, qh, kh, eb = (s.sb(n, [P, T]) for n in ("kk", "qh", "kh", "eb"))
        dif, ex = s.sb("dif", [P, 2, T]), s.sb("ex", [P, 2, T])
        qt, kt = s.sb("qt", [P, 2, T]), s.sb("kt", [P, 2, T])
        acc, vtok, ktok = s.sb("acc", [P, T]), s.sb("vtok", [P, T]), s.sb("ktok", [P, T])
        S = s.sb("S", [P, NC, P])
        masks = s.sb("masks", [P, NL, P], I32)
        m0 = s.sb("m0", [P, T])
        sc = [banks(k, 0), banks(k, 2)]
        pv, po = banks(k, 4), banks(k, 6)

        ld_par, ld_f, ld_q, ld_i, ld_z = (s.sem("ld_" + n) for n in ("par", "f", "q", "i", "z"))
        small, lb_exp, lb_in, lb_log = (s.sem(n) for n in ("small", "lb_exp", "lb_in", "lb_log"))
        own, own_a, head_done = s.sem("own"), s.sem("own_a"), s.sem("head_done")
        nabs_ready, ln1_ready, dk_ready, ek_ready, nd_ready, ln2_ready = (
            s.sem(n) for n in ("nabs_ready", "ln1_ready", "dk_ready", "ek_ready", "nd_ready", "ln2_ready"))
        b_ready, eb_ready = s.sem("b_ready"), s.sem("eb_ready")
        dif_ready, ex_ready, ops_ready, sc_ready, sc_taken = (
            s.sem(n) for n in ("dif_ready", "ex_ready", "ops_ready", "sc_ready", "sc_taken"))
        tr_ready, tr_taken, kv_ready, S_ready = (
            s.sem(n) for n in ("tr_ready", "tr_taken", "kv_ready", "S_ready"))
        o_ready, sq_ready, ms_ready, rstd_ready, ez_ready = (
            s.sem(n) for n in ("o_ready", "sq_ready", "ms_ready", "rstd_ready", "ez_ready"))
        block = s.block()
        proj = k.scratch["proj"]

        @block.sync
        def _(sp):
            sp.dma_start(par[:, :, 0:3], I["hg_par"][l]).then_inc(ld_par, 16)
            sp.dma_start(masks[:], I["level_masks"]).then_inc(ld_par, 16)
            for h in rounds(sp, HG):
                wait(sp, head_done, h)
                sp.dma_start(f[:], proj[h + CF]).then_inc(ld_f, 16)
                sp.dma_start(q[:], proj[h + CQ]).then_inc(ld_q, 16)
                sp.dma_start(iv[:], proj[h + CI]).then_inc(ld_i, 16)
                sp.dma_start(z[:], proj[h + CZ]).then_inc(ld_z, 16)

        @block.gpsimd
        def _(pool):
            for h in rounds(pool, HG):
                for n in range(NL):
                    wait(pool, b_ready, h + 1)
                    wait(pool, ex_ready, h * NL + n - 1)
                    if n == 0:
                        last = chunks(b[:])[:, :, CH - 1:CH].to_broadcast([P, NC, CH])
                        pool.tensor_tensor(chunks(dif[:, 0]), last, chunks(b[:]), ALU.subtract).then_inc(dif_ready, 1)
                    else:
                        m = LEVELS[n - 1]
                        blocks = b[:].rearrange("p (b n) -> p b n", n=2 * m)
                        mid = blocks[:, :, m - 1:m].to_broadcast([P, T // (2 * m), 2 * m])
                        pool.tensor_tensor(dif[:, n % 2].rearrange("p (b n) -> p b n", n=2 * m), blocks, mid,
                                           ALU.subtract).then_inc(dif_ready, 1)

        @block.scalar
        def _(act):
            mine = Steps(act, own_a)
            act.wait_ge(small, 3)
            act.activation(tmp[:, :, 0:2], tmp[:, :, 0:2], ACT.Exp).then_inc(lb_exp, 1)
            act.wait_ge(lb_in, 2)
            act.activation(tmp[:, :, 2:4], tmp[:, :, 0:2], ACT.Ln).then_inc(lb_log, 1)
            PER = 4
            for h in rounds(act, HG):
                mine.loop(h * PER)
                wait(act, nabs_ready, h + 1)
                mine.do(act.activation(t1[:], t1[:], ACT.Exp))
                act.activation(t1[:], t1[:], ACT.Ln, bias=1.0).then_inc(ln1_ready, 1)
                wait(act, dk_ready, h + 1)
                act.activation(kk[:], kk[:], ACT.Exp).then_inc(ek_ready, 1)
                wait(act, nd_ready, h + 1)
                mine.do(act.activation(t1[:], t1[:], ACT.Exp))
                act.activation(t1[:], t1[:], ACT.Ln, bias=1.0).then_inc(ln2_ready, 1)
                wait(act, b_ready, h + 1)
                act.activation(eb[:], b[:], ACT.Exp).then_inc(eb_ready, 1)
                wait(act, tr_ready, h * 2 + 1)
                act.activation(vtok[:], pv, ACT.Copy).then_inc(tr_taken, 1)
                for n in range(NL):
                    wait(act, dif_ready, h * NL + (n + 1))
                    wait(act, ops_ready, h * NL + (n - 1))
                    if n == 0:
                        act.activation(ex[:, 0], dif[:, 0], ACT.Exp).then_inc(ex_ready, 1)
                    else:
                        m = LEVELS[n - 1]
                        act.activation(halves(ex[:, n % 2], m, 0), halves(dif[:, n % 2], m, 0), ACT.Exp, scale=-1.0)
                        act.activation(halves(ex[:, n % 2], m, 1), halves(dif[:, n % 2], m, 1), ACT.Exp).then_inc(ex_ready, 1)
                    if n == 2:
                        wait(act, tr_ready, h * 2 + 2)
                        act.activation(ktok[:], po, ACT.Copy).then_inc(tr_taken, 1)
                wait(act, ld_z, h * 16 + 16, 16)
                mine.do(act.activation(t1[:], z[:], ACT.Exp, scale=-1.0))
                act.activation(t1[:], t1[:], ACT.Identity, bias=1.0).then_inc(ez_ready, 1)
                wait(act, o_ready, h + 1)
                act.activation(t2[:], po, ACT.Square).then_inc(sq_ready, 1)
                wait(act, ms_ready, h + 1)
                mine.do(act.activation(t2[:], pv, ACT.Ln, scale=1.0 / P, bias=RMS_EPS))
                act.activation(t2[:], t2[:], ACT.Exp, scale=-0.5).then_inc(rstd_ready, 1)
                assert mine.n == PER

        def take_scores(dve, h, n):
            wait(dve, sc_ready, h * NL + (n + 1))
            wait(dve, sc_taken, h * NL + n)
            dve.copy_predicated(chunks(acc[:]), masks[:, n:n + 1, :].to_broadcast([P, NC, P]), chunks(sc[n % 2]))\
               .then_inc(sc_taken, 1)

        @block.vector
        def _(dve):
            mine = Steps(dve, own)
            mine.mark(dve.memset(acc[:], 0.0))
            mine.mark(dve.memset(qt[:], 0.0))
            mine.mark(dve.memset(kt[:], 0.0))
            mine.do(dve.memset(m0[:], 1.0))
            mine.mark(dve.memset(chunks(m0[:])[:, :, 0:1], 0.0))
            dve.wait_ge(ld_par, 32)
            mine.do(dve.tensor_tensor(tmp[:, :, 2:3], par[:, :, 0:1], par[:, :, 1:2], ALU.max))
            for c in range(2):
                dve.tensor_tensor(tmp[:, :, c:c + 1], par[:, :, c:c + 1], tmp[:, :, 2:3], ALU.subtract).then_inc(small, 1)
            dve.memset(par[:, :, 6:8], 0.0).then_inc(small, 1)
            dve.wait_ge(lb_exp, 1)
            dve.wait_ge(small, 3)
            mine.do(dve.tensor_tensor(tmp[:, :, 2:3], tmp[:, :, 0:1], tmp[:, :, 1:2], ALU.add))
            mine.do(dve.reciprocal(tmp[:, :, 2:3], tmp[:, :, 2:3]))
            mine.do(dve.tensor_tensor(tmp[:, :, 0:2], tmp[:, :, 0:2], tmp[:, :, 2:3].to_broadcast([P, HG, 2]), ALU.mult))
            if l:
                mine.do(dve.tensor_tensor(tmp[:, :, 3:4], tmp[:, :, 0:1], tmp[:, :, 1:2], ALU.add))
            else:
                mine.do(dve.tensor_copy(tmp[:, :, 3:4], tmp[:, :, 0:1]))
            mine.do(dve.tensor_tensor(tmp[:, :, 3:4], tmp[:, :, 3:4], tmp[:, :, 0:1], ALU.subtract))
            mine.do(dve.tensor_scalar(par[:, :, 3:4], tmp[:, :, 3:4], -1.0, 1.0, ALU.mult, ALU.add))
            dve.tensor_scalar(tmp[:, :, 0:1], tmp[:, :, 3:4], LB_FLOOR, 2.0 ** 50, ALU.max, ALU.mult).then_inc(lb_in, 1)
            dve.tensor_scalar(tmp[:, :, 1:2], par[:, :, 3:4], 1e-18, None, ALU.max).then_inc(lb_in, 1)
            dve.wait_ge(lb_log, 1)
            mine.do(dve.tensor_scalar(par[:, :, 4:5], tmp[:, :, 2:3], -50 * LN2, None, ALU.add))
            mine.do(dve.tensor_tensor(par[:, :, 5:6], tmp[:, :, 3:4], par[:, :, 4:5], ALU.subtract))
            BASE, PER = mine.n, 11
            for h in rounds(dve, HG):
                mine.loop(h * PER + BASE)
                mine.do(dve.tensor_copy(cur[:].unsqueeze(1), par[:, bass.ds(h, 1), :]))
                wait(dve, ld_f, h * 16 + 16, 16)
                dve.scalar_tensor_tensor(t1[:], f[:], -1.0, f[:], ALU.mult, ALU.min).then_inc(nabs_ready, 1)
                wait(dve, ln1_ready, h + 1)
                mine.do(dve.scalar_tensor_tensor(t2[:], f[:], 0.0, t1[:], ALU.min, ALU.subtract))
                dve.tensor_tensor(kk[:], t2[:], f[:], ALU.subtract).then_inc(dk_ready, 1)
                wait(dve, dk_ready, h + 1)
                mine.do(dve.tensor_scalar(t2[:], t2[:], cur[:, 5:6], None, ALU.add))
                dve.scalar_tensor_tensor(t1[:], t2[:], -1.0, t2[:], ALU.mult, ALU.min).then_inc(nd_ready, 1)
                wait(dve, ln2_ready, h + 1)
                mine.do(dve.scalar_tensor_tensor(t2[:], t2[:], 0.0, t1[:], ALU.max, ALU.add))
                mine.do(dve.tensor_scalar(t2[:], t2[:], cur[:, 4:5], None, ALU.add))
                dve.tensor_tensor_scan(b[:], m0[:], t2[:], 0.0, ALU.mult, ALU.add).then_inc(b_ready, 1)
                wait(dve, ek_ready, h + 1)
                mine.do(dve.tensor_scalar(kk[:], kk[:], cur[:, 3:4], None, ALU.mult))
                wait(dve, eb_ready, h + 1)
                wait(dve, ld_q, h * 16 + 16, 16)
                mine.mark(dve.tensor_tensor(qh[:], q[:], eb[:], ALU.mult))
                for n in range(NL):
                    wait(dve, ex_ready, h * NL + (n + 1))
                    if n == 0:
                        dve.tensor_tensor(kh[:], kk[:], ex[:, 0], ALU.mult).then_inc(ops_ready, 1)
                        continue
                    m, u = LEVELS[n - 1], n % 2
                    wait(dve, sc_ready, h * NL + (n - 2))
                    dve.tensor_tensor(halves(kt[:, u], m, 0), halves(kk[:], m, 0), halves(ex[:, u], m, 0), ALU.mult)
                    dve.tensor_tensor(halves(qt[:, u], m, 1), halves(q[:], m, 1), halves(ex[:, u], m, 1), ALU.mult)\
                       .then_inc(ops_ready, 1)
                    if n >= 2:
                        take_scores(dve, h, n - 2)
                take_scores(dve, h, NL - 2)
                take_scores(dve, h, NL - 1)
                wait(dve, kv_ready, h + 1)
                for c in range(1, NC):
                    kv = pv[:, (c - 1) * P:c * P]
                    if c == 1:
                        ins = dve.tensor_copy(S[:, 1], kv)
                    else:
                        ins = dve.scalar_tensor_tensor(S[:, c], S[:, c - 1], eb[:, c * CH - 1:c * CH], kv, ALU.mult, ALU.add)
                    ins.then_inc(S_ready, 1)
                    wait(dve, S_ready, h * (NC - 1) + c)
                wait(dve, ez_ready, h + 1)
                mine.do(dve.reciprocal(t1[:], t1[:]))
                mine.mark(dve.tensor_tensor(t1[:], t1[:], z[:], ALU.mult))
                wait(dve, rstd_ready, h + 1)
                mine.do(dve.tensor_tensor(t2[:], po, t2[:], ALU.mult))
                mine.do(dve.tensor_scalar(t2[:], t2[:], cur[:, 2:3], None, ALU.mult))
                dve.tensor_tensor(k.yhg[:, h, :] if isinstance(h, int) else k.yhg[:, bass.ds(h, 1), :],
                                  t2[:] if isinstance(h, int) else t2[:].unsqueeze(1),
                                  t1[:] if isinstance(h, int) else t1[:].unsqueeze(1), ALU.mult).then_inc(head_done, 1)
                wait(dve, head_done, h + 1)
                assert mine.n == PER, mine.n

        @block.tensor
        def _(pe):
            for h in rounds(pe, HG):
                wait(pe, head_done, h)
                wait(pe, ld_i, h * 16 + 16, 16)
                for c in range(NC):
                    tr = pe.transpose(pv[:, c * P:(c + 1) * P], iv[:, c * P:(c + 1) * P], k.eye[:])
                tr.then_inc(tr_ready, 1)
                wait(pe, ops_ready, h * NL + 1)
                for c in range(NC):
                    tr = pe.transpose(po[:, c * P:(c + 1) * P], kh[:, c * P:(c + 1) * P], k.eye[:])
                tr.then_inc(tr_ready, 1)
                for n in range(NL):
                    wait(pe, sc_taken, h * NL + (n - 1))
                    if n < NL - 1:
                        wait(pe, ops_ready, h * NL + (n + 2))
                        a, r = kt[:, (n + 1) % 2], qt[:, (n + 1) % 2]
                    else:
                        a, r = kk[:], q[:]
                    for c in range(NC):
                        mm = pe.matmul(sc[n % 2][:, c * P:(c + 1) * P], a[:, c * P:(c + 1) * P], r[:, c * P:(c + 1) * P],
                                       start=True, stop=True)
                    mm.then_inc(sc_ready, 1)
                wait(pe, tr_taken, h * 2 + 2)
                for c in range(NC - 1):
                    mm = pe.matmul(pv[:, c * P:(c + 1) * P], ktok[:, c * P:(c + 1) * P], vtok[:, c * P:(c + 1) * P],
                                   start=True, stop=True)
                mm.then_inc(kv_ready, 1)
                wait(pe, sc_taken, h * NL + NL)
                for c in range(NC):
                    w = slice(c * P, (c + 1) * P)
                    if c:
                        wait(pe, S_ready, h * (NC - 1) + c)
                        pe.matmul(po[:, w], S[:, c, :], qh[:, w], start=True, stop=False)
                    mm = pe.matmul(po[:, w], vtok[:, w], acc[:, w], start=(c == 0), stop=True)
                mm.then_inc(o_ready, 1)
                wait(pe, sq_ready, h + 1)
                for a in range(2):
                    mm = pe.matmul(pv[:, a * HALF:(a + 1) * HALF], k.ones[:], t2[:, a * HALF:(a + 1) * HALF],
                                   start=True, stop=True)
                mm.then_inc(ms_ready, 1)


def rwkv(k, l):
    nc, I = k.nc, k.I
    HD = 64
    GC = 4
    LV = [2, 4, 8, 16, 32, 64]
    NLV = len(LV)
    NPAR = 15
    G2 = NC // GC
    with Stage(k, f"rw{l}") as s:
        raw = s.sb("raw", [P, 4, T + 1])
        lo = s.sb("lo", [P, T])
        par, cur = s.sb("par", [P, PAIRS, NPAR]), s.sb("cur", [P, NPAR])
        t1, t2, t3 = (s.sb(n, [P, T]) for n in ("t1", "t2", "t3"))
        b, lw, a, kk, km = (s.sb(n, [P, T]) for n in ("b", "lw", "a", "kk", "km"))
        X, XT, CT = (s.sb(n, [P, 2, GC, CH]) for n in ("X", "XT", "CT"))
        Ep, Em, Ex = (x[:].rearrange("p e c n -> p (e c n)") for x in (X, XT, CT))
        Y = t3[:].rearrange("p (e c n) -> p e c n", e=2, c=GC)
        AR = s.sb("AR", [P, NC, 2, CH])
        B, Kd = s.sb("B", [P, T]), s.sb("Kd", [P, T])
        At, Bt, Kt, Vt = (x[:].rearrange("p (c n) -> p c n", c=NC) for x in (kk, a, km, lw))
        LN, MP = s.sb("LN", [P, 2, GC, 2, CH]), s.sb("MP", [P, 2, GC, 2, CH])
        dd = LN[:].rearrange("p e c a n -> p e (c a n)")
        vf = MP[:].rearrange("p e c a n -> p e (c a n)")[:, 0, :]
        XA = b[:, 0:HALF].rearrange("p (c n) -> p c n", c=GC)
        MV = b[:, HALF:T].rearrange("p (e c n) -> p e c n", e=2, c=GC)
        SA, Sc, G = s.sb("SA", [P, P]), s.sb("Sc", [P, NC + 1, HD]), s.sb("G", [P, NC])
        mLN, lev = s.sb("mLN", [P, 2, CH]), s.sb("lev", [P, 1 + NLV, CH])
        lev1T = s.sb("lev1T", [P, CH])
        bones, lora, vup = s.sb("bones", [P, P]), s.sb("lora", [P, P]), s.sb("vup", [32, P])
        proj, vfirst = k.scratch["proj"], k.scratch["vfirst"]
        r, kx, v, z = (raw[:, n, 1:T + 1] for n in range(4))

        def h2(ap, i):
            return ap[:, i * HALF:(i + 1) * HALF]

        names = ("st_spare ld_par ld_low ld_r ld_k ld_v ld_z ld_lora ld_vf st_v own own_a low_in low_tanh  pair_done "
                 "dif_ready shifted pre_ready exps_ready mix_free kk0_ready sq_ready ss_ready ssm_ready rn_ready b_ready "
                 "D_ready E_ready G_in G_ready ops_ready rk_ready tr_ready tr_taken bon_ready bon_done "
                 "pr_ready pr_taken l_ready x_ready ct_ready yy_ready yy_taken dx_ready mv_ready mv_taken xa_ready xa_taken "
                 "sa_psum sa_ready u_ready S_ready y_ready y_taken mu_ready ysq_in ysq_ready var_ready rstd_ready ez_ready")
        sm = {n: s.sem(n) for n in names.split()}
        (st_spare, ld_par, ld_low, ld_r, ld_k, ld_v, ld_z, ld_lora, ld_vf, st_v, own, own_a, low_in, low_tanh, pair_done,
         dif_ready, shifted, pre_ready, exps_ready, mix_free, kk0_ready, sq_ready, ss_ready, ssm_ready, rn_ready, b_ready,
         D_ready, E_ready, G_in, G_ready, ops_ready, rk_ready, tr_ready, tr_taken, bon_ready, bon_done,
         pr_ready, pr_taken, l_ready, x_ready, ct_ready, yy_ready, yy_taken, dx_ready, mv_ready, mv_taken, xa_ready, xa_taken,
         sa_psum, sa_ready, u_ready, S_ready, y_ready, y_taken, mu_ready, ysq_in, ysq_ready, var_ready, rstd_ready,
         ez_ready) = (sm[n] for n in names.split())
        tiles = [(1, kx, ld_k, CK), (0, r, ld_r, CR), (2, v, ld_v, CV), (3, z, ld_z, CY)]
        block = s.block()

        @block.sync
        def _(sp):
            sp.dma_start(raw[:, 0, 1:T + 1], proj[CLOW]).then_inc(ld_low, 16)
            sp.dma_start(par[:, :, 0:13], I["rw_par"][l]).then_inc(ld_par, 16)
            sp.dma_start(mLN[:], I["causal_masks"]).then_inc(ld_par, 16)
            sp.dma_start(lev[:], I["pair_masks"]).then_inc(ld_par, 16)
            sp.dma_start(lev1T[:], I["pair_mask_t"]).then_inc(ld_par, 16)
            for p in rounds(sp, PAIRS):
                if isinstance(p, int):
                    sp.wait_ge(low_in, 1)
                wait(sp, pair_done, p)
                for n, ap, ld, col in tiles:
                    if n == 2 and not l:
                        wait(sp, st_v, p * 16, 16)
                    sp.dma_start(ap, proj[p + col]).then_inc(ld, 16)
                    if n == 1:
                        sp.dma_start(lora[:], I["rw_lora"][l, p]).then_inc(ld_lora, 16)
                        if l:
                            sp.dma_start(vup[:], I["v_up"][p]).then_inc(ld_lora, 16)
                            sp.dma_start(vf, vfirst[p]).then_inc(ld_vf, 16)
                if not l:
                    spare = k.scratch["yrow"].rearrange("(r b) n -> r b n", r=P)
                    n = (SLOT_BLOCKS - NE_BLOCKS) // PAIRS
                    sp.dma_start(spare[:, bass.ds(p * n + NE_BLOCKS, n), :],
                                 k.xT[:, 0:1, :].to_broadcast([P, n, D])).then_inc(st_spare, 16)
            if not l:
                sp.wait_ge(st_spare, 16 * PAIRS)

        @block.gpsimd
        def _(pool):
            for p in rounds(pool, PAIRS):
                for i, (n, ap, ld, _c) in enumerate(tiles):
                    wait(pool, ld, p * 16 + 16, 16)
                    wait(pool, shifted, p * 4 + (i - 1))
                    if i < 2:
                        wait(pool, pair_done, p)
                    pool.tensor_tensor(dd[:, i % 2], raw[:, n, 0:T], ap, ALU.subtract).then_inc(dif_ready, 1)
                wait(pool, b_ready, p + 1)
                mid = chunks(b[:])[:, :, CH // 2 - 1:CH // 2].to_broadcast([P, NC, CH])
                pool.tensor_tensor(chunks(t1[:]), chunks(b[:]), mid, ALU.subtract).then_inc(D_ready, 1)
                wait(pool, D_ready, p * 2 + 1)
                pool.tensor_tensor(lw[:], t1[:], lw[:], ALU.subtract).then_inc(D_ready, 1)
                for g in range(G2):
                    for n in range(NLV):
                        wait(pool, pr_taken, (p * G2 + g) * 4 + 2)
                        wait(pool, yy_ready, (p * G2 + g) * 2 * NLV + 2 * n)
                        if g == 0 and n == 0:
                            wait(pool, ops_ready, p * 4 + 4)
                        for e in range(2):
                            pool.tensor_tensor(CT[:, e], LN[:, e, :, 0, :],
                                               lev[:, 1 + n:2 + n, :].to_broadcast([P, GC, CH]), ALU.mult)\
                                .then_inc(ct_ready, 1)

        @block.scalar
        def _(act):
            mine = Steps(act, own_a)
            act.wait_ge(low_in, 1)
            act.activation(lo[0:HD, :], lo[0:HD, :], ACT.Tanh).then_inc(low_tanh, 1)
            PER = 2
            for p in rounds(act, PAIRS):
                mine.loop(p * PER)
                wait(act, pre_ready, p * (2 + l) + 1)
                wait(act, shifted, p * 4 + 1)
                wait(act, pair_done, p)
                act.activation(t1[:], banks(k, 0), ACT.Sigmoid, bias=cur[:, 4:5]).then_inc(exps_ready, 1)
                wait(act, pre_ready, p * (2 + l) + 2)
                act.activation(a[:], banks(k, 2), ACT.Sigmoid, bias=cur[:, 5:6]).then_inc(exps_ready, 1)
                if l:
                    wait(act, pre_ready, p * 3 + 3)
                    act.activation(t3[:], banks(k, 4), ACT.Sigmoid, bias=cur[:, 11:12]).then_inc(exps_ready, 1)
                else:
                    wait(act, shifted, p * 4 + 3)
                    act.dma_start(vfirst[p], v).then_inc(st_v, 16)
                wait(act, kk0_ready, p + 1)
                act.activation(t2[:], kk[:], ACT.Square).then_inc(sq_ready, 1)
                wait(act, ssm_ready, p + 1)
                mine.do(act.activation(t2[:], t2[:], ACT.Ln, scale=2.0 ** 20))
                act.activation(t2[:], t2[:], ACT.Exp, scale=-0.5, bias=cur[:, 14:15]).then_inc(rn_ready, 1)
                wait(act, D_ready, p * 2 + 1)
                act.activation(Ep, t1[:], ACT.Exp).then_inc(E_ready, 1)
                act.activation(Em, t1[:], ACT.Exp, scale=-1.0).then_inc(E_ready, 1)
                wait(act, D_ready, p * 2 + 2)
                act.activation(Ex, lw[:], ACT.Exp).then_inc(E_ready, 1)
                wait(act, G_in, p + 1)
                act.activation(G[:], G[:], ACT.Exp).then_inc(G_ready, 1)
                wait(act, ops_ready, p * 4 + 4)
                wait(act, rk_ready, p + 1)
                for n, dst in enumerate((At, Bt, Kt, Vt)):
                    wait(act, tr_ready, p * 4 + (n + 1))
                    act.activation(dst.rearrange("p c n -> p (c n)"), banks(k, 2 * n), ACT.Copy).then_inc(tr_taken, 1)
                for g in range(G2):
                    q = p * G2 + g
                    wait(act, mv_ready, q + 1)
                    act.activation(b[:, HALF:T], k.ps[:, 6, :], ACT.Copy).then_inc(mv_taken, 1)
                    for n in range(NLV):
                        for e in range(2):
                            wait(act, yy_ready, q * 2 * NLV + (2 * n + e + 1))
                            wait(act, dx_ready, q * 2 * NLV + (2 * (n - 1) + e + 1))
                            act.activation(Y[:, e].rearrange("p c n -> p (c n)"), k.ps[:, e, :], ACT.Copy).then_inc(yy_taken, 1)
                    wait(act, xa_ready, q + 1)
                    act.activation(b[:, 0:HALF], k.ps[:, 7, :], ACT.Copy).then_inc(xa_taken, 1)
                wait(act, ysq_in, p + 1)
                act.activation(t3[:], t2[:], ACT.Square).then_inc(ysq_ready, 1)
                wait(act, var_ready, p + 1)
                mine.do(act.activation(t3[:], banks(k, 2), ACT.Ln, scale=1.0 / HD, bias=GN_EPS))
                act.activation(t3[:], t3[:], ACT.Exp, scale=-0.5).then_inc(rstd_ready, 1)
                wait(act, shifted, p * 4 + 4)
                act.activation(b[:], z, ACT.Sigmoid).then_inc(ez_ready, 1)
                assert mine.n == PER
            if not l:
                act.wait_ge(st_v, 16 * PAIRS)

        @block.vector
        def _(dve):
            mine = Steps(dve, own)
            mine.mark(dve.memset(raw[:, :, 0:1], 0.0))
            mine.mark(dve.memset(bones[:], 0.0))
            mine.mark(dve.memset(Sc[:, 0], 0.0))
            mine.settle()
            for e in range(2):
                mine.mark(dve.memset(bones[e * HD:(e + 1) * HD, e * HD:(e + 1) * HD], 1.0))
            dve.wait_ge(ld_par, 64)
            mine.mark(dve.tensor_scalar(par[:, :, 13:14], par[:, :, 7:8], -1.0, 1.0, ALU.mult, ALU.add))
            mine.mark(dve.memset(par[:, :, 14:15], 10 * LN2))
            dve.wait_ge(ld_low, 16)
            mine.do(dve.tensor_tensor(t1[:], raw[:, 0, 0:T], r, ALU.subtract))
            dve.scalar_tensor_tensor(lo[:], t1[:], par[:, 0, 12:13], r, ALU.mult, ALU.add).then_inc(low_in, 1)
            dve.wait_ge(low_tanh, 1)
            BASE, PER = mine.n, 31 + 3 * l
            for p in rounds(dve, PAIRS):
                mine.loop(p * PER + BASE)
                mine.do(dve.tensor_copy(cur[:].unsqueeze(1), par[:, bass.ds(p, 1), :]))
                for i, (n, ap, ld, _c) in enumerate(tiles):
                    wait(dve, dif_ready, p * 4 + (i + 1))
                    dve.scalar_tensor_tensor(ap, dd[:, i % 2], cur[:, n:n + 1], ap, ALU.mult, ALU.add).then_inc(shifted, 1)
                wait(dve, shifted, p * 4 + 4)
                dve.tensor_scalar(kk[:], kx, cur[:, 6:7], None, ALU.mult).then_inc(kk0_ready, 1)
                wait(dve, exps_ready, p * (2 + l) + 1)
                mine.do(dve.tensor_scalar(lw[:], t1[:], -E_HALF, None, ALU.mult))
                for c in range(NC):
                    cs = slice(c * CH, (c + 1) * CH)
                    ins = dve.tensor_tensor_scan(b[:, cs], k.ones[:], lw[:, cs], 0.0, ALU.mult, ALU.add)
                ins.then_inc(b_ready, 1)
                wait(dve, b_ready, p + 1)
                cb = chunks(b[:])
                mine.do(dve.tensor_tensor(G[:].unsqueeze(2), cb[:, :, CH - 1:CH], cb[:, :, CH // 2 - 1:CH // 2], ALU.subtract))
                dve.tensor_tensor(G[:, 0:NC - 1].unsqueeze(2), G[:, 0:NC - 1].unsqueeze(2), cb[:, 1:NC, CH // 2 - 1:CH // 2],
                                  ALU.add).then_inc(G_in, 1)
                wait(dve, exps_ready, p * (2 + l) + 2)
                if l:
                    wait(dve, exps_ready, p * 3 + 3)
                    wait(dve, ld_vf, p * 16 + 16, 16)
                    mine.do(dve.tensor_tensor(vf, vf, v, ALU.subtract))
                    mine.do(dve.tensor_tensor(vf, vf, t3[:], ALU.mult))
                    mine.do(dve.tensor_tensor(v, v, vf, ALU.add))
                wait(dve, ss_ready, p + 1)
                dve.tensor_scalar(t2[:], banks(k, 6), L2_EPS ** 2, None, ALU.max).then_inc(ssm_ready, 1)
                mine.do(dve.tensor_scalar(km[:], a[:], cur[:, 7:8], cur[:, 13:14], ALU.mult, ALU.add))
                mine.do(dve.tensor_tensor(km[:], km[:], kx, ALU.mult))
                wait(dve, rn_ready, p + 1)
                mine.do(dve.tensor_tensor(kk[:], kk[:], t2[:], ALU.mult))
                wait(dve, E_ready, p * 3 + 3)
                dve.tensor_tensor(AR[:, :, 0, :], chunks(kk[:]), chunks(Ex), ALU.mult).then_inc(ops_ready, 1)
                mine.do(dve.tensor_tensor(B[:], kk[:], a[:], ALU.mult))
                dve.tensor_tensor(B[:], B[:], Em, ALU.mult).then_inc(ops_ready, 1)
                dve.tensor_tensor(Kd[:], km[:], Em, ALU.mult).then_inc(ops_ready, 1)
                dve.tensor_tensor(AR[:, :, 1, :], chunks(r), chunks(Ep), ALU.mult).then_inc(ops_ready, 1)
                dve.scalar_tensor_tensor(t2[:], r, cur[:, 8:9], km[:], ALU.mult, ALU.mult).then_inc(rk_ready, 1)
                wait(dve, bon_ready, p + 1)
                dve.tensor_tensor(t1[:], banks(k, 0), v, ALU.mult).then_inc(bon_done, 1)
                wait(dve, G_ready, p + 1)
                for g in range(G2):
                    q = p * G2 + g
                    for n, dst in enumerate((LN, MP)):
                        for e in range(2):
                            wait(dve, pr_ready, q * 4 + (2 * n + e + 1))
                            dve.tensor_tensor(dst[:, e].rearrange("p c a n -> p c (a n)"),
                                              banks(k, 4 * n + 2 * e).rearrange("p (c m) -> p c m", c=GC),
                                              mLN[:].rearrange("p a n -> p (a n)").unsqueeze(1).to_broadcast([P, GC, 2 * CH]),
                                              ALU.mult).then_inc(pr_taken, 1)
                    for e in range(2):
                        wait(dve, pr_taken, q * 4 + 4)
                        wait(dve, l_ready, q * 2 + (e + 1))
                        mine.mark(dve.tensor_tensor(X[:, e], k.ps[:, e, :].rearrange("p (c n) -> p c n", c=GC),
                                                    lev1T[:].unsqueeze(1).to_broadcast([P, GC, CH]), ALU.mult))
                        mine.do(dve.tensor_tensor(XT[:, e], LN[:, e, :, 0, :], lev[:, 0:1, :].to_broadcast([P, GC, CH]), ALU.mult))
                        eye = k.eye[:].unsqueeze(1).to_broadcast([P, GC, CH])
                        mine.mark(dve.tensor_tensor(X[:, e], eye, X[:, e], ALU.subtract))
                        dve.tensor_tensor(XT[:, e], eye, XT[:, e], ALU.subtract).then_inc(x_ready, 1)
                    for n in range(NLV):
                        for e in range(2):
                            wait(dve, dx_ready, q * 2 * NLV + (2 * n + e + 1))
                            wait(dve, x_ready, q * 2 * (NLV + 1) + (2 * n + e + 1))
                            if n < NLV - 1:
                                dve.tensor_tensor(X[:, e], X[:, e], k.ps[:, 4 + e, :].rearrange("p (c n) -> p c n", c=GC),
                                                  ALU.subtract)
                            dve.tensor_tensor(XT[:, e], XT[:, e], k.ps[:, 2 + e, :].rearrange("p (c n) -> p c n", c=GC),
                                              ALU.subtract).then_inc(x_ready, 1)
                    for cc in range(GC):
                        c = g * GC + cc
                        w = p * NC + c
                        wait(dve, sa_psum, w + 1)
                        if c:
                            wait(dve, u_ready, w)
                            wait(dve, y_ready, w)
                        else:
                            wait(dve, y_ready, w)
                        dve.tensor_scalar(SA[:].rearrange("p (e n) -> p e n", e=2), k.ps[:, 0:2, 0:HD], -1.0, None, ALU.mult).then_inc(sa_ready, 1)
                        wait(dve, u_ready, w + 1)
                        mine.do(dve.tensor_tensor(Sc[:, c + 1], k.ps[:, 2, 0:HD], Sc[:, c], ALU.add))
                        dve.tensor_scalar(Sc[:, c + 1], Sc[:, c + 1], G[:, c:c + 1], None, ALU.mult).then_inc(S_ready, 1)
                        wait(dve, S_ready, w + 1)
                    wait(dve, y_ready, p * NC + (g * GC + GC))
                    dve.tensor_copy(t2[:, g * HALF:(g + 1) * HALF], k.ps[:, 4, :]).then_inc(y_taken, 1)
                wait(dve, mu_ready, p + 1)
                dve.scalar_tensor_tensor(t2[:], banks(k, 0), -1.0 / HD, t2[:], ALU.mult, ALU.add).then_inc(ysq_in, 1)
                wait(dve, rstd_ready, p + 1)
                mine.do(dve.tensor_tensor(t2[:], t2[:], t3[:], ALU.mult))
                mine.do(dve.tensor_scalar(t2[:], t2[:], cur[:, 9:10], cur[:, 10:11], ALU.mult, ALU.add))
                mine.do(dve.tensor_tensor(t2[:], t2[:], t1[:], ALU.add))
                wait(dve, ez_ready, p + 1)
                mine.do(dve.tensor_tensor(b[:], b[:], z, ALU.mult))
                dve.tensor_tensor(k.yrw[:, bass.ds(p, 1), :], t2[:].unsqueeze(1), b[:].unsqueeze(1), ALU.mult)\
                   .then_inc(pair_done, 1)
                wait(dve, pair_done, p + 1)
                assert mine.n == PER, mine.n

        @block.tensor
        def _(pe):
            pe.wait_ge(low_tanh, 1)
            for p in rounds(pe, PAIRS):
                wait(pe, pair_done, p)
                wait(pe, ld_lora, p * 16 * (1 + l) + 16 * (1 + l), 16 * (1 + l))
                for i in range(2):
                    mm = pe.matmul(k.ps[:, i, :], lora[0:HD, :], h2(lo[0:HD], i), start=True, stop=True)
                mm.then_inc(pre_ready, 1)
                for i in range(2):
                    mm = pe.matmul(k.ps[:, 2 + i, :], lora[HD:P, :], h2(lo[HD:P], i), start=True, stop=True)
                mm.then_inc(pre_ready, 1)
                if l:
                    for i in range(2):
                        mm = pe.matmul(k.ps[:, 4 + i, :], vup[:], h2(k.vd[:], i), start=True, stop=True)
                    mm.then_inc(pre_ready, 1)
                wait(pe, sq_ready, p + 1)
                for i in range(2):
                    mm = pe.matmul(k.ps[:, 6 + i, :], bones[:], h2(t2[:], i), start=True, stop=True)
                mm.then_inc(ss_ready, 1)
                for n, need in enumerate((1, 2, 3, 4)):
                    wait(pe, exps_ready, p * (2 + l) + (2 + l))
                    wait(pe, ssm_ready, p + 1)
                    wait(pe, ops_ready, p * 4 + need)
                    for c in range(NC):
                        src = (AR[:, c, 0, :], B[:, c * CH:(c + 1) * CH], Kd[:, c * CH:(c + 1) * CH],
                               raw[:, 2, 1 + c * CH:1 + (c + 1) * CH])[n]
                        tr = pe.transpose(k.ps[:, 2 * n + c // 4, (c % 4) * CH:(c % 4 + 1) * CH], src, k.eye[:])
                    tr.then_inc(tr_ready, 1)
                wait(pe, rk_ready, p + 1)
                wait(pe, tr_taken, p * 4 + 1)
                for i in range(2):
                    mm = pe.matmul(k.ps[:, i, :], bones[:], h2(t2[:], i), start=True, stop=True)
                mm.then_inc(bon_ready, 1)
                wait(pe, tr_taken, p * 4 + 4)
                wait(pe, bon_done, p + 1)
                for g in range(G2):
                    q = p * G2 + g
                    wait(pe, y_taken, q)
                    for n, lhs in enumerate((B, Kd)):
                        for e in range(2):
                            er = slice(e * HD, (e + 1) * HD)
                            for cc in range(GC):
                                c = g * GC + cc
                                mm = pe.matmul(k.ps[:, 4 * n + 2 * e + cc // 2, (cc % 2) * 256:(cc % 2 + 1) * 256],
                                               lhs[er, c * CH:(c + 1) * CH], AR[er, c, :, :].rearrange("p a n -> p (a n)"),
                                               start=True, stop=True)
                            mm.then_inc(pr_ready, 1)
                    for e in range(2):
                        er = slice(e * HD, (e + 1) * HD)
                        wait(pe, pr_taken, q * 4 + 1)
                        for cc in range(GC):
                            c = g * GC + cc
                            mm = pe.matmul(k.ps[:, e, cc * CH:(cc + 1) * CH], AR[er, c, 0, :], B[er, c * CH:(c + 1) * CH],
                                           start=True, stop=True)
                        mm.then_inc(l_ready, 1)
                    wait(pe, pr_taken, q * 4 + 4)
                    for e in range(2):
                        for cc in range(GC):
                            mm = pe.matmul(k.ps[:, 6, (e * GC + cc) * HD:(e * GC + cc + 1) * HD], MP[:, e, cc, 0, :],
                                           Vt[:, g * GC + cc, e * HD:(e + 1) * HD], start=True, stop=True)
                    mm.then_inc(mv_ready, 1)
                    for n in range(NLV):
                        for e in range(2):
                            wait(pe, x_ready, q * 2 * (NLV + 1) + (2 * n + e + 1))
                            wait(pe, ct_ready, q * 2 * NLV + (2 * n + e + 1))
                            wait(pe, yy_taken, q * 2 * NLV + (2 * (n - 1) + e + 1))
                            for cc in range(GC):
                                mm = pe.matmul(k.ps[:, e, cc * CH:(cc + 1) * CH], CT[:, e, cc, :], X[:, e, cc, :],
                                               start=True, stop=True)
                            mm.then_inc(yy_ready, 1)
                        for e in range(2):
                            wait(pe, yy_taken, q * 2 * NLV + (2 * n + e + 1))
                            for cc in range(GC):
                                mm = pe.matmul(k.ps[:, 2 + e, cc * CH:(cc + 1) * CH], Y[:, e, cc, :], XT[:, e, cc, :],
                                               start=True, stop=True)
                            if n < NLV - 1:
                                for cc in range(GC):
                                    mm = pe.matmul(k.ps[:, 4 + e, cc * CH:(cc + 1) * CH], XT[:, e, cc, :], Y[:, e, cc, :],
                                                   start=True, stop=True)
                            mm.then_inc(dx_ready, 1)
                    wait(pe, x_ready, q * 2 * (NLV + 1) + 2 * (NLV + 1))
                    for e in range(2):
                        for cc in range(GC):
                            mm = pe.matmul(k.ps[e * HD:(e + 1) * HD, 7, cc * CH:(cc + 1) * CH],
                                           At[:, g * GC + cc, e * HD:(e + 1) * HD], XT[:, e, cc, :], start=True, stop=True)
                    mm.then_inc(xa_ready, 1)
                    wait(pe, mv_taken, q + 1)
                    wait(pe, xa_taken, q + 1)
                    for cc in range(GC):
                        c = g * GC + cc
                        w = p * NC + c
                        for e in range(2):
                            pe.matmul(k.ps[:, e, 0:HD], XT[:, e, cc, :], MV[:, e, cc, :], start=True, stop=False)
                            if e == 0 and c:
                                wait(pe, S_ready, w)
                            mm = pe.matmul(k.ps[:, e, 0:HD], XA[e * HD:(e + 1) * HD, cc, :],
                                           Sc[e * HD:(e + 1) * HD, c, :], start=False, stop=True)
                        mm.then_inc(sa_psum, 1)
                        for e in range(2):
                            ec = slice(e * HD, (e + 1) * HD)
                            pe.matmul(k.ps[ec, 2, 0:HD], Kt[:, c, ec], Vt[:, c, ec], start=True, stop=False)
                            if e == 0:
                                wait(pe, sa_ready, w + 1)
                            mm = pe.matmul(k.ps[ec, 2, 0:HD], Bt[:, c, ec], SA[:, ec], start=False, stop=True)
                        mm.then_inc(u_ready, 1)
                        for e in range(2):
                            ec = slice(e * HD, (e + 1) * HD)
                            y = k.ps[ec, 4, cc * CH:(cc + 1) * CH]
                            pe.matmul(y, Vt[:, c, ec], MP[:, e, cc, 1, :], start=True, stop=False)
                            pe.matmul(y, SA[:, ec], LN[:, e, cc, 1, :], start=False, stop=False)
                            mm = pe.matmul(y, Sc[ec, c, :], AR[ec, c, 1, :], start=False, stop=True)
                        mm.then_inc(y_ready, 1)
                wait(pe, y_taken, p * G2 + G2)
                wait(pe, S_ready, p * NC + NC)
                for i in range(2):
                    mm = pe.matmul(k.ps[:, i, :], bones[:], h2(t2[:], i), start=True, stop=True)
                mm.then_inc(mu_ready, 1)
                wait(pe, ysq_ready, p + 1)
                for i in range(2):
                    mm = pe.matmul(k.ps[:, 2 + i, :], bones[:], h2(t3[:], i), start=True, stop=True)
                mm.then_inc(var_ready, 1)


def merge(k, l):
    nc, I = k.nc, k.I
    NJ = D // P
    with Stage(k, f"mix{l}") as s:
        hT, mT = s.sb("hT", [P, KT, T]), s.sb("mT", [P, KT, T])
        sc1, gate, gcur = s.sb("sc1", [P, KT]), s.sb("gate", [P, KT]), s.sb("gcur", [P, 1])
        lnp = s.sb("lnp", [P, 2, KT])
        w = s.sb("w", [P, 2, 24, P])
        wo = w[:, :, 0:KT, :]
        sg = s.sb("sg", [P, 2, 2 * HALF])
        t = s.sb("t", [P, T])
        rstd = s.sb("rstd", [P, T])
        ld_w, ld_wo = [s.sem("ld_w0"), s.sem("ld_w1")], [s.sem("ld_wo0"), s.sem("ld_wo1")]
        ld_p = s.sem("ld_p")
        (h_ready, gates_ready, ys_ready, sg_ready, mul_done, m_ready, gate_in, gcur_ready, o_ready, t_ready, x_ready,
         mean_ready, xc_ready, sq_ready, var_ready, own_a, rstd_ready, own) = (s.sem(n) for n in (
             "h_ready gates_ready ys_ready sg_ready mul_done m_ready gate_in gcur_ready o_ready t_ready x_ready "
             "mean_ready xc_ready sq_ready var_ready own_a rstd_ready own").split())
        block = s.block()

        @block.sync
        def _(sp):
            for i in rounds(sp, NJ // 2):
                for b in range(2):
                    j = i * 2 + b
                    wait(sp, ys_ready, 2 * j - 2)
                    sp.dma_start(w[:, b, 0:8], I["w_in"][l, j + CG1]).then_inc(ld_w[b], 16)
                    sp.dma_start(w[:, b, 8:16], I["w_in"][l, j + CG2]).then_inc(ld_w[b], 16)
                    sp.dma_start(w[:, b, 16:20], I["w_branch_hg"][l, j]).then_inc(ld_w[b], 16)
                    sp.dma_start(w[:, b, 20:24], I["w_branch_rw"][l, j]).then_inc(ld_w[b], 16)
            sp.dma_start(lnp[:], I["ln_par"][l]).then_inc(ld_p, 16)
            for i in rounds(sp, NJ // 2):
                for b in range(2):
                    j = i * 2 + b
                    if isinstance(i, int):
                        sp.wait_ge(ys_ready, 2 * (NJ - 1 + b))
                    wait(sp, o_ready, 2 * j - 2)
                    sp.dma_start(wo[:, b], I["w_out"][l, j]).then_inc(ld_wo[b], 16)

        @block.scalar
        def _(act):
            mine = Steps(act, own_a)
            for j in rounds(act, NJ):
                for half in range(2):
                    wait(act, gates_ready, j * 2 + (half + 1))
                    wait(act, mul_done, j * 2 + (half - 1))
                    act.activation(sg[:, half], banks(k, 4 * half), ACT.Sigmoid).then_inc(sg_ready, 1)
            for j in rounds(act, NJ):
                wait(act, gcur_ready, j + 1)
                wait(act, x_ready, j)
                for half in range(2):
                    wait(act, o_ready, j * 2 + (half + 1))
                    hs = slice(half * HALF, (half + 1) * HALF)
                    act.activation(t[:, hs], k.ps[:, half, :], ACT.Copy, scale=gcur[:, 0:1]).then_inc(t_ready, 1)
            for j in range(KT):
                act.wait_ge(xc_ready, j + 1)
                act.activation(mT[:, j], k.xT[:, j], ACT.Square).then_inc(sq_ready, 1)
            act.wait_ge(var_ready, 1)
            mine.do(act.activation(rstd[:], banks(k, 4), ACT.Ln, scale=1.0 / D, bias=LN_EPS))
            act.activation(rstd[:], rstd[:], ACT.Exp, scale=-0.5).then_inc(rstd_ready, 1)

        @block.vector
        def _(dve):
            mine = Steps(dve, own)
            modulate(dve, Steps(dve, h_ready), k, hT, l, sc1)
            c = l * NADA1 + 2 * KT
            mine.do(dve.tensor_scalar(gate[:], k.cond[:, c:c + KT, 0], 1.0, None, ALU.add))
            for j in rounds(dve, NJ):
                for half in range(2):
                    hs = slice(half * HALF, (half + 1) * HALF)
                    wait(dve, ys_ready, j * 2 + (half + 1))
                    wait(dve, sg_ready, j * 2 + (half + 1))
                    dve.tensor_tensor(sg[:, half], sg[:, half], banks(k, 4 * half + 2), ALU.mult).then_inc(m_ready, 1)
                    wait(dve, m_ready, j * 2 + (half + 1))
                    dve.tensor_tensor(mT[:, bass.ds(j, 1), hs], sg[:, half, 0:HALF].unsqueeze(1),
                                      sg[:, half, HALF:T].unsqueeze(1), ALU.add).then_inc(mul_done, 1)
            BASE = mine.n
            for j in rounds(dve, NJ):
                wait(dve, t_ready, j * 2)
                dve.tensor_copy(gcur[:], gate[:, bass.ds(j, 1)]).then_inc(gcur_ready, 1)
                wait(dve, t_ready, j * 2 + 2)
                xj = k.xT[:, bass.ds(j, 1), :]
                dve.scalar_tensor_tensor(xj, xj, ALPHA, t[:].unsqueeze(1), ALU.mult, ALU.add).then_inc(x_ready, 1)
            dve.wait_ge(ld_p, 16)
            dve.wait_ge(mean_ready, 1)
            dve.wait_ge(x_ready, NJ)
            for j in range(KT):
                dve.scalar_tensor_tensor(k.xT[:, j], banks(k, 2), -1.0 / D, k.xT[:, j], ALU.mult, ALU.add).then_inc(xc_ready, 1)
            dve.wait_ge(xc_ready, KT)
            dve.wait_ge(sq_ready, KT)
            dve.wait_ge(rstd_ready, 1)
            for j in range(KT):
                mine.mark(dve.tensor_tensor(k.xT[:, j], k.xT[:, j], rstd[:], ALU.mult))
            mine.settle()
            for j in range(KT):
                mine.mark(dve.tensor_scalar(k.xT[:, j], k.xT[:, j], lnp[:, 0, j:j + 1], lnp[:, 1, j:j + 1], ALU.mult, ALU.add))
            mine.settle()

        @block.tensor
        def _(pe):
            for i in rounds(pe, NJ // 2):
                for b in range(2):
                    wait(pe, ld_w[b], i * 64 + 64, 64)
                    j = i * 2 + b
                    if isinstance(j, int) and j == 0:
                        pe.wait_ge(h_ready, KT + 1)
                    for half in range(2):
                        hs = slice(half * HALF, (half + 1) * HALF)
                        wait(pe, mul_done, j * 2 + (half - 1))
                        for g in range(2):
                            for x in range(KT):
                                mm = pe.matmul(k.ps[:, 4 * half + g, :], w[:, b, 8 * g + x, :], hT[:, x, hs],
                                               start=(x == 0), stop=(x == KT - 1))
                        mm.then_inc(gates_ready, 1)
                        for g, y in enumerate((k.yhg, k.yrw)):
                            for x in range(4):
                                mm = pe.matmul(k.ps[:, 4 * half + 2 + g, :], w[:, b, 16 + 4 * g + x, :], y[:, x, hs],
                                               start=(x == 0), stop=(x == 3))
                        mm.then_inc(ys_ready, 1)
            pe.wait_ge(mul_done, 2 * NJ)
            for i in rounds(pe, NJ // 2):
                for b in range(2):
                    j = i * 2 + b
                    wait(pe, ld_wo[b], i * 16 + 16, 16)
                    for half in range(2):
                        wait(pe, t_ready, j * 2 + (half - 1))
                        for x in range(KT):
                            mm = pe.matmul(k.ps[:, half, :], wo[:, b, x, :], mT[:, x, half * HALF:(half + 1) * HALF],
                                           start=(x == 0), stop=(x == KT - 1))
                        mm.then_inc(o_ready, 1)
            for x in range(KT):
                pe.wait_ge(x_ready, x + 1)
                for half in range(2):
                    mm = pe.matmul(k.ps[:, 2 + half, :], k.ones[:], k.xT[:, x, half * HALF:(half + 1) * HALF],
                                   start=(x == 0), stop=(x == KT - 1))
            mm.then_inc(mean_ready, 1)
            for x in range(KT):
                pe.wait_ge(sq_ready, x + 1)
                for half in range(2):
                    mm = pe.matmul(k.ps[:, 4 + half, :], k.ones[:], mT[:, x, half * HALF:(half + 1) * HALF],
                                   start=(x == 0), stop=(x == KT - 1))
            mm.then_inc(var_ready, 1)


CTX = 256
NKC = CTX // P
HD2 = 64
SCALE2 = HD2 ** -0.5
QH = 4
W2Q, W2K, W2V, W2P = 0, 4, 5, 6
POOLS = (2, 4, 8, 16)
PAD = 8
C2 = 2 * NADA1


def rms_modulated(k, name, jobs):
    nc, I = k.nc, k.I
    with Stage(k, name) as s:
        gain = s.sb("gain", [P, 2, KT])
        coef = s.sb("coef", [P, len(jobs), KT])
        rstd = s.sb("rstd", [P, len(jobs), T])
        ld, sq_ready, ss_ready, own_a, rstd_ready, own, scaled, done = (
            s.sem(n) for n in "ld sq_ready ss_ready own_a rstd_ready own scaled done".split())
        block = s.block()

        @block.sync
        def _(sp):
            sp.dma_start(gain[:], I["norm_g"]).then_inc(ld, 16)

        @block.scalar
        def _(act):
            mine = Steps(act, own_a)
            for i, (src, dst, N, g, c, v) in enumerate(jobs):
                for j in range(KT):
                    act.activation(dst[:, j, 0:N], src[:, j, 0:N], ACT.Square).then_inc(sq_ready, 1)
            for i, (src, dst, N, g, c, v) in enumerate(jobs):
                act.wait_ge(ss_ready, i + 1)
                ss = banks(k, 2 * i)[:, 0:N]
                mine.do(act.activation(rstd[:, i, 0:N], ss, ACT.Ln, scale=1.0 / D, bias=EPS))
                act.activation(rstd[:, i, 0:N], rstd[:, i, 0:N], ACT.Exp, scale=-0.5).then_inc(rstd_ready, 1)
                for j in range(KT):
                    act.wait_ge(scaled, i * KT + j + 1)
                    act.activation(dst[:, j, 0:N], dst[:, j, 0:N], ACT.Identity, bias=k.cond[:, c + j, v:v + 1]).then_inc(done, 1)

        @block.tensor
        def _(pe):
            for i, (src, dst, N, g, c, v) in enumerate(jobs):
                for j in range(KT):
                    pe.wait_ge(sq_ready, i * KT + j + 1)
                    for a in range(0, N, HALF):
                        n = min(HALF, N - a)
                        mm = pe.matmul(banks(k, 2 * i)[:, a:a + n], k.ones[:], dst[:, j, a:a + n], start=(j == 0), stop=(j == KT - 1))
                mm.then_inc(ss_ready, 1)

        @block.vector
        def _(dve):
            mine = Steps(dve, own)
            dve.wait_ge(ld, 16)
            for i, (src, dst, N, g, c, v) in enumerate(jobs):
                mine.do(dve.tensor_scalar(coef[:, i], k.cond[:, c + KT:c + 2 * KT, v], 1.0, None, ALU.add))
                mine.do(dve.tensor_tensor(coef[:, i], coef[:, i], gain[:, g], ALU.mult))
                dve.wait_ge(rstd_ready, i + 1)
                for j in range(KT):
                    dve.scalar_tensor_tensor(dst[:, j, 0:N], src[:, j, 0:N], coef[:, i, j:j + 1], rstd[:, i, 0:N],
                                             ALU.mult, ALU.mult).then_inc(scaled, 1)


def attention(k, hcT):
    nc, I = k.nc, k.I
    NB = T // P
    SW = CTX + 3 * P
    with Stage(k, "attn") as s:
        w = s.sb("w", [P, KT, P])
        wkv = s.sb("wkv", [P, 2, KT, P])
        cos, sin, rot = s.sb("cos", [P, T]), s.sb("sin", [P, T]), s.sb("rot", [P, P])
        kT, qT, raw = s.sb("kT", [P, CTX + T]), s.sb("qT", [P, T]), s.sb("raw", [P, T])
        vt = s.sb("vt", [P, NKC + NB, P])
        band = s.sb("band", [P, 3 * P])
        sink, scur = s.sb("sink", [P, QH, 2]), s.sb("scur", [P, 2])
        S = s.sb("S", [P, 2, SW])
        PT = s.sb("PT", [P, 2, 5, P])
        st = s.sb("st", [P, 2, 6])
        names = ("ld_c ld_kv ld_q kp_ready k_raw rot_ready kc_taken own vps_ready v_taken "
                 "q_ready q_raw qrot_ready q_done s_ready s_loc s_ctx max_ready e_ready es_ready p_ready pt_ready "
                 "pt_taken o_ready o_taken")
        (ld_c, ld_kv, ld_q, kp_ready, k_raw, rot_ready, kc_taken, own, vps_ready, v_taken,
         q_ready, q_raw, qrot_ready, q_done, s_ready, s_loc, s_ctx, max_ready, e_ready, es_ready, p_ready, pt_ready,
         pt_taken, o_ready, o_taken) = (s.sem(n) for n in names.split())
        block = s.block()
        mix = k.mix

        def width(n):
            a = max(n - 1, 0)
            return a, min(n + 1, NB - 1) - a + 1

        @block.sync
        def _(sp):
            sp.dma_start(wkv[:, 0], I["w_in2"][W2K]).then_inc(ld_kv, 16)
            sp.dma_start(wkv[:, 1], I["w_in2"][W2V]).then_inc(ld_kv, 16)
            sp.dma_start(rot[:], I["rot"]).then_inc(ld_c, 16)
            sp.dma_start(cos[:], I["cos"]).then_inc(ld_c, 16)
            sp.dma_start(sin[:], I["sin"]).then_inc(ld_c, 16)
            sp.dma_start(band[:], I["band"]).then_inc(ld_c, 16)
            sp.dma_start(sink[:], I["sink"]).then_inc(ld_c, 16)
            for j in rounds(sp, QH):
                wait(sp, q_ready, j)
                sp.dma_start(w[:], I["w_in2"][j + W2Q]).then_inc(ld_q, 16)

        @block.scalar
        def _(act):
            act.wait_ge(kp_ready, 1)
            act.activation(raw[:], banks(k, 0), ACT.Copy).then_inc(k_raw, 1)
            act.wait_ge(kp_ready, 2)
            act.activation(kT[:, 0:CTX], k.ps[:, 2, 0:CTX], ACT.Copy).then_inc(kc_taken, 1)
            act.wait_ge(vps_ready, 1)
            act.activation(vt[:, 0:NKC + 2, :].rearrange("p a n -> p (a n)"), k.ps[:, 5, :], ACT.Copy).then_inc(v_taken, 1)
            act.wait_ge(vps_ready, 2)
            act.activation(vt[:, NKC + 2:NKC + 6, :].rearrange("p a n -> p (a n)"), k.ps[:, 6, :], ACT.Copy).then_inc(v_taken, 1)
            act.wait_ge(vps_ready, 3)
            act.activation(vt[:, NKC + 6:NKC + 8, :].rearrange("p a n -> p (a n)"), k.ps[:, 7, 0:2 * P], ACT.Copy).then_inc(v_taken, 1)
            for j in rounds(act, QH):
                if isinstance(j, int):
                    act.wait_ge(own, 1)
                wait(act, q_ready, j + 1)
                act.activation(raw[:], banks(k, 0), ACT.Copy).then_inc(q_raw, 1)
                for n in range(NB):
                    a, nb = width(n)
                    u = j * 2 * NB + 2 * n
                    for e in range(2):
                        wait(act, s_ready, u + (e + 1))
                        wait(act, pt_ready, u + (e - 1))
                        act.activation(S[:, e, 0:CTX], k.ps[:, 2 * e + 1, 0:CTX], ACT.Copy, scale=SCALE2).then_inc(s_ctx, 1)
                    for e in range(2):
                        wait(act, max_ready, u + (e + 1))
                        act.activation(S[:, e, 0:CTX + nb * P], S[:, e, 0:CTX + nb * P], ACT.Exp, bias=st[:, e, 1:2],
                                       accum_out=st[:, e, 2:3]).then_inc(e_ready, 1)
                        act.activation(st[:, e, 3:4], scur[:, e:e + 1], ACT.Exp, bias=st[:, e, 1:2]).then_inc(es_ready, 1)
                    for e in range(2):
                        wait(act, pt_ready, u + (e + 1))
                        wait(act, o_ready, u + (e - 1))
                        act.activation(PT[:, e, 0:4, :].rearrange("p a n -> p (a n)"), k.ps[:, 4 + e, :], ACT.Copy).then_inc(pt_taken, 1)

        @block.vector
        def _(dve):
            mine = Steps(dve, own)

            def rope(dst, rotated):
                mine.do(dve.tensor_tensor(dst, raw[:], cos[:], ALU.mult))
                mine.do(dve.tensor_tensor(raw[:], rotated, sin[:], ALU.mult))
                return dve.tensor_tensor(dst, dst, raw[:], ALU.add)

            dve.wait_ge(ld_c, 80)
            dve.wait_ge(rot_ready, 1)
            dve.tensor_tensor(kT[:, CTX:], raw[:], cos[:], ALU.mult).then_inc(k_raw, 1)
            dve.wait_ge(k_raw, 2)
            dve.tensor_tensor(raw[:], banks(k, 3), sin[:], ALU.mult).then_inc(k_raw, 1)
            dve.wait_ge(k_raw, 3)
            dve.tensor_tensor(kT[:, CTX:], kT[:, CTX:], raw[:], ALU.add).then_inc(own, 1)
            BASE, PER = 1, 3 + NB * 2 * 3
            for j in rounds(dve, QH):
                mine.loop(j * PER + BASE)
                mine.mark(dve.tensor_copy(scur[:].unsqueeze(1), sink[:, bass.ds(j, 1), :]))
                wait(dve, qrot_ready, j + 1)
                rope(qT[:], banks(k, 2)).then_inc(q_done, 1)
                for n in range(NB):
                    a, nb = width(n)
                    u = j * 2 * NB + 2 * n
                    b0 = (a - (n - 1)) * P
                    for e in range(2):
                        wait(dve, s_ready, u + (e + 1))
                        wait(dve, pt_ready, u + (e - 1))
                        dve.scalar_tensor_tensor(S[:, e, CTX:CTX + nb * P], k.ps[:, 2 * e, 0:nb * P], SCALE2,
                                                 band[:, b0:b0 + nb * P], ALU.mult, ALU.add).then_inc(s_loc, 1)
                        wait(dve, s_loc, u + (e + 1))
                        wait(dve, s_ctx, u + (e + 1))
                        mine.do(dve.tensor_reduce(st[:, e, 0:1], S[:, e, 0:CTX + nb * P], AX, ALU.max))
                        dve.tensor_scalar(st[:, e, 1:2], st[:, e, 0:1], scur[:, e:e + 1], -1.0, ALU.max, ALU.mult).then_inc(max_ready, 1)
                    for e in range(2):
                        wait(dve, e_ready, u + (e + 1))
                        wait(dve, es_ready, u + (e + 1))
                        mine.do(dve.tensor_tensor(st[:, e, 4:5], st[:, e, 2:3], st[:, e, 3:4], ALU.add))
                        mine.do(dve.reciprocal(st[:, e, 5:6], st[:, e, 4:5]))
                        dve.tensor_scalar(S[:, e, 0:CTX + nb * P], S[:, e, 0:CTX + nb * P], st[:, e, 5:6], None, ALU.mult)\
                           .then_inc(p_ready, 1)
                    if nb == 3:
                        for e in range(2):
                            wait(dve, pt_ready, u + 2)
                            wait(dve, o_ready, u + (e - 1))
                            dve.tensor_copy(PT[:, e, 4, :], k.ps[:, 6, e * P:(e + 1) * P]).then_inc(pt_taken, 1)
                    wait(dve, o_ready, u + 2)
                    dve.tensor_copy(mix[:, bass.ds(j, 1), n * P:(n + 1) * P], k.ps[:, 7:8, 0:P]).then_inc(o_taken, 1)
                assert mine.n == PER, mine.n

        @block.tensor
        def _(pe):
            pe.wait_ge(ld_kv, 32)
            for half in range(2):
                for t in range(KT):
                    mm = pe.matmul(k.ps[:, half, :], wkv[:, 0, t, :], k.hT2[:, t, half * HALF:(half + 1) * HALF],
                                   start=(t == 0), stop=(t == KT - 1))
            mm.then_inc(kp_ready, 1)
            for t in range(KT):
                mm = pe.matmul(k.ps[:, 2, 0:CTX], wkv[:, 0, t, :], hcT[:, t, :], start=(t == 0), stop=(t == KT - 1))
            mm.then_inc(kp_ready, 1)
            for g, tiles in enumerate(((-2, -1, 0, 1), (2, 3, 4, 5), (6, 7))):
                for i, a in enumerate(tiles):
                    for t in range(KT):
                        lhs = hcT[:, t, (a + 2) * P:(a + 3) * P] if a < 0 else k.hT2[:, t, a * P:(a + 1) * P]
                        mm = pe.matmul(k.ps[:, 5 + g, i * P:(i + 1) * P], lhs, wkv[:, 1, t, :], start=(t == 0), stop=(t == KT - 1))
                mm.then_inc(vps_ready, 1)
            pe.wait_ge(ld_c, 80)
            pe.wait_ge(k_raw, 1)
            for half in range(2):
                mm = pe.matmul(k.ps[:, 3 + half, :], rot[:], raw[:, half * HALF:(half + 1) * HALF], start=True, stop=True)
            mm.then_inc(rot_ready, 1)
            pe.wait_ge(v_taken, 3)
            pe.wait_ge(kc_taken, 1)
            pe.wait_ge(own, 1)
            for j in rounds(pe, QH):
                wait(pe, ld_q, j * 16 + 16, 16)
                wait(pe, e_ready, j * 2 * NB)
                for half in range(2):
                    for t in range(KT):
                        mm = pe.matmul(k.ps[:, half, :], w[:, t, :], k.hT2[:, t, half * HALF:(half + 1) * HALF],
                                       start=(t == 0), stop=(t == KT - 1))
                mm.then_inc(q_ready, 1)
                wait(pe, q_raw, j + 1)
                for half in range(2):
                    mm = pe.matmul(k.ps[:, 2 + half, :], rot[:], raw[:, half * HALF:(half + 1) * HALF], start=True, stop=True)
                mm.then_inc(qrot_ready, 1)

                def scores(n):
                    a, nb = width(n)
                    u = j * 2 * NB + 2 * n
                    for e in range(2):
                        er = slice(e * HD2, (e + 1) * HD2)
                        if n == 0:
                            wait(pe, q_done, j + 1)
                        else:
                            wait(pe, s_loc, u + (e - 1))
                            wait(pe, s_ctx, u + (e - 1))
                        pe.matmul(k.ps[:, 2 * e, 0:nb * P], qT[er, n * P:(n + 1) * P], kT[er, CTX + a * P:CTX + (a + nb) * P],
                                  start=True, stop=True)
                        pe.matmul(k.ps[:, 2 * e + 1, 0:CTX], qT[er, n * P:(n + 1) * P], kT[er, 0:CTX],
                                  start=True, stop=True).then_inc(s_ready, 1)

                scores(0)
                for n in range(NB):
                    a, nb = width(n)
                    u = j * 2 * NB + 2 * n
                    if n + 1 < NB:
                        scores(n + 1)
                    taken = sum(4 if width(m)[1] == 3 else 2 for m in range(n))
                    per = sum(4 if width(m)[1] == 3 else 2 for m in range(NB))
                    for e in range(2):
                        wait(pe, p_ready, u + (e + 1))
                        wait(pe, pt_taken, j * per + taken)
                        for i in range(NKC + nb):
                            out = k.ps[:, 4 + e, i * P:(i + 1) * P] if i < 4 else k.ps[:, 6, e * P:(e + 1) * P]
                            tr = pe.transpose(out, S[:, e, i * P:(i + 1) * P], k.eye[:])
                        tr.then_inc(pt_ready, 1)
                    wait(pe, o_taken, j * NB + n)
                    wait(pe, pt_taken, j * per + (taken + (4 if nb == 3 else 2)))
                    for e in range(2):
                        ec = slice(e * HD2, (e + 1) * HD2)
                        for i in range(NKC + nb):
                            v = vt[:, i if i < NKC else NKC + a + i - NKC, ec]
                            mm = pe.matmul(k.ps[ec, 7, 0:P], v, PT[:, e, i, :], start=(i == 0), stop=(i == NKC + nb - 1))
                        mm.then_inc(o_ready, 1)


def pooling(k):
    nc, I = k.nc, k.I
    NG = len(POOLS)
    with Stage(k, "pool") as s:
        w, pw = s.sb("w", [P, 2, KT, P]), s.sb("pw", [P, NG, P])
        inv, scale = s.sb("inv", [P, NG, T]), s.sb("scale", [P, NG])
        pp = s.sb("pp", [P, 2, T + 2 * PAD])
        ws = s.sb("ws", [P, 2, T + 2 * PAD])
        ld_w, ld_c = [s.sem("ld_w0"), s.sem("ld_w1")], s.sem("ld_c")
        p_ready, p_taken, d_ready, y_ready, y_taken, own = (s.sem(n) for n in "p_ready p_taken d_ready y_ready y_taken own".split())
        block = s.block()

        @block.sync
        def _(sp):
            for g in range(NG):
                if g == 2:
                    sp.dma_start(pw[:], I["pool_w"]).then_inc(ld_c, 16)
                    sp.dma_start(inv[:], I["pool_inv"]).then_inc(ld_c, 16)
                    sp.dma_start(scale[:], I["pool_scale"]).then_inc(ld_c, 16)
                if g >= 2:
                    sp.wait_ge(p_ready, g - 1)
                sp.dma_start(w[:, g % 2], I["w_in2"][W2P + g]).then_inc(ld_w[g % 2], 16)

        @block.tensor
        def _(pe):
            def product(g):
                pe.wait_ge(d_ready, g + 1)
                if g:
                    pe.wait_ge(y_taken, g)
                for half in range(2):
                    mm = pe.matmul(k.ps[:, 4 + half, :], pw[:, g, :], ws[:, 0, half * HALF:(half + 1) * HALF], start=True, stop=True)
                mm.then_inc(y_ready, 1)

            for g in range(NG):
                pe.wait_ge(ld_w[g % 2], 16 * (g // 2 + 1))
                if g >= 2:
                    pe.wait_ge(p_taken, g - 1)
                for half in range(2):
                    for t in range(KT):
                        mm = pe.matmul(k.ps[:, 2 * (g % 2) + half, :], w[:, g % 2, t, :], k.hT2[:, t, half * HALF:(half + 1) * HALF],
                                       start=(t == 0), stop=(t == KT - 1))
                mm.then_inc(p_ready, 1)
                if g:
                    product(g - 1)
            product(NG - 1)

        @block.scalar
        def _(act):
            act.wait_ge(own, 1)
            for g in range(NG):
                act.wait_ge(p_ready, g + 1)
                if g >= 2:
                    act.wait_ge(d_ready, g - 1)
                act.activation(pp[:, g % 2, PAD:PAD + T], banks(k, 2 * (g % 2)), ACT.Copy).then_inc(p_taken, 1)
                if g:
                    act.wait_ge(ld_c, 48)
                    act.wait_ge(y_ready, g)
                    act.activation(k.mix[:, 4 + g - 1, :], banks(k, 4), ACT.Copy, scale=scale[:, g - 1:g]).then_inc(y_taken, 1)
            act.wait_ge(y_ready, NG)
            act.activation(k.mix[:, 3 + NG, :], banks(k, 4), ACT.Copy, scale=scale[:, NG - 1:NG]).then_inc(y_taken, 1)

        @block.vector
        def _(dve):
            mine = Steps(dve, own)
            mine.do(dve.memset(pp[:], 0.0))
            dve.wait_ge(ld_c, 48)
            for g, win in enumerate(POOLS):
                dve.wait_ge(p_taken, g + 1)
                if g:
                    dve.wait_ge(y_ready, g)
                src, n, step = pp[:, g % 2], T + 2 * PAD, 1
                for i in range(g + 1):
                    n -= step
                    dst = ws[:, i % 2]
                    mine.do(dve.tensor_tensor(dst[:, 0:n], src[:, 0:n], src[:, step:step + n], ALU.add))
                    src, step = dst, 2 * step
                first = PAD - win // 2
                mine.do(dve.tensor_tensor(ws[:, (g + 1) % 2, 0:T], src[:, first:first + T], inv[:, g], ALU.mult))
                dve.tensor_tensor(ws[:, 0, 0:T], ws[:, (g + 1) % 2, 0:T], pp[:, g % 2, PAD:PAD + T], ALU.subtract).then_inc(d_ready, 1)
                dve.wait_ge(d_ready, g + 1)


def project_out(k):
    nc, I = k.nc, k.I
    with Stage(k, "out") as s:
        w = s.sb("w", [P, 2, KT, P])
        ld_w = [s.sem("ld_w0"), s.sem("ld_w1")]
        o_ready, taken = s.sem("o_ready"), s.sem("taken")
        block = s.block()

        @block.sync
        def _(sp):
            for j in range(KT):
                if j >= 2:
                    sp.wait_ge(o_ready, j - 1)
                sp.dma_start(w[:, j % 2], I["w_out2"][j]).then_inc(ld_w[j % 2], 16)

        @block.tensor
        def _(pe):
            for j in range(KT):
                pe.wait_ge(ld_w[j % 2], 16 * (j // 2 + 1))
                if j >= 2:
                    pe.wait_ge(taken, j - 1)
                for half in range(2):
                    for t in range(KT):
                        mm = pe.matmul(k.ps[:, 2 * (j % 2) + half, :], w[:, j % 2, t, :], k.mix[:, t, half * HALF:(half + 1) * HALF],
                                       start=(t == 0), stop=(t == KT - 1))
                mm.then_inc(o_ready, 1)

        @block.vector
        def _(dve):
            for j in range(KT):
                dve.wait_ge(o_ready, j + 1)
                dve.scalar_tensor_tensor(k.xT[:, j], banks(k, 2 * (j % 2)), k.cond[:, C2 + 2 * KT + j, 1:2], k.xT[:, j],
                                         ALU.mult, ALU.add).then_inc(taken, 1)

NE = 64
NG = 8
TOPG, TOPK = 4, 8
DE = 256
ROUTED_SCALE = 2.5
NTT = T // P
NBLK = NE + T * TOPK // P
assert NBLK >= NE - 1 + T * TOPK // P and NBLK <= P
NR = NBLK // 2
BIG = 1e30


def used_rounds(eng, k):
    final = eng.snap(eng.value_load(k.nr[0:1, 0:1], min_val=0, max_val=NR - NE // 2) + (NE // 2 - 1))
    yield 0, False
    yield 1, False
    with eng.Fori(2, NR - 1) as i:
        with eng.If(i < final):
            yield i, False
    yield final, True


def route(k):
    nc, I = k.nc, k.I
    acc = k.mix
    with Stage(k, "route") as s:
        wr, bias = s.sb("wr", [P, KT, NE]), s.sb("bias", [P, NE])
        lower = s.sb("lower", [P, NG, NG])
        causal = s.sb("causal", [P, P])
        pidx, tokid = s.sb("pidx", [P, 1]), s.sb("tokid", [P, NTT], I32)
        zero = s.sb("zero", [P, NBLK], I32)
        sc, bi, sel, mask, gate, key = (s.sb(n, [P, NTT, NE]) for n in ("sc", "bi", "sel", "mask", "gate", "key"))
        u1, u2 = s.sb("u1", [P, NTT, NG, 4]), s.sb("u2", [P, NTT, NG, 4])
        v1, v2, v3 = (s.sb(n, [P, NTT, NG, 4]) for n in ("v1", "v2", "v3"))
        cmp = s.sb("cmp", [P, NTT, NG, NG])
        gs, gm, top = s.sb("gs", [P, NTT, NG]), s.sb("gm", [P, NTT, NG]), s.sb("top", [P, NTT, 8])
        tot = s.sb("tot", [P, NTT])
        ri, qi = s.sb("ri", [P, NTT * NE], I32), s.sb("qi", [P, NTT * NE], I32)
        ci, nb, end = s.sb("ci", [P, NE], I32), s.sb("nb", [P, NE]), s.sb("end", [P, NE])
        slotv, ebf, ebi = s.sb("slotv", [P, NTT, 8]), s.sb("ebf", [P, 1]), s.sb("ebi", [P, 1], I32)
        pick = s.sb("pick", [P, 8, NE])
        cmp2 = pick[:].rearrange("p t (g n) -> p t g n", g=NG)
        hrow = s.sb("hrow", [P, 2, D])
        wgu, wd = s.sb("wgu", [P, 2, 2, KT, P]), s.sb("wd", [P, 2, D])
        aT = s.sb("aT", [P, 2, T])
        sg = hrow[:, 0]
        names = ("ld_c ld_z z_set st_z ld_s ld_d lg_ready sc_ready own mask_ready rank_ready slots_ready st_slot eb_ready st_eb ld_back "
                 "h_ready h_taken st_h0 st_h1 g_ready u_ready sg_ready act_ready d_ready d_taken tq")
        (ld_c, ld_z, z_set, st_z, ld_s, ld_d, lg_ready, sc_ready, own, mask_ready, rank_ready, slots_ready, st_slot, eb_ready, st_eb,
         ld_back, h_ready, h_taken, st_h0, st_h1, g_ready, u_ready, sg_ready, act_ready, d_ready, d_taken, tq) = (
            s.sem(n) for n in names.split())
        st_h = [st_h0, st_h1]
        block = s.block()
        rowtok, ebd = k.scratch["rowtok"], k.scratch["ebd"]

        @block.sync
        def _(sp):
            for dst, src in ((wr, "w_router"), (bias, "router_bias"), (lower, "lower_groups"), (causal, "causal"),
                             (pidx, "pidx"), (tokid, "tokid")):
                sp.dma_start(dst[:], I[src]).then_inc(ld_c, 16)
            sp.wait_ge(z_set, 1)
            sp.dma_start(rowtok.rearrange("(p b) o -> p (b o)", p=P), zero[:]).then_inc(st_z, 16)
            sp.dma_start(wgu[:], I["ws_gu"]).then_inc(ld_s, 16)
            sp.dma_start(wd[:], I["ws_down"]).then_inc(ld_d, 16)
            sp.wait_ge(eb_ready, 1)
            sp.dma_start(ebd[:, :], ebi[:]).then_inc(st_eb, 16)
            sp.wait_ge(st_eb, 16)
            sp.dma_start(k.eb[:], ebd.rearrange("p o -> o p")).then_inc(ld_back, 16)
            sp.wait_ge(st_slot, 16 * NTT * TOPK)
            sp.dma_start(k.idx[:], rowtok.rearrange("(p b) o -> p (b o)", p=P)).then_inc(ld_back, 16)
            sp.wait_ge(ld_back, 32)

        @block.gpsimd
        def _(pool):
            pool.memset(zero[:], 0).then_inc(z_set, 1)
            pool.wait_ge(st_z, 16)
            pool.wait_ge(slots_ready, 1)
            for i in range(NTT):
                for j in range(TOPK):
                    pool.indirect_dma_start(rowtok, bass.IndirectOffsetOnAxis(ap=k.slot[:, i, j:j + 1], axis=0),
                                            tokid[:, i:i + 1], None).then_inc(st_slot, 16)
            pool.wait_ge(st_slot, 16 * NTT * TOPK)

        @block.scalar
        def _(act):
            act.wait_ge(lg_ready, 1)
            act.activation(sc[:].rearrange("p a e -> p (a e)"), k.ps[:, 0, :], ACT.Sigmoid).then_inc(sc_ready, 1)
            for i in range(NTT):
                act.wait_ge(h_ready, i + 1)
                if i >= 2:
                    act.wait_ge(st_h[i % 2], 16 * (i // 2))
                act.activation(hrow[:, i % 2, :], banks(k, 2 + 2 * (i % 2)), ACT.Copy).then_inc(h_taken, 1)
                act.wait_ge(h_taken, i + 1)
                act.dma_start(k.scratch["hrow"][i * P:(i + 1) * P, :], hrow[:, i % 2, :]).then_inc(st_h[i % 2], 16)
            for f in range(2):
                act.wait_ge(g_ready, f + 1)
                if f:
                    act.wait_ge(act_ready, f)
                act.wait_ge(st_h[0], 16 * NTT // 2)
                act.activation(sg, banks(k, 2), ACT.Sigmoid).then_inc(sg_ready, 1)
                act.wait_ge(sg_ready, 2 * f + 1)
                act.activation(aT[:, f], banks(k, 2), ACT.Copy).then_inc(sg_ready, 1)
            for i in range(NTT):
                act.wait_ge(d_ready, i + 1)
                act.activation(acc[:, i], banks(k, 2 + 2 * (i % 2)), ACT.Copy).then_inc(d_taken, 1)
            for b in range(2):
                act.wait_ge(st_h[b], 16 * NTT // 2)

        @block.vector
        def _(dve):
            mine = Steps(dve, own)

            def tt(out, a, b, op):
                mine.do(dve.tensor_tensor(out, a, b, op))

            dve.wait_ge(ld_c, 96)
            dve.wait_ge(sc_ready, 1)
            tt(bi[:], sc[:], bias[:].unsqueeze(1).to_broadcast([P, NTT, NE]), ALU.add)
            b8 = bi[:].rearrange("p t (g n) -> p (t g) n", g=NG)
            def f4(x, a, b):
                return x[:].rearrange("p t g n -> p (t g) n")[:, :, a:b]
            tt(f4(u1, 0, 4), b8[:, :, 0:4], b8[:, :, 4:8], ALU.max)
            tt(f4(u2, 0, 4), b8[:, :, 0:4], b8[:, :, 4:8], ALU.min)
            for m in (2, 1):
                tt(f4(v1, 0, m), f4(u1, 0, m), f4(u1, m, 2 * m), ALU.max)
                tt(f4(v2, 0, m), f4(u1, 0, m), f4(u1, m, 2 * m), ALU.min)
                tt(f4(v3, 0, m), f4(u2, 0, m), f4(u2, m, 2 * m), ALU.max)
                tt(f4(u2, 0, m), f4(v2, 0, m), f4(v3, 0, m), ALU.max)
                mine.do(dve.tensor_copy(f4(u1, 0, m), f4(v1, 0, m)))
            tt(gs[:].rearrange("p t g -> p (t g)").unsqueeze(2), f4(u1, 0, 1), f4(u2, 0, 1), ALU.add)
            full = [P, NTT, NG, NG]
            other, self_ = gs[:].unsqueeze(2).to_broadcast(full), gs[:].unsqueeze(3).to_broadcast(full)
            tt(cmp[:], other, self_, ALU.is_equal)
            tt(cmp[:], cmp[:], lower[:].unsqueeze(1).to_broadcast(full), ALU.mult)
            tt(cmp2, other, self_, ALU.is_gt)
            tt(cmp[:], cmp[:], cmp2, ALU.add)
            mine.do(dve.tensor_reduce(gm[:], cmp[:], AX, ALU.add))
            mine.do(dve.tensor_scalar(gm[:], gm[:], float(TOPG), None, ALU.is_lt))
            g64 = gm[:].rearrange("p t g -> p (t g)").unsqueeze(2).to_broadcast([P, NTT * NG, 8])
            flat = lambda x: x[:].rearrange("p t (g n) -> p (t g) n", g=NG)
            tt(flat(sel), flat(bi), g64, ALU.mult)
            mine.do(dve.tensor_scalar(gs[:], gm[:], -1.0, BIG, ALU.add, ALU.mult))
            tt(flat(sel), flat(sel), gs[:].rearrange("p t g -> p (t g)").unsqueeze(2).to_broadcast([P, NTT * NG, 8]), ALU.add)
            for i in range(NTT):
                mine.mark(dve.max(top[:, i], sel[:, i]))
            mine.settle()
            for i in range(NTT):
                mine.mark(dve.match_replace(key[:, i], top[:, i], sel[:, i], -3e38))
            mine.settle()
            dve.tensor_scalar(mask[:], key[:], -3e38, None, ALU.is_equal).then_inc(mask_ready, 1)
            dve.wait_ge(mask_ready, 1)
            tt(gate[:], sc[:], mask[:], ALU.mult)
            mine.do(dve.tensor_reduce(tot[:], gate[:], AX, ALU.add))
            mine.do(dve.reciprocal(tot[:], tot[:]))
            mine.do(dve.tensor_scalar(tot[:], tot[:], ROUTED_SCALE, None, ALU.mult))
            tt(gate[:], gate[:], tot[:].unsqueeze(2).to_broadcast([P, NTT, NE]), ALU.mult)
            dve.wait_ge(rank_ready, 1)
            mine.do(dve.tensor_copy(ci[:], k.ps[:, 7, 0:NE]))
            mine.do(dve.tensor_scalar(ci[:], ci[:], P - 1, None, ALU.add))
            mine.do(dve.tensor_scalar(ci[:], ci[:], 7, None, ALU.arith_shift_right))
            mine.do(dve.tensor_copy(nb[:], ci[:]))
            mine.do(dve.tensor_tensor_scan(end[:], k.ones[:, 0:NE], nb[:], 0.0, ALU.mult, ALU.add))
            tt(nb[:], end[:], nb[:], ALU.subtract)
            mine.do(dve.tensor_scalar(k.nr[:], end[0:1, NE - 1:NE], 1.0, None, ALU.add))
            mine.do(dve.tensor_scalar(k.nr[:], k.nr[:], 1, None, ALU.arith_shift_right))
            mine.do(dve.tensor_scalar(k.nr[:], k.nr[:], -(NE // 2), None, ALU.add))
            mine.do(dve.tensor_copy(ri[:], k.ps[:, 6, :]))
            mine.do(dve.tensor_scalar(qi[:], ri[:], 7, None, ALU.arith_shift_right))
            mine.do(dve.tensor_scalar(ri[:], ri[:], P - 1, None, ALU.bitwise_and))
            fl = lambda x: x[:].rearrange("p t e -> p (t e)")
            mine.do(dve.tensor_copy(fl(key), ri[:]))
            mine.do(dve.tensor_copy(fl(sel), qi[:]))
            mine.do(dve.scalar_tensor_tensor(fl(key), fl(key), float(NBLK), fl(sel), ALU.mult, ALU.add))
            tt(key[:], key[:], nb[:].unsqueeze(1).to_broadcast([P, NTT, NE]), ALU.add)
            tt(key[:], key[:], mask[:], ALU.mult)
            tt(key[:], key[:], mask[:], ALU.add)
            mine.do(dve.tensor_scalar(key[:], key[:], -1.0, None, ALU.add))
            for i in range(NTT):
                mine.mark(dve.max(slotv[:, i], key[:, i]))
            mine.settle()
            dve.tensor_copy(k.slot[:], slotv[:]).then_inc(slots_ready, 1)
            for i in range(NTT):
                tt(pick[:], key[:, i:i + 1, :].to_broadcast([P, 8, NE]), slotv[:, i].unsqueeze(2).to_broadcast([P, 8, NE]), ALU.is_equal)
                tt(pick[:], pick[:], gate[:, i:i + 1, :].to_broadcast([P, 8, NE]), ALU.mult)
                mine.do(dve.tensor_reduce(k.gates[:, i], pick[:], AX, ALU.add))
            mine.do(dve.tensor_scalar(end[:], end[:], pidx[:, 0:1], None, ALU.is_le))
            mine.do(dve.tensor_reduce(ebf[:], end[:], AX, ALU.add))
            mine.do(dve.tensor_scalar(ebf[:], ebf[:], float(NE - 1), None, ALU.min))
            dve.tensor_copy(ebi[:], ebf[:]).then_inc(eb_ready, 1)
            for f in range(2):
                dve.wait_ge(sg_ready, 2 * f + 2)
                tt(aT[:, f], aT[:, f], sg, ALU.mult)
                dve.wait_ge(u_ready, f + 1)
                dve.tensor_tensor(aT[:, f], aT[:, f], banks(k, 4), ALU.mult).then_inc(act_ready, 1)

        @block.tensor
        def _(pe):
            pe.wait_ge(ld_c, 96)
            for i in range(NTT):
                for t in range(KT):
                    mm = pe.matmul(k.ps[:, 0, i * NE:(i + 1) * NE], k.hT2[:, t, i * P:(i + 1) * P], wr[:, t, :],
                                   start=(t == 0), stop=(t == KT - 1))
            mm.then_inc(lg_ready, 1)
            for i in range(NTT):
                if i >= 2:
                    pe.wait_ge(h_taken, i - 1)
                for t in range(KT):
                    tr = pe.transpose(k.ps[:, 2 + 2 * (i % 2) + t // 4, (t % 4) * P:(t % 4 + 1) * P],
                                      k.hT2[:, t, i * P:(i + 1) * P], k.eye[:])
                tr.then_inc(h_ready, 1)
            pe.wait_ge(mask_ready, 1)
            for i in range(NTT):
                for m in range(i):
                    pe.matmul(k.ps[:, 6, i * NE:(i + 1) * NE], k.ones[:], mask[:, m], start=(m == 0), stop=False)
                pe.matmul(k.ps[:, 6, i * NE:(i + 1) * NE], causal[:], mask[:, i], start=(i == 0), stop=True)
            for i in range(NTT):
                mm = pe.matmul(k.ps[:, 7, 0:NE], k.ones[:], mask[:, i], start=(i == 0), stop=(i == NTT - 1))
            mm.then_inc(rank_ready, 1)
            pe.wait_ge(h_taken, NTT)
            pe.wait_ge(ld_s, 16)
            for f in range(2):
                if f:
                    pe.wait_ge(act_ready, f)
                for m in range(2):
                    for half in range(2):
                        for t in range(KT):
                            mm = pe.matmul(k.ps[:, 2 + 2 * m + half, :], wgu[:, m, f, t, :],
                                           k.hT2[:, t, half * HALF:(half + 1) * HALF], start=(t == 0), stop=(t == KT - 1))
                    mm.then_inc((g_ready, u_ready)[m], 1)
            pe.wait_ge(act_ready, 2)
            pe.wait_ge(ld_d, 16)
            for i in range(NTT):
                if i >= 2:
                    pe.wait_ge(d_taken, i - 1)
                for half in range(2):
                    for f in range(2):
                        mm = pe.matmul(k.ps[:, 2 + 2 * (i % 2) + half, :], aT[:, f, i * P:(i + 1) * P],
                                       wd[:, f, half * HALF:(half + 1) * HALF], start=(f == 0), stop=(f == 1))
                mm.then_inc(d_ready, 1)


def experts(k):
    nc, I = k.nc, k.I
    with Stage(k, "exp") as s:
        gu, wd = s.sb("gu", [P, 2, KT, 2 * DE]), s.sb("wd", [P, 2, 2, D])
        x, y = k.hT2[:, 0:2], k.hT2[:, 4:6]
        xT = k.hT2[:, 2:4].rearrange("p u (t n) -> p u t n", t=KT)
        idx = s.sb("idx", [P, 2], I32)
        sg, a = s.sb("sg", [P, 2, DE]), s.sb("a", [P, 2, DE])
        aT = s.sb("aT", [P, 2, P])
        ld_gu, ld_wd, ld_x, st_y = ([s.sem(f"{n}{b}") for b in range(2)] for n in ("ld_gu", "ld_wd", "ld_x", "st_y"))
        names = ("idx_ready xtr_ready xt_act xt_dve gu_ready sg_ready sgg_ready act_ready atr_ready at_taken down_ready y_act y_dve")
        (idx_ready, xtr_ready, xt_act, xt_dve, gu_ready, sg_ready, sgg_ready, act_ready, atr_ready, at_taken, down_ready,
         y_act, y_dve) = (s.sem(n) for n in names.split())
        block = s.block()
        yrow = k.scratch["yrow"].rearrange("(p b) n -> p b n", p=P)
        hrow = k.scratch["hrow"]

        @block.sync
        def _(sp):
            for i, last in used_rounds(sp, k):
                for u in range(2):
                    b = i * 2 + u
                    e = sp.value_load(k.eb[0:1, b:b + 1] if isinstance(b, int) else k.eb[0:1, bass.ds(b, 1)],
                                      min_val=0, max_val=NE - 1)
                    wait(sp, gu_ready, b - 1)
                    sp.dma_start(gu[:, u], I["w_gu"][e]).then_inc(ld_gu[u], 16)
                    wait(sp, down_ready, b - 1)
                    sp.dma_start(wd[:, u], I["w_down"][e]).then_inc(ld_wd[u], 16)

        @block.gpsimd
        def _(pool):
            copied, following = pool.alloc_register("copied"), pool.alloc_register("following")
            pool.reg_mov(following, 1)
            for i, last in used_rounds(pool, k):
                for u in range(2):
                    b = i * 2 + u
                    wait(pool, ld_x[u], i * 16, 16)
                    wait(pool, xtr_ready, b - 1)
                    pool.tensor_copy(idx[:, u:u + 1], k.idx[:, bass.ds(b, 1)]).then_inc(idx_ready, 1)
                    pool.reg_mov(copied, following)
                    pool.wait_ge(idx_ready, copied)
                    pool.reg_add(following, copied, 1)
                    pool.indirect_dma_start(x[:, u, :], None, hrow, bass.IndirectOffsetOnAxis(ap=idx[:, u:u + 1], axis=0))\
                        .then_inc(ld_x[u], 16)
            pool.reg_sub(copied, following, 1)
            pool.wait_ge(idx_ready, copied)
            for u in range(2):
                wait(pool, st_y[u], i * 16 + 16, 16)

        def turned(eng, b, u, half, put, signal):
            wait(eng, xtr_ready, b + 1)
            wait(eng, gu_ready, b - 1)
            put(xT[:, u, 4 * half:4 * half + 4, :].rearrange("p t n -> p (t n)"), k.ps[:, half, :]).then_inc(signal, 1)

        def outputs(eng, i, b, u, half, put, signal):
            wait(eng, down_ready, b + 1)
            wait(eng, st_y[u], i * 16, 16)
            put(y[:, u, half * HALF:(half + 1) * HALF], k.ps[:, 4 + half, :]).then_inc(signal, 1)

        @block.scalar
        def _(act):
            def put(o, i):
                return act.activation(o, i, ACT.Copy)

            def turn_a(b):
                wait(act, atr_ready, b + 1)
                wait(act, down_ready, b)
                put(aT[:].rearrange("p f n -> p (f n)"), k.ps[:, 3, 0:DE]).then_inc(at_taken, 1)

            def store(i, b, u):
                outputs(act, i, b, u, 0, put, y_act)
                wait(act, y_act, b + 1)
                wait(act, y_dve, b + 1)
                act.dma_start(yrow[:, bass.ds(b, 1), :], y[:, u:u + 1, :]).then_inc(st_y[u], 16)

            turned(act, 0, 0, 0, put, xt_act)
            for i, last in used_rounds(act, k):
                for u in range(2):
                    b = i * 2 + u
                    if not (isinstance(b, int) and b == 0):
                        turn_a(b - 1)
                    wait(act, gu_ready, b + 1)
                    wait(act, act_ready, b - 1)
                    act.activation(sg[:, u], k.ps[:, 2 if u == 0 else 6, 0:DE], ACT.Sigmoid).then_inc(sg_ready, 1)
                    if not (last and u):
                        turned(act, b + 1, 1 - u, 0, put, xt_act)
                    if not (isinstance(b, int) and b == 0):
                        store(i if u else i - 1, b - 1, 1 - u)
            turn_a(b)
            store(i, b, 1)

        @block.vector
        def _(dve):
            def put(o, i):
                return dve.tensor_copy(o, i)

            turned(dve, 0, 0, 1, put, xt_dve)
            for i, last in used_rounds(dve, k):
                for u in range(2):
                    b = i * 2 + u
                    g = k.ps[:, 2 if u == 0 else 6, :]
                    wait(dve, sg_ready, b + 1)
                    dve.tensor_tensor(sg[:, u], sg[:, u], g[:, 0:DE], ALU.mult).then_inc(sgg_ready, 1)
                    wait(dve, sgg_ready, b + 1)
                    wait(dve, atr_ready, b - 1)
                    dve.tensor_tensor(a[:, u], sg[:, u], g[:, DE:2 * DE], ALU.mult).then_inc(act_ready, 1)
                    if not (last and u):
                        turned(dve, b + 1, 1 - u, 1, put, xt_dve)
                    if not (isinstance(b, int) and b == 0):
                        outputs(dve, i if u else i - 1, b - 1, 1 - u, 1, put, y_dve)
            outputs(dve, i, b, 1, 1, put, y_dve)

        @block.tensor
        def _(pe):
            def turn_x(i, b, u):
                wait(pe, ld_x[u], i * 16 + 16, 16)
                wait(pe, xt_act, b)
                wait(pe, xt_dve, b)
                for t in range(KT):
                    tr = pe.transpose(k.ps[:, t // 4, (t % 4) * P:(t % 4 + 1) * P], x[:, u, t * P:(t + 1) * P], k.eye[:])
                tr.then_inc(xtr_ready, 1)

            def turn_a(b, u):
                wait(pe, act_ready, b + 1)
                wait(pe, at_taken, b)
                for f in range(2):
                    tr = pe.transpose(k.ps[:, 3, f * P:(f + 1) * P], a[:, u, f * P:(f + 1) * P], k.eye[:])
                tr.then_inc(atr_ready, 1)

            def down(i, b, u):
                wait(pe, at_taken, b + 1)
                wait(pe, ld_wd[u], i * 16 + 16, 16)
                wait(pe, y_act, b)
                wait(pe, y_dve, b)
                for half in range(2):
                    for f in range(2):
                        mm = pe.matmul(k.ps[:, 4 + half, :], aT[:, f, :], wd[:, u, f, half * HALF:(half + 1) * HALF],
                                       start=(f == 0), stop=(f == 1))
                mm.then_inc(down_ready, 1)

            turn_x(0, 0, 0)
            for i, last in used_rounds(pe, k):
                for u in range(2):
                    b = i * 2 + u
                    first = isinstance(b, int) and b == 0
                    if not first:
                        turn_a(b - 1, 1 - u)
                    wait(pe, xt_act, b + 1)
                    wait(pe, xt_dve, b + 1)
                    wait(pe, ld_gu[u], i * 16 + 16, 16)
                    wait(pe, act_ready, b - 1)
                    for t in range(KT):
                        mm = pe.matmul(k.ps[:, 2 if u == 0 else 6, :], xT[:, u, t, :], gu[:, u, t, :],
                                       start=(t == 0), stop=(t == KT - 1))
                    mm.then_inc(gu_ready, 1)
                    if not (last and u):
                        turn_x(i + 1 if u else i, b + 1, 1 - u)
                    if not first:
                        down(i if u else i - 1, b - 1, 1 - u)
            turn_a(b, 1)
            down(i, b, 1)


def combine(k):
    nc, I = k.nc, k.I
    acc = k.mix
    NBUF = 6
    with Stage(k, "comb") as s:
        y = s.sb("y", [P, NBUF, D])
        fg, rstd = s.sb("fg", [P, KT]), s.sb("rstd", [P, T])
        ld_y = [s.sem(f"ld_y{b}") for b in range(NBUF)]
        names = "ld_g summed turned x_ready sq_ready ss_ready own_a rstd_ready o_ready st_o"
        (ld_g, summed, turned, x_ready, sq_ready, ss_ready, own_a, rstd_ready, o_ready, st_o) = (s.sem(n) for n in names.split())
        block = s.block()

        @block.sync
        def _(sp):
            sp.dma_start(fg[:], I["final_g"]).then_inc(ld_g, 16)
            for j in range(KT):
                sp.wait_ge(o_ready, j + 1)
                sp.dma_start(k.out[j], k.hT2[:, j]).then_inc(st_o, 16)
            sp.wait_ge(st_o, 16 * KT)

        @block.gpsimd
        def _(pool):
            for i in range(NTT):
                for j in range(TOPK):
                    n = i * TOPK + j
                    if n >= NBUF:
                        pool.wait_ge(summed, n - NBUF + 1)
                    pool.indirect_dma_start(y[:, n % NBUF, :], None, k.scratch["yrow"],
                                            bass.IndirectOffsetOnAxis(ap=k.slot[:, i, j:j + 1], axis=0)).then_inc(ld_y[n % NBUF], 16)

        @block.vector
        def _(dve):
            def to_residual(i):
                dve.wait_ge(turned, i + 1)
                for t in range(KT):
                    ins = dve.scalar_tensor_tensor(k.xT[:, t, i * P:(i + 1) * P], k.ps[:, 2 * (i % 2) + t // 4, (t % 4) * P:(t % 4 + 1) * P],
                                                   k.cond[:, C2 + 5 * KT + t, 1:2], k.xT[:, t, i * P:(i + 1) * P], ALU.mult, ALU.add)
                ins.then_inc(x_ready, 1)

            for i in range(NTT):
                for j in range(TOPK):
                    n = i * TOPK + j
                    dve.wait_ge(ld_y[n % NBUF], 16 * (n // NBUF + 1))
                    if j:
                        dve.wait_ge(summed, n)
                    dve.scalar_tensor_tensor(acc[:, i], y[:, n % NBUF, :], k.gates[:, i, j:j + 1], acc[:, i],
                                             ALU.mult, ALU.add).then_inc(summed, 1)
                if i:
                    to_residual(i - 1)
            to_residual(NTT - 1)
            dve.wait_ge(ld_g, 16)
            dve.wait_ge(rstd_ready, 1)
            dve.wait_ge(x_ready, NTT)
            for j in range(KT):
                dve.scalar_tensor_tensor(k.hT2[:, j], k.xT[:, j], fg[:, j:j + 1], rstd[:], ALU.mult, ALU.mult).then_inc(o_ready, 1)

        @block.tensor
        def _(pe):
            for i in range(NTT):
                pe.wait_ge(summed, (i + 1) * TOPK)
                if i >= 2:
                    pe.wait_ge(x_ready, i - 1)
                for t in range(KT):
                    tr = pe.transpose(k.ps[:, 2 * (i % 2) + t // 4, (t % 4) * P:(t % 4 + 1) * P], acc[:, i, t * P:(t + 1) * P], k.eye[:])
                tr.then_inc(turned, 1)
            for j in range(KT):
                pe.wait_ge(sq_ready, j + 1)
                for half in range(2):
                    mm = pe.matmul(k.ps[:, 4 + half, :], k.ones[:], k.hT2[:, j, half * HALF:(half + 1) * HALF],
                                   start=(j == 0), stop=(j == KT - 1))
            mm.then_inc(ss_ready, 1)

        @block.scalar
        def _(act):
            act.wait_ge(x_ready, NTT)
            for j in range(KT):
                act.activation(k.hT2[:, j], k.xT[:, j], ACT.Square).then_inc(sq_ready, 1)
            act.wait_ge(ss_ready, 1)
            act.activation(rstd[:], banks(k, 4), ACT.Ln, scale=1.0 / D, bias=EPS).then_inc(own_a, 1)
            act.wait_ge(own_a, 1)
            act.activation(rstd[:], rstd[:], ACT.Exp, scale=-0.5).then_inc(rstd_ready, 1)


def program(nc, I, out):
    with ExitStack() as ctx:
        scratch = {
            "proj": nc.dram_tensor("proj", (NSCAN, P, T), F32).ap(),
            "vfirst": nc.dram_tensor("vfirst", (PAIRS, P, T), F32).ap(),
            "rowtok": nc.dram_tensor("rowtok", (NBLK * P, 1), I32).ap(),
            "ebd": nc.dram_tensor("ebd", (NBLK, 1), I32).ap(),
            "hrow": nc.dram_tensor("hrow", (T, D), F32).ap(),
            "yrow": nc.dram_tensor("yrow", (NBLK * P, D), F32).ap(),
        }
        k = Kernel(nc, I, out, ctx, scratch)
        modulation(k)
        for l in range(L):
            projection(k, l)
            hgrn(k, l)
            rwkv(k, l)
            merge(k, l)
        k.second_block()
        with Stage(k, "ctx") as s:
            ctxT, hcT = s.sb("ctxT", [P, KT, CTX]), s.sb("hcT", [P, KT, CTX])
            ld = s.sem("ld")
            with nc.Block() as block:
                @block.sync
                def _(sp):
                    sp.dma_start(ctxT[:], I["ctxT"]).then_inc(ld, 16)
                    sp.wait_ge(ld, 16)
            rms_modulated(k, "norm1", [(k.xT, k.hT2, T, 0, C2, 1), (ctxT, hcT, CTX, 0, C2, 2)])
            attention(k, hcT)
        pooling(k)
        project_out(k)
        rms_modulated(k, "norm2", [(k.xT, k.hT2, T, 1, C2 + 3 * KT, 1)])
        route(k)
        experts(k)
        combine(k)


def slabs(w):
    kk, n = w.shape
    return np.ascontiguousarray(w.reshape(kk // 128, 128, n // 128, 128).transpose(2, 1, 0, 3))
def cols(v):
    return np.ascontiguousarray(np.swapaxes(v.reshape(v.shape[:-1] + (-1, 128)), -1, -2))
def lay(i):
    o = {}
    o["xT"] = np.ascontiguousarray(i["x"][0].T).reshape(8, 128, 1024)
    o["c3"] = np.ascontiguousarray(np.stack([cols(i["c"][0]), cols(i["c_2"][0]), cols(i["c_ctx_2"])], -1))
    o["w_ada"] = np.concatenate([slabs(i["w_ada"][0]), slabs(i["w_ada"][1]), slabs(i["w_ada_2"][0])]).reshape(24, 4, 128, 8, 128).transpose(0,2,1,3,4).copy()
    o["b_ada"] = np.concatenate([cols(i["b_ada"][0]), cols(i["b_ada"][1]), cols(i["b_ada_2"][0])], -1)
    o["w_in"] = np.stack([slabs(w) for w in i["w_in"]])
    o["v_down"] = np.ascontiguousarray(i["rw_v_down"][0].reshape(8, 128, 32).transpose(1, 0, 2))
    return o
def lay2(i, o):
    b = cols(i["hg_lower_bounds"])
    g = cols(i["hg_norm_g"])
    o["hg_par"] = np.ascontiguousarray(np.stack([np.stack([b[0], b[1], g[l]], -1) for l in range(2)]))
    s, t = np.meshgrid(np.arange(128), np.arange(128), indexing="ij")
    ms = [((s // (2*m) == t // (2*m)) & ((s // m) % 2 == 0) & ((t // m) % 2 == 1)) for m in (64,32,16,8,4,2,1)] + [s == t]
    o["level_masks"] = np.ascontiguousarray(np.stack(ms, 1).astype(np.int32))
    return o
def lay3(i, o):
    L = 2
    mu = i["rw_mu"]
    W = 512
    z = np.zeros((W,), np.float32)
    par = []
    for l in range(L):
        c = [mu[l, n * W:(n + 1) * W] for n in range(4)] + [i["rw_w0"][l], i["rw_a0"][l], i["rw_k_k"][l], i["rw_k_a"][l],
             i["rw_r_k"][l].reshape(-1), i["rw_gn_g"][l], i["rw_gn_b"][l], i["rw_v0"][l - 1] if l else z,
             np.tile(mu[l, 4 * W:], 4)]
        par.append(np.stack([cols(v) for v in c], -1))
    o["rw_par"] = np.ascontiguousarray(np.stack(par))
    o["rw_lora"] = np.stack([slabs(np.concatenate([i["rw_w_up"][l], i["rw_a_up"][l]]))[:, :, 0] for l in range(L)])
    o["v_up"] = np.ascontiguousarray(i["rw_v_up"][0].reshape(32, 4, 128).transpose(1, 0, 2))
    s, t = np.meshgrid(np.arange(128), np.arange(128), indexing="ij")
    o["causal_masks"] = np.stack([s < t, s <= t], 1).astype(np.float32)
    pm = [((s // (2*m) == t // (2*m)) & ((s // m) % 2 == 0) & ((t // m) % 2 == 1)) for m in (1,2,4,8,16,32,64)]
    o["pair_masks"] = np.stack(pm, 1).astype(np.float32)
    o["pair_mask_t"] = np.ascontiguousarray(pm[0].T.astype(np.float32))
    return o
def lay4(i, o):
    o["w_branch_hg"] = np.stack([slabs(w) for w in i["w_branch_hg"]])
    o["w_branch_rw"] = np.stack([slabs(w) for w in i["w_branch_rw"]])
    o["w_out"] = np.stack([slabs(w) for w in i["w_out"]])
    o["ln_par"] = np.ascontiguousarray(np.stack([cols(i["ln_g"]), cols(i["ln_b"])], 2))
    return o
def lay5(i, o):
    perm = np.concatenate([np.r_[j*64:(j+1)*64, (4+j)*64:(5+j)*64] for j in range(4)])
    w = i["w_in_2"][0]
    cp = np.concatenate([perm, np.arange(512, 1280)])
    o["w_in2"] = slabs(w[:, cp])
    rp = np.concatenate([perm, np.arange(512, 1024)])
    o["w_out2"] = slabs(i["w_out_2"][0][rp])
    o["ctxT"] = np.ascontiguousarray(i["ctx_2"][0].T.reshape(8, 128, 256).transpose(1, 0, 2))
    o["norm_g"] = np.ascontiguousarray(np.stack([cols(i["norm1_g_2"][0]), cols(i["norm2_g_2"][0])], 1))
    p = np.arange(128) % 64
    fr = (np.float32(10000.0) ** (-np.arange(16, dtype=np.float32) / np.float32(16)))
    t = np.arange(1024)
    pos = np.where((p < 32)[:, None], (t // 64)[None], (t % 64)[None]).astype(np.float32)
    ang = pos * fr[p % 16][:, None]
    o["cos"], o["sin"] = np.cos(ang), np.sin(ang)
    rot = np.zeros((128, 128), np.float32)
    for m in range(128):
        if m % 32 < 16: rot[m + 16, m] = -1
        else: rot[m - 16, m] = 1
    o["rot"] = rot
    a, b = np.meshgrid(np.arange(128), np.arange(384), indexing="ij")
    o["band"] = np.where(np.abs(a + 128 - b) <= 128, 0, -1e30).astype(np.float32)
    sk = i["attn_sink_2"][0]
    o["sink"] = np.ascontiguousarray(np.tile(np.stack([sk[0:4], sk[4:8]], 1)[None], (128, 1, 1)))
    o["pool_w"] = np.ascontiguousarray(i["pool_w_2"][0].transpose(1, 0, 2))
    inv = np.zeros((4, 1024), np.float32)
    for g, w_ in enumerate((2, 4, 8, 16)):
        lo = np.clip(t - w_ // 2, 0, 1024); hi = np.clip(t - w_ // 2 + w_, 0, 1024)
        inv[g] = 1 / (hi - lo).astype(np.float32)
    o["pool_inv"] = np.ascontiguousarray(np.tile(inv[None], (128, 1, 1)))
    o["pool_scale"] = cols(i["pool_scale_2"][0])
    return o
def lay6(i, o):
    o["w_router"] = np.ascontiguousarray(i["w_router_2"][0].reshape(8, 128, 64).transpose(1, 0, 2))
    o["router_bias"] = np.ascontiguousarray(np.tile(i["router_bias_2"][0][None], (128, 1)))
    a, b = np.meshgrid(np.arange(8), np.arange(8), indexing="ij")
    o["lower_groups"] = np.ascontiguousarray(np.tile((b < a).astype(np.float32)[None], (128, 1, 1)))
    s, t = np.meshgrid(np.arange(128), np.arange(128), indexing="ij")
    o["causal"] = (s < t).astype(np.float32)
    o["pidx"] = np.arange(128, dtype=np.float32)[:, None].copy()
    o["tokid"] = np.ascontiguousarray((np.arange(128)[:, None] + 128 * np.arange(8)[None]).astype(np.int32))
    o["ws_gu"] = np.ascontiguousarray(np.stack([slabs(i["ws_gate_2"][0]), slabs(i["ws_up_2"][0])]).transpose(2, 0, 1, 3, 4))
    o["ws_down"] = np.ascontiguousarray(i["ws_down_2"][0].reshape(2, 128, 1024).transpose(1, 0, 2))
    g, u = i["w_gate_2"][0], i["w_up_2"][0]
    o["w_gu"] = np.ascontiguousarray(np.concatenate([g, u], -1).reshape(64, 8, 128, 512).transpose(0, 2, 1, 3))
    o["w_down"] = np.ascontiguousarray(i["w_down_2"][0].reshape(64, 2, 128, 1024).transpose(0, 2, 1, 3))
    o["final_g"] = cols(i["final_g_2"])
    return o


def kernel(**inputs):
    import concourse.bacc as bacc
    from concourse.bass_utils import run_bass_kernel_spmd

    i = {n: np.asarray(a) for n, a in inputs.items()}
    o = lay(i)
    for part in (lay2, lay3, lay4, lay5, lay6):
        part(i, o)
    nc = bacc.Bacc("TRN2", target_bir_lowering=False, num_devices=1)
    arrays, aps = {}, {}
    for name, a in o.items():
        arrays[f"in_{name}_dram"] = a = np.ascontiguousarray(a)
        aps[name] = nc.dram_tensor(f"in_{name}_dram", a.shape, mybir.dt.from_np(a.dtype), kind="ExternalInput").ap()
    out = nc.dram_tensor("out_0_dram", (KT, P, T), F32, kind="ExternalOutput").ap()
    program(nc, aps, out)
    r = run_bass_kernel_spmd(nc, [arrays], core_ids=[0])
    return np.ascontiguousarray(r.results[0]["out_0_dram"].reshape(D, T).T)[None]
```

```python
from contextlib import ExitStack

import numpy as np

import concourse.bass as bass
from concourse import mybir

F32 = mybir.dt.float32
F32R = mybir.dt.float32r
I32 = mybir.dt.int32
ALU = mybir.AluOpType
ACT = mybir.ActivationFunctionType
AX = mybir.AxisListType.X

P = 128
T = 1024
HALF = 512
D = 1024
KT = D // P
CH = 128
NC = T // CH
L = 2
HG = 4
PAIRS = 4
CQ, CF, CI, CZ, CR, CK, CV, CY, CLOW, CG1, CG2 = 0, 4, 8, 12, 16, 20, 24, 28, 32, 33, 41
NSCAN = 33
NIN = 49
NADA1, NADA2 = 24, 48
LN_EPS, RMS_EPS, GN_EPS, L2_EPS, LB_FLOOR, EPS = 1e-5, 1e-6, 64e-5, 1e-12, 1e-30, 1e-6
ALPHA = (2 * L) ** 0.25
E_HALF = 0.6065306597126334
LN2 = 0.6931471805599453
NE_BLOCKS, SLOT_BLOCKS = 64, 128
LEVELS = [64, 32, 16, 8, 4, 2, 1]


def wait(eng, sem, value, unit=1):
    if isinstance(value, int):
        if value > 0:
            eng.wait_ge(sem, value)
        return
    value = eng.snap(value)
    if unit:
        eng.wait_ge(sem, unit)
    eng.wait_ge(sem, value)


def rounds(eng, n):
    yield 0
    if n > 1:
        with eng.Fori(1, n) as i:
            yield i


def ends(eng, n):
    yield 0
    with eng.Fori(1, n - 1) as i:
        yield i
    yield n - 1


class Steps:

    def __init__(self, eng, sem):
        self.eng, self.sem, self.base, self.n = eng, sem, 0, 0

    def loop(self, base):
        self.base, self.n = base, 0

    def mark(self, ins):
        ins.then_inc(self.sem, 1)
        self.n += 1
        return ins

    def settle(self):
        wait(self.eng, self.sem, self.base + self.n)

    def do(self, ins):
        self.mark(ins)
        self.settle()


class Kernel:

    def __init__(self, nc, I, out, ctx, scratch):
        self.nc, self.I, self.out, self.ctx = nc, I, out, ctx
        self.scratch = scratch

        def keep(name, shape, dt=F32):
            return ctx.enter_context(nc.sbuf_tensor("keep_" + name, shape, dt))

        self.xT = keep("xT", [P, KT, T])
        self.cond = keep("cond", [P, 2 * NADA1 + NADA2, 3])
        self.silu = keep("silu", [P, KT, 3])
        self.bias = keep("bias", [P, 2 * NADA1 + NADA2])
        self.ones = keep("ones", [P, P])
        self.eye = keep("eye", [P, P])
        self.mix = keep("mix", [P, KT, T])
        self.yhg = self.mix[:, 0:HG, :]
        self.yrw = self.mix[:, HG:KT, :]
        self.vd = keep("vd", [32, T])
        self.ps = ctx.enter_context(nc.psum_tensor("ps", [P, 8, HALF], F32))
        self.keep = keep

    def second_block(self):
        self.hT2 = self.keep("hT2", [P, KT, T])
        self.idx = self.keep("idx", [P, P], I32)
        self.eb = self.keep("eb", [1, P], I32)
        self.nr = self.keep("nr", [1, 1], I32)
        self.slot = self.keep("slot", [P, KT, KT], I32)
        self.gates = self.keep("gates", [P, KT, KT])


class Stage:

    def __init__(self, k, name):
        self.k, self.name, self.ctx, self.sems = k, name, ExitStack(), []

    def __enter__(self):
        self.ctx.__enter__()
        return self

    def __exit__(self, *a):
        self.ctx.__exit__(*a)
        self.k.nc.clear_and_free_semaphores(self.sems)
        self.k.nc.all_engine_barrier()

    def sb(self, name, shape, dt=F32):
        return self.ctx.enter_context(self.k.nc.sbuf_tensor(f"s_{self.name}_{name}", shape, dt))

    def sem(self, name):
        self.sems.append(self.k.nc.alloc_semaphore(f"{self.name}_{name}"))
        return self.sems[-1]

    def block(self):
        return self.ctx.enter_context(self.k.nc.Block())


def modulation(k):
    nc, I = k.nc, k.I
    GRP = 4
    NG = NADA1 // GRP
    with Stage(k, "ada") as s:
        w = s.sb("w", [P, 2, GRP, KT, P])
        c3, e3 = s.sb("c3", [P, KT, 3]), k.silu
        row = s.sb("row", [3, 2, GRP * P])
        ld_w, ld_c = [s.sem("ld_w0"), s.sem("ld_w1")], s.sem("ld_c")
        sig_ready, silu_ready = s.sem("sig_ready"), s.sem("silu_ready")
        tiles_ready, row_ready, turned, tiles_taken, own = (s.sem(n) for n in "tiles_ready row_ready turned tiles_taken own".split())
        cst, eye_clear = s.sem("cst"), s.sem("eye_clear")
        block = s.block()

        def group(g):
            return I["w_ada"][g * GRP:(g + 1) * GRP].rearrange("g p k n -> p g k n")

        @block.sync
        def _(sp):
            sp.dma_start(c3[:], I["c3"]).then_inc(ld_c, 16)
            sp.dma_start(k.bias[:], I["b_ada"]).then_inc(ld_c, 16)
            for g in range(NG):
                if g >= 2:
                    sp.wait_ge(tiles_ready, g - 1)
                sp.dma_start(w[:, g % 2], group(g)).then_inc(ld_w[g % 2], 16)

        @block.gpsimd
        def _(pool):
            pool.memset(k.ones[:], 1.0).then_inc(cst, 1)
            pool.memset(k.eye[:], 0.0).then_inc(eye_clear, 1)
            pool.wait_ge(eye_clear, 1)
            pool.affine_select(out=k.eye[:], in_=k.eye[:], compare_op=ALU.not_equal, fill=1.0, base=0,
                               pattern=[[-1, P]], channel_multiplier=1).then_inc(cst, 1)

        @block.scalar
        def _(act):
            act.wait_ge(ld_c, 32)
            act.activation(e3[:], c3[:], ACT.Sigmoid).then_inc(sig_ready, 1)
            for t in range(KT):
                act.dma_start(k.xT[:, t], I["xT"][t]).then_inc(ld_c, 16)

        @block.vector
        def _(dve):
            dve.wait_ge(sig_ready, 1)
            dve.tensor_tensor(e3[:], e3[:], c3[:], ALU.mult).then_inc(silu_ready, 1)

            def take(g):
                dve.wait_ge(turned, g + 1)
                dve.tensor_copy(k.cond[:, g * GRP:(g + 1) * GRP, :],
                                k.ps[:, 2 + g % 2, 0:3 * GRP].rearrange("p (g v) -> p g v", g=GRP)).then_inc(tiles_taken, 1)

            for g in range(NG):
                if g:
                    take(g - 1)
                dve.wait_ge(tiles_ready, g + 1)
                dve.tensor_copy(row[:, g % 2], k.ps[0:3, g % 2, :]).then_inc(row_ready, 1)
            take(NG - 1)
            dve.wait_ge(tiles_taken, NG)
            dve.wait_ge(ld_c, 32 + 16 * KT)
            dve.tensor_tensor(k.cond[:, 0:NADA1], k.cond[:, 0:NADA1], k.bias[:, 0:NADA1].unsqueeze(2).to_broadcast([P, NADA1, 3]),
                              ALU.add).then_inc(own, 1)

        @block.tensor
        def _(pe):
            pe.wait_ge(silu_ready, 1)

            def turn(g):
                pe.wait_ge(row_ready, g + 1)
                if g >= 2:
                    pe.wait_ge(tiles_taken, g - 1)
                for x in range(GRP):
                    tr = pe.transpose(k.ps[:, 2 + g % 2, 3 * x:3 * x + 3], row[:, g % 2, x * P:(x + 1) * P], k.eye[0:3, 0:3])
                tr.then_inc(turned, 1)

            for g in range(NG):
                pe.wait_ge(ld_w[g % 2], 16 * (g // 2 + 1))
                if g == 0:
                    pe.wait_ge(cst, 2)
                if g >= 2:
                    pe.wait_ge(row_ready, g - 1)
                for t in range(KT):
                    mm = pe.matmul(k.ps[0:3, g % 2, :], e3[:, t, :], w[:, g % 2, :, t, :], start=(t == 0), stop=(t == KT - 1))
                mm.then_inc(tiles_ready, 1)
                if g:
                    turn(g - 1)
            turn(NG - 1)


TERMS = ((0, 0), (0, 1), (1, 0))


def projection(k, l):
    nc, I = k.nc, k.I
    NB = 3
    R1, R2 = 1, 9
    NX = (2 * NADA1 + NADA2 - NADA1) // (NB * (R2 - R1))
    NSTEP = NSCAN + l
    with Stage(k, f"proj{l}") as s:
        hS = s.sb("hS", [P, 2, KT, T], F32R)
        sc1 = s.sb("sc1", [P, KT])
        w = s.sb("w", [P, NB, KT, P])
        wS = s.sb("wS", [P, NB, 2, KT, P], F32R)
        o = s.sb("o", [P, NB, T])
        ld_w = [s.sem(f"ld_w{b}") for b in range(NB)]
        st_o = [s.sem(f"st_o{b}") for b in range(NB)]
        h_ready, hhi_ready, hlo_v, hlo_p = (s.sem(n) for n in ("h_ready", "hhi_ready", "hlo_v", "hlo_p"))
        hi_ready, lo_ready, half_ready = s.sem("hi_ready"), s.sem("lo_ready"), s.sem("half_ready")
        taken_a, taken_v = s.sem("taken_a"), s.sem("taken_v")
        if l:
            vd_taken = s.sem("vd_taken")
        else:
            wa = s.sb("wa", [P, NX, KT, P])
            row = s.sb("row", [3, NX * P])
            ld_a, ada_ready, ada_taken = [s.sem(f"ld_a{x}") for x in range(NX)], s.sem("ada_ready"), s.sem("ada_taken")
            row_ready, turned = s.sem("row_ready"), s.sem("turned")
        block = s.block()

        def steps(eng):
            NR = NSCAN // NB
            parts = [(0, 1, False), (1, 2, True), (2, R2, True), (R2, NR - 1, False), (NR - 1, NR, False)] if not l else \
                [(0, 1, False), (1, NR - 1, False), (NR - 1, NR, False)]
            for a, z, ada in parts:
                if z == a + 1:
                    for b in range(NB):
                        yield a, b, ada
                else:
                    with eng.Fori(a, z) as i:
                        for b in range(NB):
                            yield i, b, ada
            if l:
                yield NSCAN // NB, 0, False

        @block.sync
        def _(sp):
            for i, b, ada in steps(sp):
                n = i * NB + b
                wait(sp, lo_ready, n - NB + 1)
                src = I["v_down"] if isinstance(n, int) and n == NSCAN else I["w_in"][l, n]
                sp.dma_start(w[:, b], src).then_inc(ld_w[b], 16)
                if ada:
                    m = n - R1 * NB
                    wait(sp, ada_ready, m)
                    for x in range(NX):
                        sp.dma_start(wa[:, x], I["w_ada"][m * NX + (NADA1 + x)]).then_inc(ld_a[x], 16)

        @block.gpsimd
        def _(pool):
            for t in range(0, KT, 2):
                pool.wait_ge(hhi_ready, t + 1)
                pool.tensor_tensor(hS[:, 1, t], o[:, t % NB], hS[:, 0, t], ALU.subtract).then_inc(hlo_p, 1)
            for i, b, ada in steps(pool):
                wait(pool, hi_ready, i * NB + (b + 1))
                pool.tensor_tensor(wS[:, b, 1], w[:, b], wS[:, b, 0], ALU.subtract).then_inc(lo_ready, 1)

        @block.vector
        def _(dve):
            c = l * NADA1
            dve.tensor_scalar(sc1[:], k.cond[:, c + KT:c + 2 * KT, 0], 1.0, None, ALU.add).then_inc(h_ready, 1)
            dve.wait_ge(h_ready, 1)

            def low(t):
                dve.wait_ge(hhi_ready, t + 1)
                dve.tensor_tensor(hS[:, 1, t], o[:, t % NB], hS[:, 0, t], ALU.subtract).then_inc(hlo_v, 1)

            for t in range(KT):
                if t >= NB:
                    dve.wait_ge(hlo_v, (t - NB + 1) // 2)
                    dve.wait_ge(hlo_p, (t - NB + 2) // 2)
                dve.tensor_scalar(o[:, t % NB], k.xT[:, t], sc1[:, t:t + 1], k.cond[:, c + t, 0:1],
                                  ALU.mult, ALU.add).then_inc(h_ready, 1)
                if t % 2 == 0 and t:
                    low(t - 1)
            low(KT - 1)
            for i, b, ada in steps(dve):
                n = i * NB + b
                wait(dve, half_ready, n * 2 + 2)
                if isinstance(n, int) and n == NSCAN:
                    dve.tensor_copy(k.vd[:], k.ps[0:32, 6:8, :].rearrange("p a n -> p (a n)")).then_inc(vd_taken, 1)
                    continue
                wait(dve, st_o[b], i * 16, 16)
                dve.tensor_copy(o[:, b, HALF:T], k.ps[:, 2 * b + 1, :]).then_inc(taken_v, 1)
                m = n - R1 * NB
                if ada and not (isinstance(m, int) and m == 0) or isinstance(n, int) and n == R2 * NB and not l:
                    wait(dve, turned, m)
                    dve.tensor_copy(k.cond[:, bass.ds((m - 1) * NX + NADA1, NX), :],
                                    k.ps[:, 7, 0:3 * NX].rearrange("p (g v) -> p g v", g=NX)).then_inc(ada_taken, 1)
                if ada:
                    wait(dve, ada_ready, m + 1)
                    dve.tensor_copy(row[:], k.ps[0:3, 6, 0:NX * P]).then_inc(row_ready, 1)
            if not l:
                dve.wait_ge(ada_taken, NB * (R2 - R1))
                rest = [P, NADA1 + NADA2, 3]
                dve.tensor_tensor(k.cond[:, NADA1:], k.cond[:, NADA1:], k.bias[:, NADA1:].unsqueeze(2).to_broadcast(rest),
                                  ALU.add).then_inc(ada_taken, 1)

        @block.scalar
        def _(act):
            def high(i, b):
                n = i * NB + b
                wait(act, ld_w[b], i * 16 + 16, 16)
                wait(act, half_ready, n * 2 - 2 * NB + 2)
                act.activation(wS[:, b, 0], w[:, b], ACT.Copy).then_inc(hi_ready, 1)

            high(0, 0)
            for t in range(KT):
                act.wait_ge(h_ready, t + 2)
                act.activation(hS[:, 0, t], o[:, t % NB], ACT.Copy).then_inc(hhi_ready, 1)
            high(0, 1)
            for i, b, ada in steps(act):
                n = i * NB + b
                if isinstance(n, int) and n == NSCAN:
                    continue
                if not (isinstance(n, int) and n >= NSTEP - 2):
                    high(i + (b + 2) // NB, (b + 2) % NB)
                wait(act, half_ready, n * 2 + 1)
                wait(act, st_o[b], i * 16, 16)
                act.activation(o[:, b, 0:HALF], k.ps[:, 2 * b, :], ACT.Copy).then_inc(taken_a, 1)
                wait(act, taken_a, n + 1)
                wait(act, taken_v, n + 1)
                act.dma_start(k.scratch["proj"][n], o[:, b, :]).then_inc(st_o[b], 16)
            for b in range(NB):
                act.wait_ge(st_o[b], 16 * (NSCAN // NB))

        @block.tensor
        def _(pe):
            for i, b, ada in steps(pe):
                n = i * NB + b
                last = isinstance(n, int) and n == NSCAN
                wait(pe, hi_ready, n + 1)
                wait(pe, lo_ready, n + 1)
                if not last:
                    wait(pe, taken_a, n - NB + 1)
                    wait(pe, taken_v, n - NB + 1)
                for half in range(2):
                    for t in range(KT):
                        if isinstance(n, int) and n == 0 and half == 0:
                            pe.wait_ge(hhi_ready, t + 1)
                            pe.wait_ge(hlo_v, (t + 1) // 2)
                            pe.wait_ge(hlo_p, t // 2 + 1)
                        for x, y in TERMS:
                            mm = pe.matmul(k.ps[:, 6 + half if last else 2 * b + half, :], wS[:, b, x, t, :],
                                           hS[:, y, t, half * HALF:(half + 1) * HALF],
                                           start=(t == 0 and x + y == 0), stop=(t == KT - 1 and x == 1))
                    mm.then_inc(half_ready, 1)
                m = n - R1 * NB
                if ada and not (isinstance(m, int) and m == 0) or isinstance(n, int) and n == R2 * NB and not l:
                    wait(pe, row_ready, m)
                    wait(pe, ada_taken, m - 1)
                    for x in range(NX):
                        tr = pe.matmul(k.ps[:, 7, 3 * x:3 * x + 3], row[:, x * P:(x + 1) * P], k.eye[0:3, 0:3], start=True, stop=True)
                    tr.then_inc(turned, 1)
                if ada:
                    for x in range(NX):
                        wait(pe, ld_a[x], m * 16 + 16, 16)
                    for t in range(KT):
                        mm = pe.matmul(k.ps[0:3, 6, 0:NX * P], k.silu[:, t, :], wa[:, :, t, :], start=(t == 0), stop=(t == KT - 1))
                    mm.then_inc(ada_ready, 1)


def chunks(ap):
    return ap.rearrange("p (c n) -> p c n", c=NC)


def halves(ap, m, h):
    return ap.rearrange("p (b h m) -> p b h m", h=2, m=m)[:, :, h, :]


def banks(k, a, n=2):
    return k.ps[:, a:a + n, :].rearrange("p a n -> p (a n)")


def hgrn(k, l):
    nc, I = k.nc, k.I
    NL = len(LEVELS) + 1
    with Stage(k, f"hg{l}") as s:
        q, f, iv, z = (s.sb(n, [P, T]) for n in ("q", "f", "iv", "z"))
        par = s.sb("par", [P, HG, 8])
        cur = s.sb("cur", [P, 8])
        tmp = s.sb("tmp", [P, HG, 4])
        t1, t2, b = s.sb("t1", [P, T]), s.sb("t2", [P, T]), s.sb("b", [P, T])
        kk, qh, kh, eb = (s.sb(n, [P, T]) for n in ("kk", "qh", "kh", "eb"))
        dif, ex = s.sb("dif", [P, 2, T]), s.sb("ex", [P, 2, T])
        qt, kt = s.sb("qt", [P, 2, T]), s.sb("kt", [P, 2, T])
        acc, vtok, ktok = s.sb("acc", [P, T]), s.sb("vtok", [P, T]), s.sb("ktok", [P, T])
        S = s.sb("S", [P, NC, P])
        masks = s.sb("masks", [P, NL, P], I32)
        m0 = s.sb("m0", [P, T])
        sc = [banks(k, 0), banks(k, 2)]
        pv, po = banks(k, 4), banks(k, 6)

        ld_par, ld_f, ld_q, ld_i, ld_z = (s.sem("ld_" + n) for n in ("par", "f", "q", "i", "z"))
        small, lb_exp, lb_in, lb_log = (s.sem(n) for n in ("small", "lb_exp", "lb_in", "lb_log"))
        own, own_a, head_done = s.sem("own"), s.sem("own_a"), s.sem("head_done")
        nabs_ready, ln1_ready, dk_ready, ek_ready, nd_ready, ln2_ready = (
            s.sem(n) for n in ("nabs_ready", "ln1_ready", "dk_ready", "ek_ready", "nd_ready", "ln2_ready"))
        b_ready, eb_ready = s.sem("b_ready"), s.sem("eb_ready")
        dif_ready, ex_ready, ops_ready, sc_ready, sc_taken = (
            s.sem(n) for n in ("dif_ready", "ex_ready", "ops_ready", "sc_ready", "sc_taken"))
        tr_ready, tr_taken, kv_ready, S_ready = (
            s.sem(n) for n in ("tr_ready", "tr_taken", "kv_ready", "S_ready"))
        o_ready, sq_ready, ms_ready, rstd_ready, ez_ready = (
            s.sem(n) for n in ("o_ready", "sq_ready", "ms_ready", "rstd_ready", "ez_ready"))
        block = s.block()
        proj = k.scratch["proj"]

        @block.sync
        def _(sp):
            sp.dma_start(par[:, :, 0:3], I["hg_par"][l]).then_inc(ld_par, 16)
            sp.dma_start(masks[:], I["level_masks"]).then_inc(ld_par, 16)
            for h in rounds(sp, HG):
                wait(sp, dk_ready, h)
                sp.dma_start(f[:], proj[h + CF]).then_inc(ld_f, 16)
                wait(sp, tr_ready, h * 2 - 1)
                sp.dma_start(iv[:], proj[h + CI]).then_inc(ld_i, 16)
                wait(sp, sc_ready, h * NL)
                sp.dma_start(q[:], proj[h + CQ]).then_inc(ld_q, 16)
                wait(sp, head_done, h)
                sp.dma_start(z[:], proj[h + CZ]).then_inc(ld_z, 16)

        @block.gpsimd
        def _(pool):
            for h in rounds(pool, HG):
                for n in range(NL):
                    wait(pool, b_ready, h + 1)
                    wait(pool, ex_ready, h * NL + n - 1)
                    if n == 0:
                        last = chunks(b[:])[:, :, CH - 1:CH].to_broadcast([P, NC, CH])
                        pool.tensor_tensor(chunks(dif[:, 0]), last, chunks(b[:]), ALU.subtract).then_inc(dif_ready, 1)
                    else:
                        m = LEVELS[n - 1]
                        blocks = b[:].rearrange("p (b n) -> p b n", n=2 * m)
                        mid = blocks[:, :, m - 1:m].to_broadcast([P, T // (2 * m), 2 * m])
                        pool.tensor_tensor(dif[:, n % 2].rearrange("p (b n) -> p b n", n=2 * m), blocks, mid,
                                           ALU.subtract).then_inc(dif_ready, 1)

        @block.scalar
        def _(act):
            mine = Steps(act, own_a)
            act.wait_ge(small, 3)
            act.activation(tmp[:, :, 0:2], tmp[:, :, 0:2], ACT.Exp).then_inc(lb_exp, 1)
            act.wait_ge(lb_in, 2)
            act.activation(tmp[:, :, 2:4], tmp[:, :, 0:2], ACT.Ln).then_inc(lb_log, 1)
            PER = 4
            for h in rounds(act, HG):
                mine.loop(h * PER)
                wait(act, nabs_ready, h + 1)
                mine.do(act.activation(t1[:], t1[:], ACT.Exp))
                act.activation(t1[:], t1[:], ACT.Ln, bias=1.0).then_inc(ln1_ready, 1)
                wait(act, dk_ready, h + 1)
                act.activation(kk[:], kk[:], ACT.Exp).then_inc(ek_ready, 1)
                wait(act, nd_ready, h + 1)
                mine.do(act.activation(t1[:], t1[:], ACT.Exp))
                act.activation(t1[:], t1[:], ACT.Ln, bias=1.0).then_inc(ln2_ready, 1)
                wait(act, b_ready, h + 1)
                act.activation(eb[:], b[:], ACT.Exp).then_inc(eb_ready, 1)
                wait(act, tr_ready, h * 2 + 1)
                act.activation(vtok[:], pv, ACT.Copy).then_inc(tr_taken, 1)
                for n in range(NL):
                    wait(act, dif_ready, h * NL + (n + 1))
                    wait(act, ops_ready, h * NL + (n - 1))
                    if n == 0:
                        act.activation(ex[:, 0], dif[:, 0], ACT.Exp).then_inc(ex_ready, 1)
                    else:
                        m = LEVELS[n - 1]
                        act.activation(halves(ex[:, n % 2], m, 0), halves(dif[:, n % 2], m, 0), ACT.Exp, scale=-1.0)
                        act.activation(halves(ex[:, n % 2], m, 1), halves(dif[:, n % 2], m, 1), ACT.Exp).then_inc(ex_ready, 1)
                    if n == 2:
                        wait(act, tr_ready, h * 2 + 2)
                        act.activation(ktok[:], po, ACT.Copy).then_inc(tr_taken, 1)
                wait(act, ld_z, h * 16 + 16, 16)
                mine.do(act.activation(t1[:], z[:], ACT.Exp, scale=-1.0))
                act.activation(t1[:], t1[:], ACT.Identity, bias=1.0).then_inc(ez_ready, 1)
                wait(act, o_ready, h + 1)
                act.activation(t2[:], po, ACT.Square).then_inc(sq_ready, 1)
                wait(act, ms_ready, h + 1)
                mine.do(act.activation(t2[:], pv, ACT.Ln, scale=1.0 / P, bias=RMS_EPS))
                act.activation(t2[:], t2[:], ACT.Exp, scale=-0.5).then_inc(rstd_ready, 1)
                assert mine.n == PER

        def take_scores(dve, h, n):
            wait(dve, sc_ready, h * NL + (n + 1))
            wait(dve, sc_taken, h * NL + n)
            dve.copy_predicated(chunks(acc[:]), masks[:, n:n + 1, :].to_broadcast([P, NC, P]), chunks(sc[n % 2]))\
               .then_inc(sc_taken, 1)

        @block.vector
        def _(dve):
            mine = Steps(dve, own)
            mine.mark(dve.memset(acc[:], 0.0))
            mine.mark(dve.memset(qt[:], 0.0))
            mine.mark(dve.memset(kt[:], 0.0))
            mine.do(dve.memset(m0[:], 1.0))
            mine.mark(dve.memset(chunks(m0[:])[:, :, 0:1], 0.0))
            dve.wait_ge(ld_par, 32)
            mine.do(dve.tensor_tensor(tmp[:, :, 2:3], par[:, :, 0:1], par[:, :, 1:2], ALU.max))
            for c in range(2):
                dve.tensor_tensor(tmp[:, :, c:c + 1], par[:, :, c:c + 1], tmp[:, :, 2:3], ALU.subtract).then_inc(small, 1)
            dve.memset(par[:, :, 6:8], 0.0).then_inc(small, 1)
            dve.wait_ge(lb_exp, 1)
            dve.wait_ge(small, 3)
            mine.do(dve.tensor_tensor(tmp[:, :, 2:3], tmp[:, :, 0:1], tmp[:, :, 1:2], ALU.add))
            mine.do(dve.reciprocal(tmp[:, :, 2:3], tmp[:, :, 2:3]))
            mine.do(dve.tensor_tensor(tmp[:, :, 0:2], tmp[:, :, 0:2], tmp[:, :, 2:3].to_broadcast([P, HG, 2]), ALU.mult))
            if l:
                mine.do(dve.tensor_tensor(tmp[:, :, 3:4], tmp[:, :, 0:1], tmp[:, :, 1:2], ALU.add))
            else:
                mine.do(dve.tensor_copy(tmp[:, :, 3:4], tmp[:, :, 0:1]))
            mine.do(dve.tensor_tensor(tmp[:, :, 3:4], tmp[:, :, 3:4], tmp[:, :, 0:1], ALU.subtract))
            mine.do(dve.tensor_scalar(par[:, :, 3:4], tmp[:, :, 3:4], -1.0, 1.0, ALU.mult, ALU.add))
            dve.tensor_scalar(tmp[:, :, 0:1], tmp[:, :, 3:4], LB_FLOOR, 2.0 ** 50, ALU.max, ALU.mult).then_inc(lb_in, 1)
            dve.tensor_scalar(tmp[:, :, 1:2], par[:, :, 3:4], 1e-18, None, ALU.max).then_inc(lb_in, 1)
            dve.wait_ge(lb_log, 1)
            mine.do(dve.tensor_scalar(par[:, :, 4:5], tmp[:, :, 2:3], -50 * LN2, None, ALU.add))
            mine.do(dve.tensor_tensor(par[:, :, 5:6], tmp[:, :, 3:4], par[:, :, 4:5], ALU.subtract))
            BASE, PER = mine.n, 11
            for h in rounds(dve, HG):
                mine.loop(h * PER + BASE)
                mine.do(dve.tensor_copy(cur[:].unsqueeze(1), par[:, bass.ds(h, 1), :]))
                wait(dve, ld_f, h * 16 + 16, 16)
                dve.scalar_tensor_tensor(t1[:], f[:], -1.0, f[:], ALU.mult, ALU.min).then_inc(nabs_ready, 1)
                wait(dve, ln1_ready, h + 1)
                mine.do(dve.scalar_tensor_tensor(t2[:], f[:], 0.0, t1[:], ALU.min, ALU.subtract))
                dve.tensor_tensor(kk[:], t2[:], f[:], ALU.subtract).then_inc(dk_ready, 1)
                wait(dve, dk_ready, h + 1)
                mine.do(dve.tensor_scalar(t2[:], t2[:], cur[:, 5:6], None, ALU.add))
                dve.scalar_tensor_tensor(t1[:], t2[:], -1.0, t2[:], ALU.mult, ALU.min).then_inc(nd_ready, 1)
                wait(dve, ln2_ready, h + 1)
                mine.do(dve.scalar_tensor_tensor(t2[:], t2[:], 0.0, t1[:], ALU.max, ALU.add))
                mine.do(dve.tensor_scalar(t2[:], t2[:], cur[:, 4:5], None, ALU.add))
                dve.tensor_tensor_scan(b[:], m0[:], t2[:], 0.0, ALU.mult, ALU.add).then_inc(b_ready, 1)
                wait(dve, ek_ready, h + 1)
                mine.do(dve.tensor_scalar(kk[:], kk[:], cur[:, 3:4], None, ALU.mult))
                wait(dve, eb_ready, h + 1)
                wait(dve, ld_q, h * 16 + 16, 16)
                mine.mark(dve.tensor_tensor(qh[:], q[:], eb[:], ALU.mult))
                for n in range(NL):
                    wait(dve, ex_ready, h * NL + (n + 1))
                    if n == 0:
                        dve.tensor_tensor(kh[:], kk[:], ex[:, 0], ALU.mult).then_inc(ops_ready, 1)
                        continue
                    m, u = LEVELS[n - 1], n % 2
                    wait(dve, sc_ready, h * NL + (n - 2))
                    dve.tensor_tensor(halves(kt[:, u], m, 0), halves(kk[:], m, 0), halves(ex[:, u], m, 0), ALU.mult)
                    dve.tensor_tensor(halves(qt[:, u], m, 1), halves(q[:], m, 1), halves(ex[:, u], m, 1), ALU.mult)\
                       .then_inc(ops_ready, 1)
                    if n >= 2:
                        take_scores(dve, h, n - 2)
                take_scores(dve, h, NL - 2)
                take_scores(dve, h, NL - 1)
                wait(dve, kv_ready, h + 1)
                for c in range(1, NC):
                    kv = pv[:, (c - 1) * P:c * P]
                    if c == 1:
                        ins = dve.tensor_copy(S[:, 1], kv)
                    else:
                        ins = dve.scalar_tensor_tensor(S[:, c], S[:, c - 1], eb[:, c * CH - 1:c * CH], kv, ALU.mult, ALU.add)
                    ins.then_inc(S_ready, 1)
                    wait(dve, S_ready, h * (NC - 1) + c)
                wait(dve, ez_ready, h + 1)
                mine.do(dve.reciprocal(t1[:], t1[:]))
                mine.mark(dve.tensor_tensor(t1[:], t1[:], z[:], ALU.mult))
                wait(dve, rstd_ready, h + 1)
                mine.do(dve.tensor_tensor(t2[:], po, t2[:], ALU.mult))
                mine.do(dve.tensor_scalar(t2[:], t2[:], cur[:, 2:3], None, ALU.mult))
                dve.tensor_tensor(k.yhg[:, h, :] if isinstance(h, int) else k.yhg[:, bass.ds(h, 1), :],
                                  t2[:] if isinstance(h, int) else t2[:].unsqueeze(1),
                                  t1[:] if isinstance(h, int) else t1[:].unsqueeze(1), ALU.mult).then_inc(head_done, 1)
                wait(dve, head_done, h + 1)
                assert mine.n == PER, mine.n

        @block.tensor
        def _(pe):
            for h in rounds(pe, HG):
                wait(pe, head_done, h)
                wait(pe, ld_i, h * 16 + 16, 16)
                for c in range(NC):
                    tr = pe.transpose(pv[:, c * P:(c + 1) * P], iv[:, c * P:(c + 1) * P], k.eye[:])
                tr.then_inc(tr_ready, 1)
                wait(pe, ops_ready, h * NL + 1)
                for c in range(NC):
                    tr = pe.transpose(po[:, c * P:(c + 1) * P], kh[:, c * P:(c + 1) * P], k.eye[:])
                tr.then_inc(tr_ready, 1)
                for n in range(NL):
                    wait(pe, sc_taken, h * NL + (n - 1))
                    if n < NL - 1:
                        wait(pe, ops_ready, h * NL + (n + 2))
                        a, r = kt[:, (n + 1) % 2], qt[:, (n + 1) % 2]
                    else:
                        a, r = kk[:], q[:]
                    for c in range(NC):
                        mm = pe.matmul(sc[n % 2][:, c * P:(c + 1) * P], a[:, c * P:(c + 1) * P], r[:, c * P:(c + 1) * P],
                                       start=True, stop=True)
                    mm.then_inc(sc_ready, 1)
                wait(pe, tr_taken, h * 2 + 2)
                for c in range(NC - 1):
                    mm = pe.matmul(pv[:, c * P:(c + 1) * P], ktok[:, c * P:(c + 1) * P], vtok[:, c * P:(c + 1) * P],
                                   start=True, stop=True)
                mm.then_inc(kv_ready, 1)
                wait(pe, sc_taken, h * NL + NL)
                for c in range(NC):
                    w = slice(c * P, (c + 1) * P)
                    if c:
                        wait(pe, S_ready, h * (NC - 1) + c)
                        pe.matmul(po[:, w], S[:, c, :], qh[:, w], start=True, stop=False)
                    mm = pe.matmul(po[:, w], vtok[:, w], acc[:, w], start=(c == 0), stop=True)
                mm.then_inc(o_ready, 1)
                wait(pe, sq_ready, h + 1)
                for a in range(2):
                    mm = pe.matmul(pv[:, a * HALF:(a + 1) * HALF], k.ones[:], t2[:, a * HALF:(a + 1) * HALF],
                                   start=True, stop=True)
                mm.then_inc(ms_ready, 1)


def rwkv(k, l):
    nc, I = k.nc, k.I
    HD = 64
    GC = 4
    LV = [2, 4, 8, 16, 32, 64]
    NLV = len(LV)
    NPAR = 15
    G2 = NC // GC
    with Stage(k, f"rw{l}") as s:
        raw = s.sb("raw", [P, 4, T + 1])
        lo = s.sb("lo", [P, T])
        par, cur = s.sb("par", [P, PAIRS, NPAR]), s.sb("cur", [P, NPAR])
        t1, t2, t3 = (s.sb(n, [P, T]) for n in ("t1", "t2", "t3"))
        b, lw, a, kk, km = (s.sb(n, [P, T]) for n in ("b", "lw", "a", "kk", "km"))
        X, XT, CT = (s.sb(n, [P, 2, GC, CH]) for n in ("X", "XT", "CT"))
        Ep, Em, Ex = (x[:].rearrange("p e c n -> p (e c n)") for x in (X, XT, CT))
        Y = t3[:].rearrange("p (e c n) -> p e c n", e=2, c=GC)
        AR = s.sb("AR", [P, NC, 2, CH])
        B, Kd = s.sb("B", [P, T]), s.sb("Kd", [P, T])
        At, Bt, Kt, Vt = (x[:].rearrange("p (c n) -> p c n", c=NC) for x in (kk, a, km, lw))
        LN, MP = s.sb("LN", [P, 2, GC, 2, CH]), s.sb("MP", [P, 2, GC, 2, CH])
        dd = LN[:].rearrange("p e c a n -> p e (c a n)")
        vf = MP[:].rearrange("p e c a n -> p e (c a n)")[:, 0, :]
        XA = b[:, 0:HALF].rearrange("p (c n) -> p c n", c=GC)
        MV = b[:, HALF:T].rearrange("p (e c n) -> p e c n", e=2, c=GC)
        SA, Sc, G = s.sb("SA", [P, P]), s.sb("Sc", [P, NC + 1, HD]), s.sb("G", [P, NC])
        SG = s.sb("SG", [P, HD])
        mLN, lev = s.sb("mLN", [P, 2, CH]), s.sb("lev", [P, 1 + NLV, CH])
        lev1T = s.sb("lev1T", [P, CH])
        bones, lora, vup = s.sb("bones", [P, P]), s.sb("lora", [P, P]), s.sb("vup", [32, P])
        proj, vfirst = k.scratch["proj"], k.scratch["vfirst"]
        r, kx, v, z = (raw[:, n, 1:T + 1] for n in range(4))

        def h2(ap, i):
            return ap[:, i * HALF:(i + 1) * HALF]

        names = ("st_spare ld_par ld_low ld_r ld_k ld_v ld_z ld_lora ld_vf st_v own own_a low_in low_tanh  pair_done "
                 "dif_ready shifted pre_ready exps_ready kk0_ready sq_ready ss_ready ssm_ready rn_ready b_ready "
                 "D_ready E_ready G_in G_ready ops_ready rk_ready tr_ready tr_taken bon_ready bon_done "
                 "pr_ready pr_taken l_ready x_ready ct_ready yy_ready yy_taken dx_ready mv_ready mv_taken xa_ready xa_taken "
                 "sa_psum sa_ready u_ready S_ready y_ready y_taken mu_ready ysq_in ysq_ready var_ready rstd_ready ez_ready")
        sm = {n: s.sem(n) for n in names.split()}
        (st_spare, ld_par, ld_low, ld_r, ld_k, ld_v, ld_z, ld_lora, ld_vf, st_v, own, own_a, low_in, low_tanh, pair_done,
         dif_ready, shifted, pre_ready, exps_ready, kk0_ready, sq_ready, ss_ready, ssm_ready, rn_ready, b_ready,
         D_ready, E_ready, G_in, G_ready, ops_ready, rk_ready, tr_ready, tr_taken, bon_ready, bon_done,
         pr_ready, pr_taken, l_ready, x_ready, ct_ready, yy_ready, yy_taken, dx_ready, mv_ready, mv_taken, xa_ready, xa_taken,
         sa_psum, sa_ready, u_ready, S_ready, y_ready, y_taken, mu_ready, ysq_in, ysq_ready, var_ready, rstd_ready,
         ez_ready) = (sm[n] for n in names.split())
        tiles = [(1, kx, ld_k, CK), (0, r, ld_r, CR), (2, v, ld_v, CV), (3, z, ld_z, CY)]
        block = s.block()

        @block.sync
        def _(sp):
            sp.dma_start(raw[:, 0, 1:T + 1], proj[CLOW]).then_inc(ld_low, 16)
            sp.dma_start(par[:, :, 0:13], I["rw_par"][l]).then_inc(ld_par, 16)
            sp.dma_start(mLN[:], I["causal_masks"]).then_inc(ld_par, 16)
            sp.dma_start(lev[:], I["pair_masks"]).then_inc(ld_par, 16)
            sp.dma_start(lev1T[:], I["pair_mask_t"]).then_inc(ld_par, 16)
            for p in rounds(sp, PAIRS):
                if isinstance(p, int):
                    sp.wait_ge(low_in, 1)
                wait(sp, rk_ready, p)
                sp.dma_start(kx, proj[p + CK]).then_inc(ld_k, 16)
                sp.dma_start(r, proj[p + CR]).then_inc(ld_r, 16)
                wait(sp, ssm_ready, p)
                sp.dma_start(lora[:], I["rw_lora"][l, p]).then_inc(ld_lora, 16)
                if l:
                    sp.dma_start(vup[:], I["v_up"][p]).then_inc(ld_lora, 16)
                else:
                    wait(sp, st_v, p * 16, 16)
                wait(sp, bon_done, p)
                sp.dma_start(v, proj[p + CV]).then_inc(ld_v, 16)
                wait(sp, pair_done, p)
                sp.dma_start(z, proj[p + CY]).then_inc(ld_z, 16)
                if l:
                    sp.dma_start(vf, vfirst[p]).then_inc(ld_vf, 16)
                if not l:
                    spare = k.scratch["yrow"].rearrange("(r b) n -> r b n", r=P)
                    n = (SLOT_BLOCKS - NE_BLOCKS) // PAIRS
                    sp.dma_start(spare[:, bass.ds(p * n + NE_BLOCKS, n), :],
                                 k.xT[:, 0:1, :].to_broadcast([P, n, D])).then_inc(st_spare, 16)
            if not l:
                sp.wait_ge(st_spare, 16 * PAIRS)

        @block.gpsimd
        def _(pool):
            for p in rounds(pool, PAIRS):
                for i, (n, ap, ld, _c) in enumerate(tiles):
                    wait(pool, ld, p * 16 + 16, 16)
                    wait(pool, shifted, p * 4 + (i - 1))
                    if i < 2:
                        wait(pool, pair_done, p)
                    pool.tensor_tensor(dd[:, i % 2], raw[:, n, 0:T], ap, ALU.subtract).then_inc(dif_ready, 1)
                wait(pool, b_ready, p + 1)
                mid = chunks(b[:])[:, :, CH // 2 - 1:CH // 2].to_broadcast([P, NC, CH])
                pool.tensor_tensor(chunks(t1[:]), chunks(b[:]), mid, ALU.subtract).then_inc(D_ready, 1)
                wait(pool, D_ready, p * 2 + 1)
                pool.tensor_tensor(lw[:], t1[:], lw[:], ALU.subtract).then_inc(D_ready, 1)
                for g in range(G2):
                    for n in range(NLV):
                        wait(pool, pr_taken, (p * G2 + g) * 4 + 2)
                        wait(pool, yy_ready, (p * G2 + g) * 2 * NLV + 2 * n)
                        if g == 0 and n == 0:
                            wait(pool, ops_ready, p * 4 + 4)
                        for e in range(2):
                            pool.tensor_tensor(CT[:, e], LN[:, e, :, 0, :],
                                               lev[:, 1 + n:2 + n, :].to_broadcast([P, GC, CH]), ALU.mult)\
                                .then_inc(ct_ready, 1)

        @block.scalar
        def _(act):
            mine = Steps(act, own_a)
            act.wait_ge(low_in, 1)
            act.activation(lo[0:HD, :], lo[0:HD, :], ACT.Tanh).then_inc(low_tanh, 1)
            PER = 2
            for p in rounds(act, PAIRS):
                mine.loop(p * PER)
                wait(act, pre_ready, p * (2 + l) + 1)
                wait(act, shifted, p * 4 + 1)
                wait(act, pair_done, p)
                act.activation(t1[:], banks(k, 0), ACT.Sigmoid, bias=cur[:, 4:5]).then_inc(exps_ready, 1)
                wait(act, pre_ready, p * (2 + l) + 2)
                act.activation(a[:], banks(k, 2), ACT.Sigmoid, bias=cur[:, 5:6]).then_inc(exps_ready, 1)
                if l:
                    wait(act, pre_ready, p * 3 + 3)
                    act.activation(t3[:], banks(k, 4), ACT.Sigmoid, bias=cur[:, 11:12]).then_inc(exps_ready, 1)
                else:
                    wait(act, shifted, p * 4 + 3)
                    act.dma_start(vfirst[p], v).then_inc(st_v, 16)
                wait(act, kk0_ready, p + 1)
                act.activation(t2[:], kk[:], ACT.Square).then_inc(sq_ready, 1)
                wait(act, ssm_ready, p + 1)
                mine.do(act.activation(t2[:], t2[:], ACT.Ln, scale=2.0 ** 20))
                act.activation(t2[:], t2[:], ACT.Exp, scale=-0.5, bias=cur[:, 14:15]).then_inc(rn_ready, 1)
                wait(act, D_ready, p * 2 + 1)
                act.activation(Ep, t1[:], ACT.Exp).then_inc(E_ready, 1)
                act.activation(Em, t1[:], ACT.Exp, scale=-1.0).then_inc(E_ready, 1)
                wait(act, D_ready, p * 2 + 2)
                act.activation(Ex, lw[:], ACT.Exp).then_inc(E_ready, 1)
                wait(act, G_in, p + 1)
                act.activation(G[:], G[:], ACT.Exp).then_inc(G_ready, 1)
                wait(act, ops_ready, p * 4 + 4)
                wait(act, rk_ready, p + 1)
                for n, dst in enumerate((At, Bt, Kt, Vt)):
                    wait(act, tr_ready, p * 4 + (n + 1))
                    act.activation(dst.rearrange("p c n -> p (c n)"), banks(k, 2 * n), ACT.Copy).then_inc(tr_taken, 1)
                for g in range(G2):
                    q = p * G2 + g
                    wait(act, mv_ready, q + 1)
                    act.activation(b[:, HALF:T], k.ps[:, 6, :], ACT.Copy).then_inc(mv_taken, 1)
                    for n in range(NLV):
                        for e in range(2):
                            wait(act, yy_ready, q * 2 * NLV + (2 * n + e + 1))
                            wait(act, dx_ready, q * 2 * NLV + (2 * (n - 1) + e + 1))
                            act.activation(Y[:, e].rearrange("p c n -> p (c n)"), k.ps[:, e, :], ACT.Copy).then_inc(yy_taken, 1)
                    wait(act, xa_ready, q + 1)
                    act.activation(b[:, 0:HALF], k.ps[:, 7, :], ACT.Copy).then_inc(xa_taken, 1)
                wait(act, ysq_in, p + 1)
                act.activation(t3[:], t2[:], ACT.Square).then_inc(ysq_ready, 1)
                wait(act, var_ready, p + 1)
                mine.do(act.activation(t3[:], banks(k, 2), ACT.Ln, scale=1.0 / HD, bias=GN_EPS))
                act.activation(t3[:], t3[:], ACT.Exp, scale=-0.5).then_inc(rstd_ready, 1)
                wait(act, shifted, p * 4 + 4)
                act.activation(b[:], z, ACT.Sigmoid).then_inc(ez_ready, 1)
                assert mine.n == PER
            if not l:
                act.wait_ge(st_v, 16 * PAIRS)

        @block.vector
        def _(dve):
            mine = Steps(dve, own)
            mine.mark(dve.memset(raw[:, :, 0:1], 0.0))
            mine.mark(dve.memset(bones[:], 0.0))
            mine.mark(dve.memset(Sc[:, 0], 0.0))
            mine.settle()
            for e in range(2):
                mine.mark(dve.memset(bones[e * HD:(e + 1) * HD, e * HD:(e + 1) * HD], 1.0))
            dve.wait_ge(ld_par, 64)
            mine.mark(dve.tensor_scalar(par[:, :, 13:14], par[:, :, 7:8], -1.0, 1.0, ALU.mult, ALU.add))
            mine.mark(dve.memset(par[:, :, 14:15], 10 * LN2))
            dve.wait_ge(ld_low, 16)
            mine.do(dve.tensor_tensor(t1[:], raw[:, 0, 0:T], r, ALU.subtract))
            dve.scalar_tensor_tensor(lo[:], t1[:], par[:, 0, 12:13], r, ALU.mult, ALU.add).then_inc(low_in, 1)
            dve.wait_ge(low_tanh, 1)
            BASE, PER = mine.n, 31 + 3 * l
            for p in rounds(dve, PAIRS):
                mine.loop(p * PER + BASE)
                mine.do(dve.tensor_copy(cur[:].unsqueeze(1), par[:, bass.ds(p, 1), :]))

                def shift(i):
                    n, ap = tiles[i][0:2]
                    wait(dve, dif_ready, p * 4 + (i + 1))
                    dve.scalar_tensor_tensor(ap, dd[:, i % 2], cur[:, n:n + 1], ap, ALU.mult, ALU.add).then_inc(shifted, 1)

                shift(0)
                wait(dve, shifted, p * 4 + 1)
                dve.tensor_scalar(kk[:], kx, cur[:, 6:7], None, ALU.mult).then_inc(kk0_ready, 1)
                shift(1)
                shift(2)
                wait(dve, shifted, p * 4 + 3)
                wait(dve, exps_ready, p * (2 + l) + 1)
                mine.do(dve.tensor_scalar(lw[:], t1[:], -E_HALF, None, ALU.mult))
                for c in range(NC):
                    cs = slice(c * CH, (c + 1) * CH)
                    ins = dve.tensor_tensor_scan(b[:, cs], k.ones[:], lw[:, cs], 0.0, ALU.mult, ALU.add)
                ins.then_inc(b_ready, 1)
                wait(dve, b_ready, p + 1)
                cb = chunks(b[:])
                mine.do(dve.tensor_tensor(G[:].unsqueeze(2), cb[:, :, CH - 1:CH], cb[:, :, CH // 2 - 1:CH // 2], ALU.subtract))
                dve.tensor_tensor(G[:, 0:NC - 1].unsqueeze(2), G[:, 0:NC - 1].unsqueeze(2), cb[:, 1:NC, CH // 2 - 1:CH // 2],
                                  ALU.add).then_inc(G_in, 1)
                wait(dve, exps_ready, p * (2 + l) + 2)
                if l:
                    wait(dve, exps_ready, p * 3 + 3)
                    wait(dve, ld_vf, p * 16 + 16, 16)
                    mine.do(dve.tensor_tensor(vf, vf, v, ALU.subtract))
                    mine.do(dve.tensor_tensor(vf, vf, t3[:], ALU.mult))
                    mine.do(dve.tensor_tensor(v, v, vf, ALU.add))
                wait(dve, ss_ready, p + 1)
                dve.tensor_scalar(t2[:], banks(k, 6), L2_EPS ** 2, None, ALU.max).then_inc(ssm_ready, 1)
                mine.do(dve.tensor_scalar(km[:], a[:], cur[:, 7:8], cur[:, 13:14], ALU.mult, ALU.add))
                mine.do(dve.tensor_tensor(km[:], km[:], kx, ALU.mult))
                wait(dve, rn_ready, p + 1)
                mine.do(dve.tensor_tensor(kk[:], kk[:], t2[:], ALU.mult))
                wait(dve, E_ready, p * 3 + 3)
                dve.tensor_tensor(AR[:, :, 0, :], chunks(kk[:]), chunks(Ex), ALU.mult).then_inc(ops_ready, 1)
                mine.do(dve.tensor_tensor(B[:], kk[:], a[:], ALU.mult))
                dve.tensor_tensor(B[:], B[:], Em, ALU.mult).then_inc(ops_ready, 1)
                dve.tensor_tensor(Kd[:], km[:], Em, ALU.mult).then_inc(ops_ready, 1)
                dve.tensor_tensor(AR[:, :, 1, :], chunks(r), chunks(Ep), ALU.mult).then_inc(ops_ready, 1)
                dve.scalar_tensor_tensor(t2[:], r, cur[:, 8:9], km[:], ALU.mult, ALU.mult).then_inc(rk_ready, 1)
                shift(3)
                wait(dve, bon_ready, p + 1)
                dve.tensor_tensor(t1[:], banks(k, 0), v, ALU.mult).then_inc(bon_done, 1)
                wait(dve, G_ready, p + 1)
                for g in range(G2):
                    q = p * G2 + g
                    for n, dst in enumerate((LN, MP)):
                        for e in range(2):
                            wait(dve, pr_ready, q * 4 + (2 * n + e + 1))
                            dve.tensor_tensor(dst[:, e].rearrange("p c a n -> p c (a n)"),
                                              banks(k, 4 * n + 2 * e).rearrange("p (c m) -> p c m", c=GC),
                                              mLN[:].rearrange("p a n -> p (a n)").unsqueeze(1).to_broadcast([P, GC, 2 * CH]),
                                              ALU.mult).then_inc(pr_taken, 1)
                    for e in range(2):
                        wait(dve, pr_taken, q * 4 + 4)
                        wait(dve, l_ready, q * 2 + (e + 1))
                        mine.mark(dve.tensor_tensor(X[:, e], k.ps[:, e, :].rearrange("p (c n) -> p c n", c=GC),
                                                    lev1T[:].unsqueeze(1).to_broadcast([P, GC, CH]), ALU.mult))
                        mine.do(dve.tensor_tensor(XT[:, e], LN[:, e, :, 0, :], lev[:, 0:1, :].to_broadcast([P, GC, CH]), ALU.mult))
                        eye = k.eye[:].unsqueeze(1).to_broadcast([P, GC, CH])
                        mine.mark(dve.tensor_tensor(X[:, e], eye, X[:, e], ALU.subtract))
                        dve.tensor_tensor(XT[:, e], eye, XT[:, e], ALU.subtract).then_inc(x_ready, 1)
                    for n in range(NLV):
                        for e in range(2):
                            wait(dve, dx_ready, q * 2 * NLV + (2 * n + e + 1))
                            wait(dve, x_ready, q * 2 * (NLV + 1) + (2 * n + e + 1))
                            if n < NLV - 1:
                                dve.tensor_tensor(X[:, e], X[:, e], k.ps[:, 4 + e, :].rearrange("p (c n) -> p c n", c=GC),
                                                  ALU.subtract)
                            dve.tensor_tensor(XT[:, e], XT[:, e], k.ps[:, 2 + e, :].rearrange("p (c n) -> p c n", c=GC),
                                              ALU.subtract).then_inc(x_ready, 1)
                    for cc in range(GC):
                        c = g * GC + cc
                        w = p * NC + c
                        wait(dve, sa_psum, w + 1)
                        if c:
                            wait(dve, u_ready, w)
                            wait(dve, y_ready, w)
                        else:
                            wait(dve, y_ready, w)
                        dve.tensor_scalar(SA[:].rearrange("p (e n) -> p e n", e=2), k.ps[:, 0:2, 0:HD], -1.0, None, ALU.mult).then_inc(sa_ready, 1)
                        mine.do(dve.tensor_scalar(SG[:], Sc[:, c], G[:, c:c + 1], None, ALU.mult))
                        wait(dve, u_ready, w + 1)
                        dve.scalar_tensor_tensor(Sc[:, c + 1], k.ps[:, 2, 0:HD], G[:, c:c + 1], SG[:], ALU.mult, ALU.add)\
                           .then_inc(S_ready, 1)
                        wait(dve, S_ready, w + 1)
                    wait(dve, y_ready, p * NC + (g * GC + GC))
                    dve.tensor_copy(t2[:, g * HALF:(g + 1) * HALF], k.ps[:, 4, :]).then_inc(y_taken, 1)
                wait(dve, mu_ready, p + 1)
                dve.scalar_tensor_tensor(t2[:], banks(k, 0), -1.0 / HD, t2[:], ALU.mult, ALU.add).then_inc(ysq_in, 1)
                wait(dve, rstd_ready, p + 1)
                mine.do(dve.tensor_tensor(t2[:], t2[:], t3[:], ALU.mult))
                mine.do(dve.tensor_scalar(t2[:], t2[:], cur[:, 9:10], cur[:, 10:11], ALU.mult, ALU.add))
                mine.do(dve.tensor_tensor(t2[:], t2[:], t1[:], ALU.add))
                wait(dve, ez_ready, p + 1)
                mine.do(dve.tensor_tensor(b[:], b[:], z, ALU.mult))
                dve.tensor_tensor(k.yrw[:, bass.ds(p, 1), :], t2[:].unsqueeze(1), b[:].unsqueeze(1), ALU.mult)\
                   .then_inc(pair_done, 1)
                wait(dve, pair_done, p + 1)
                assert mine.n == PER, mine.n

        @block.tensor
        def _(pe):
            pe.wait_ge(low_tanh, 1)
            for p in rounds(pe, PAIRS):
                wait(pe, pair_done, p)
                wait(pe, ld_lora, p * 16 * (1 + l) + 16 * (1 + l), 16 * (1 + l))
                for i in range(2):
                    mm = pe.matmul(k.ps[:, i, :], lora[0:HD, :], h2(lo[0:HD], i), start=True, stop=True)
                mm.then_inc(pre_ready, 1)
                for i in range(2):
                    mm = pe.matmul(k.ps[:, 2 + i, :], lora[HD:P, :], h2(lo[HD:P], i), start=True, stop=True)
                mm.then_inc(pre_ready, 1)
                if l:
                    for i in range(2):
                        mm = pe.matmul(k.ps[:, 4 + i, :], vup[:], h2(k.vd[:], i), start=True, stop=True)
                    mm.then_inc(pre_ready, 1)
                wait(pe, sq_ready, p + 1)
                for i in range(2):
                    mm = pe.matmul(k.ps[:, 6 + i, :], bones[:], h2(t2[:], i), start=True, stop=True)
                mm.then_inc(ss_ready, 1)
                for n, need in enumerate((1, 2, 3, 4)):
                    wait(pe, exps_ready, p * (2 + l) + (2 + l))
                    wait(pe, ssm_ready, p + 1)
                    wait(pe, ops_ready, p * 4 + need)
                    for c in range(NC):
                        src = (AR[:, c, 0, :], B[:, c * CH:(c + 1) * CH], Kd[:, c * CH:(c + 1) * CH],
                               raw[:, 2, 1 + c * CH:1 + (c + 1) * CH])[n]
                        tr = pe.transpose(k.ps[:, 2 * n + c // 4, (c % 4) * CH:(c % 4 + 1) * CH], src, k.eye[:])
                    tr.then_inc(tr_ready, 1)
                wait(pe, rk_ready, p + 1)
                wait(pe, tr_taken, p * 4 + 1)
                for i in range(2):
                    mm = pe.matmul(k.ps[:, i, :], bones[:], h2(t2[:], i), start=True, stop=True)
                mm.then_inc(bon_ready, 1)
                wait(pe, tr_taken, p * 4 + 4)
                wait(pe, bon_done, p + 1)
                for g in range(G2):
                    q = p * G2 + g
                    wait(pe, y_taken, q)
                    for n, lhs in enumerate((B, Kd)):
                        for e in range(2):
                            er = slice(e * HD, (e + 1) * HD)
                            for cc in range(GC):
                                c = g * GC + cc
                                mm = pe.matmul(k.ps[:, 4 * n + 2 * e + cc // 2, (cc % 2) * 256:(cc % 2 + 1) * 256],
                                               lhs[er, c * CH:(c + 1) * CH], AR[er, c, :, :].rearrange("p a n -> p (a n)"),
                                               start=True, stop=True)
                            mm.then_inc(pr_ready, 1)
                    for e in range(2):
                        er = slice(e * HD, (e + 1) * HD)
                        wait(pe, pr_taken, q * 4 + 1)
                        for cc in range(GC):
                            c = g * GC + cc
                            mm = pe.matmul(k.ps[:, e, cc * CH:(cc + 1) * CH], AR[er, c, 0, :], B[er, c * CH:(c + 1) * CH],
                                           start=True, stop=True)
                        mm.then_inc(l_ready, 1)
                    wait(pe, pr_taken, q * 4 + 4)
                    for e in range(2):
                        for cc in range(GC):
                            mm = pe.matmul(k.ps[:, 6, (e * GC + cc) * HD:(e * GC + cc + 1) * HD], MP[:, e, cc, 0, :],
                                           Vt[:, g * GC + cc, e * HD:(e + 1) * HD], start=True, stop=True)
                    mm.then_inc(mv_ready, 1)
                    for n in range(NLV):
                        for e in range(2):
                            wait(pe, x_ready, q * 2 * (NLV + 1) + (2 * n + e + 1))
                            wait(pe, ct_ready, q * 2 * NLV + (2 * n + e + 1))
                            wait(pe, yy_taken, q * 2 * NLV + (2 * (n - 1) + e + 1))
                            for cc in range(GC):
                                mm = pe.matmul(k.ps[:, e, cc * CH:(cc + 1) * CH], CT[:, e, cc, :], X[:, e, cc, :],
                                               start=True, stop=True)
                            mm.then_inc(yy_ready, 1)
                        for e in range(2):
                            wait(pe, yy_taken, q * 2 * NLV + (2 * n + e + 1))
                            for cc in range(GC):
                                mm = pe.matmul(k.ps[:, 2 + e, cc * CH:(cc + 1) * CH], Y[:, e, cc, :], XT[:, e, cc, :],
                                               start=True, stop=True)
                            if n < NLV - 1:
                                for cc in range(GC):
                                    mm = pe.matmul(k.ps[:, 4 + e, cc * CH:(cc + 1) * CH], XT[:, e, cc, :], Y[:, e, cc, :],
                                                   start=True, stop=True)
                            mm.then_inc(dx_ready, 1)
                    wait(pe, x_ready, q * 2 * (NLV + 1) + 2 * (NLV + 1))
                    for e in range(2):
                        for cc in range(GC):
                            mm = pe.matmul(k.ps[e * HD:(e + 1) * HD, 7, cc * CH:(cc + 1) * CH],
                                           At[:, g * GC + cc, e * HD:(e + 1) * HD], XT[:, e, cc, :], start=True, stop=True)
                    mm.then_inc(xa_ready, 1)
                    wait(pe, mv_taken, q + 1)
                    wait(pe, xa_taken, q + 1)
                    for cc in range(GC):
                        c = g * GC + cc
                        w = p * NC + c
                        for e in range(2):
                            pe.matmul(k.ps[:, e, 0:HD], XT[:, e, cc, :], MV[:, e, cc, :], start=True, stop=False)
                            if e == 0 and c:
                                wait(pe, S_ready, w)
                            mm = pe.matmul(k.ps[:, e, 0:HD], XA[e * HD:(e + 1) * HD, cc, :],
                                           Sc[e * HD:(e + 1) * HD, c, :], start=False, stop=True)
                        mm.then_inc(sa_psum, 1)
                        for e in range(2):
                            ec = slice(e * HD, (e + 1) * HD)
                            pe.matmul(k.ps[ec, 2, 0:HD], Kt[:, c, ec], Vt[:, c, ec], start=True, stop=False)
                            if e == 0:
                                wait(pe, sa_ready, w + 1)
                            mm = pe.matmul(k.ps[ec, 2, 0:HD], Bt[:, c, ec], SA[:, ec], start=False, stop=True)
                        mm.then_inc(u_ready, 1)
                        for e in range(2):
                            ec = slice(e * HD, (e + 1) * HD)
                            y = k.ps[ec, 4, cc * CH:(cc + 1) * CH]
                            pe.matmul(y, Vt[:, c, ec], MP[:, e, cc, 1, :], start=True, stop=False)
                            pe.matmul(y, SA[:, ec], LN[:, e, cc, 1, :], start=False, stop=False)
                            mm = pe.matmul(y, Sc[ec, c, :], AR[ec, c, 1, :], start=False, stop=True)
                        mm.then_inc(y_ready, 1)
                wait(pe, y_taken, p * G2 + G2)
                wait(pe, S_ready, p * NC + NC)
                for i in range(2):
                    mm = pe.matmul(k.ps[:, i, :], bones[:], h2(t2[:], i), start=True, stop=True)
                mm.then_inc(mu_ready, 1)
                wait(pe, ysq_ready, p + 1)
                for i in range(2):
                    mm = pe.matmul(k.ps[:, 2 + i, :], bones[:], h2(t3[:], i), start=True, stop=True)
                mm.then_inc(var_ready, 1)


def merge(k, l):
    nc, I = k.nc, k.I
    NJ = D // P
    NQ = 3 * NJ
    with Stage(k, f"mix{l}") as s:
        hS, mS = s.sb("hS", [P, 2, KT, HALF], F32R), s.sb("mS", [P, 2, KT, HALF], F32R)
        sc1, gate, gcur = s.sb("sc1", [P, KT]), s.sb("gate", [P, KT]), s.sb("gcur", [P, 1])
        shift = s.sb("shift", [P, KT])
        lnp = s.sb("lnp", [P, 2, KT])
        w, wS = s.sb("w", [P, 2, KT, P]), s.sb("wS", [P, 2, 2, KT, P], F32R)
        wb = s.sb("wb", [P, 2, KT, P])
        sg, tmp = s.sb("sg", [P, 2, 2, HALF]), s.sb("tmp", [P, HALF])
        t = s.sb("t", [P, 2, HALF])
        sq, rstd = s.sb("sq", [P, KT, HALF]), s.sb("rstd", [P, HALF])
        ld_w, ld_wb = [s.sem("ld_w0"), s.sem("ld_w1")], [s.sem("ld_wb0"), s.sem("ld_wb1")]
        ld_p = s.sem("ld_p")
        (own_h, h_ready, hi_ready, lo_ready, slab_done, ys_ready, sg_ready, m_ready, mul_done, gcur_ready, t_ready, x_ready,
         mean_ready, xc_ready, sq_ready, var_ready, own_a, rstd_ready, own, own_n) = (s.sem(n) for n in (
             "own_h h_ready hi_ready lo_ready slab_done ys_ready sg_ready m_ready mul_done gcur_ready t_ready x_ready "
             "mean_ready xc_ready sq_ready var_ready own_a rstd_ready own own_n").split())
        block = s.block()

        @block.sync
        def _(sp):
            sp.dma_start(lnp[:], I["ln_par"][l]).then_inc(ld_p, 16)
            for hf in range(2):
                for i in rounds(sp, NJ // 2):
                    for b in range(2):
                        j = i * 2 + b
                        for g, first in enumerate((CG1, CG2)):
                            wait(sp, lo_ready, j * 2 + (hf * NQ + g - 1))
                            sp.dma_start(w[:, g], I["w_in"][l, j + first]).then_inc(ld_w[g], 16)
                        wait(sp, ys_ready, j * 2 + (hf * 2 * NJ - 2))
                        sp.dma_start(wb[:, b, 0:4], I["w_branch_hg"][l, j]).then_inc(ld_wb[b], 16)
                        sp.dma_start(wb[:, b, 4:8], I["w_branch_rw"][l, j]).then_inc(ld_wb[b], 16)
                for i in rounds(sp, NJ // 2):
                    for b in range(2):
                        j = i * 2 + b
                        wait(sp, lo_ready, j + (hf * NQ + 2 * NJ - 1))
                        sp.dma_start(w[:, b], I["w_out"][l, j]).then_inc(ld_w[b], 16)

        @block.gpsimd
        def _(pool):
            for i in rounds(pool, NQ):
                for b in range(2):
                    wait(pool, hi_ready, i * 2 + (b + 1))
                    pool.tensor_tensor(wS[:, b, 1], w[:, b], wS[:, b, 0], ALU.subtract).then_inc(lo_ready, 1)

        @block.scalar
        def _(act):
            mine = Steps(act, own_a)

            def high(q, b, loaded):
                wait(act, ld_w[b], loaded, 16)
                wait(act, slab_done, q - 1)
                act.activation(wS[:, b, 0], w[:, b], ACT.Copy).then_inc(hi_ready, 1)

            def squares(hf):
                for j in range(KT):
                    act.wait_ge(xc_ready, hf * KT + j + 1)
                    act.activation(sq[:, j], k.xT[:, j, hf * HALF:(hf + 1) * HALF], ACT.Square).then_inc(sq_ready, 1)

            def deviation(hf):
                act.wait_ge(var_ready, hf + 1)
                mine.do(act.activation(rstd[:], k.ps[:, 6, :], ACT.Ln, scale=1.0 / D, bias=LN_EPS))
                act.activation(rstd[:], rstd[:], ACT.Exp, scale=-0.5).then_inc(rstd_ready, 1)

            high(0, 0, 16)
            high(1, 1, 16)
            for hf in range(2):
                for i in rounds(act, NJ // 2):
                    for b in range(2):
                        j = i * 2 + b
                        for g in range(2):
                            q = j * 2 + (hf * NQ + g)
                            wait(act, slab_done, q + 1)
                            wait(act, mul_done, j + (hf * NJ - 1))
                            act.activation(sg[:, b, g], k.ps[:, 4 * b + g, :], ACT.Sigmoid).then_inc(sg_ready, 1)
                            high(q + 2, g, (j + (hf * NQ // 2 + 2)) * 16)
                        if hf and isinstance(i, int) and b == 0:
                            deviation(0)
                for i in rounds(act, NJ // 2) if hf == 0 else ends(act, NJ // 2):
                    for b in range(2):
                        j = i * 2 + b
                        q = j + (hf * NQ + 2 * NJ)
                        wait(act, gcur_ready, j + (hf * NJ + 1))
                        wait(act, x_ready, j + (hf * NJ - 1))
                        wait(act, slab_done, q + 1)
                        act.activation(t[:, b], k.ps[:, 4 * b, :], ACT.Copy, scale=gcur[:, 0:1]).then_inc(t_ready, 1)
                        if not (hf and isinstance(i, int) and i):
                            high(q + 2, b, i * 16 + (hf * NQ // 2 + NJ + 2) * 16)
                squares(hf)
            deviation(1)

        @block.vector
        def _(dve):
            mine = Steps(dve, own)
            c = l * NADA1
            dve.tensor_copy(shift[:], k.cond[:, c:c + KT, 0]).then_inc(own_h, 1)
            dve.tensor_scalar(sc1[:], k.cond[:, c + KT:c + 2 * KT, 0], 1.0, None, ALU.add).then_inc(own_h, 1)
            dve.tensor_scalar(gate[:], k.cond[:, c + 2 * KT:c + 3 * KT, 0], 1.0, None, ALU.add).then_inc(own_h, 1)
            dve.wait_ge(own_h, 3)

            def split_h(j, hf, before):
                hs = slice(hf * HALF, (hf + 1) * HALF)
                x1, y1 = tmp[:].unsqueeze(1), bass.ds(j, 1)
                wait(dve, h_ready, before)
                mine.do(dve.tensor_scalar(x1, k.xT[:, y1, hs], sc1[:, y1], shift[:, y1], ALU.mult, ALU.add))
                mine.do(dve.tensor_copy(hS[:, 0, y1], x1))
                dve.tensor_tensor(hS[:, 1, y1], x1, hS[:, 0, y1], ALU.subtract).then_inc(h_ready, 1)

            norm = Steps(dve, own_n)

            def centre(hf):
                hs = slice(hf * HALF, (hf + 1) * HALF)
                dve.wait_ge(mean_ready, hf + 1)
                dve.wait_ge(x_ready, (hf + 1) * NJ)
                for j in range(KT):
                    dve.scalar_tensor_tensor(k.xT[:, j, hs], k.ps[:, 7, :], -1.0 / D, k.xT[:, j, hs], ALU.mult, ALU.add)\
                       .then_inc(xc_ready, 1)

            def normalise(hf):
                hs = slice(hf * HALF, (hf + 1) * HALF)
                dve.wait_ge(ld_p, 16)
                dve.wait_ge(xc_ready, (hf + 1) * KT)
                dve.wait_ge(sq_ready, (hf + 1) * KT)
                dve.wait_ge(rstd_ready, hf + 1)
                for j in range(KT):
                    norm.mark(dve.tensor_tensor(k.xT[:, j, hs], k.xT[:, j, hs], rstd[:], ALU.mult))
                norm.settle()
                for j in range(KT):
                    norm.mark(dve.tensor_scalar(k.xT[:, j, hs], k.xT[:, j, hs], lnp[:, 0, j:j + 1], lnp[:, 1, j:j + 1],
                                                ALU.mult, ALU.add))
                norm.settle()

            for j in range(KT):
                split_h(j, 0, j)
            base = mine.n
            for hf in range(2):
                hs = slice(hf * HALF, (hf + 1) * HALF)
                for i in rounds(dve, NJ // 2):
                    for b in range(2):
                        j = i * 2 + b
                        mine.loop(j + base)
                        for g in range(2):
                            wait(dve, sg_ready, j * 2 + (hf * 2 * NJ + g + 1))
                            wait(dve, ys_ready, j * 2 + (hf * 2 * NJ + g + 1))
                            dve.tensor_tensor(sg[:, b, g], sg[:, b, g], k.ps[:, 4 * b + 2 + g, :], ALU.mult).then_inc(m_ready, 1)
                        wait(dve, m_ready, j * 2 + (hf * 2 * NJ + 2))
                        wait(dve, h_ready, j + (KT + hf * (KT + NJ)))
                        dve.tensor_tensor(tmp[:], sg[:, b, 0], sg[:, b, 1], ALU.add).then_inc(mul_done, 1)
                        wait(dve, mul_done, j + (hf * NJ + 1))
                        y1 = bass.ds(j, 1)
                        if hf and isinstance(i, int) and b == 0:
                            dve.wait_ge(slab_done, NQ)
                        mine.do(dve.tensor_copy(mS[:, 0, y1], tmp[:].unsqueeze(1)))
                        dve.tensor_tensor(mS[:, 1, y1], tmp[:].unsqueeze(1), mS[:, 0, y1], ALU.subtract).then_inc(h_ready, 1)
                        if hf and isinstance(i, int) and b == 0:
                            normalise(0)
                base += NJ
                per = 2 if hf == 0 else 0
                for i in rounds(dve, NJ // 2):
                    for b in range(2):
                        j = i * 2 + b
                        mine.loop(j * per + base)
                        wait(dve, t_ready, j + hf * NJ)
                        dve.tensor_copy(gcur[:], gate[:, bass.ds(j, 1)]).then_inc(gcur_ready, 1)
                        if hf == 0:
                            split_h(j, 1, j + (KT + NJ))
                        wait(dve, t_ready, j + (hf * NJ + 1))
                        xj = k.xT[:, bass.ds(j, 1), hs]
                        dve.scalar_tensor_tensor(xj, xj, ALPHA, t[:, b:b + 1], ALU.mult, ALU.add).then_inc(x_ready, 1)
                base += per * NJ
                centre(hf)
            normalise(1)

        @block.tensor
        def _(pe):
            def split_product(bank, b, src, q, need=None):
                wait(pe, hi_ready, q + 1)
                wait(pe, lo_ready, q + 1)
                for x in range(KT):
                    if need is not None:
                        pe.wait_ge(h_ready, need + x)
                    for u, v in TERMS:
                        mm = pe.matmul(k.ps[:, bank, :], wS[:, b, u, x, :], src[:, v, x, :],
                                       start=(x == 0 and u + v == 0), stop=(x == KT - 1 and u == 1))
                mm.then_inc(slab_done, 1)

            def mean(hf):
                for x in range(KT):
                    pe.wait_ge(x_ready, hf * NJ + x + 1)
                    mm = pe.matmul(k.ps[:, 7, :], k.ones[:], k.xT[:, x, hf * HALF:(hf + 1) * HALF],
                                   start=(x == 0), stop=(x == KT - 1))
                mm.then_inc(mean_ready, 1)

            def variance(hf):
                for x in range(KT):
                    pe.wait_ge(sq_ready, hf * KT + x + 1)
                    mm = pe.matmul(k.ps[:, 6, :], k.ones[:], sq[:, x, :], start=(x == 0), stop=(x == KT - 1))
                mm.then_inc(var_ready, 1)

            for hf in range(2):
                hs = slice(hf * HALF, (hf + 1) * HALF)
                for i in rounds(pe, NJ // 2):
                    for b in range(2):
                        j = i * 2 + b
                        wait(pe, mul_done, j + (hf * NJ - 1))
                        if hf and isinstance(i, int):
                            pe.wait_ge(t_ready, NJ)
                        for g, y in enumerate((k.yhg, k.yrw)):
                            first = isinstance(i, int) and b == 0 and g == 0
                            split_product(4 * b + g, g, hS, j * 2 + (hf * NQ + g), hf * (NJ + KT) + 1 if first else None)
                            if g == 0:
                                wait(pe, ld_wb[b], i * 32 + (hf * NJ // 2 + 1) * 32, 32)
                            if hf and isinstance(i, int) and b == 1:
                                pe.wait_ge(rstd_ready, 1)
                            for x in range(4):
                                mm = pe.matmul(k.ps[:, 4 * b + 2 + g, :], wb[:, b, 4 * g + x, :], y[:, x, hs],
                                               start=(x == 0), stop=(x == 3))
                            mm.then_inc(ys_ready, 1)
                        if hf and isinstance(i, int) and b == 0:
                            variance(0)
                for i in rounds(pe, NJ // 2):
                    for b in range(2):
                        j = i * 2 + b
                        if isinstance(i, int) and b == 0:
                            pe.wait_ge(h_ready, KT + NJ + hf * (KT + NJ))
                        wait(pe, t_ready, j + (hf * NJ - 1))
                        split_product(4 * b, b, mS, j + (hf * NQ + 2 * NJ))
                mean(hf)
            variance(1)


CTX = 256
NKC = CTX // P
HD2 = 64
SCALE2 = HD2 ** -0.5
QH = 4
W2Q, W2K, W2V, W2P = 0, 4, 5, 6
POOLS = (2, 4, 8, 16)
PAD = 8
C2 = 2 * NADA1


def rms_modulated(k, name, jobs):
    nc, I = k.nc, k.I
    with Stage(k, name) as s:
        gain = s.sb("gain", [P, 2, KT])
        coef = s.sb("coef", [P, len(jobs), KT])
        rstd = s.sb("rstd", [P, len(jobs), T])
        ld, sq_ready, ss_ready, own_a, rstd_ready, own, scaled, done = (
            s.sem(n) for n in "ld sq_ready ss_ready own_a rstd_ready own scaled done".split())
        block = s.block()

        @block.sync
        def _(sp):
            sp.dma_start(gain[:], I["norm_g"]).then_inc(ld, 16)

        @block.scalar
        def _(act):
            mine = Steps(act, own_a)
            for i, (src, dst, N, g, c, v) in enumerate(jobs):
                for j in range(KT):
                    act.activation(dst[:, j, 0:N], src[:, j, 0:N], ACT.Square).then_inc(sq_ready, 1)
            for i, (src, dst, N, g, c, v) in enumerate(jobs):
                act.wait_ge(ss_ready, i + 1)
                ss = banks(k, 2 * i)[:, 0:N]
                mine.do(act.activation(rstd[:, i, 0:N], ss, ACT.Ln, scale=1.0 / D, bias=EPS))
                act.activation(rstd[:, i, 0:N], rstd[:, i, 0:N], ACT.Exp, scale=-0.5).then_inc(rstd_ready, 1)
                for j in range(KT):
                    act.wait_ge(scaled, i * KT + j + 1)
                    act.activation(dst[:, j, 0:N], dst[:, j, 0:N], ACT.Identity, bias=k.cond[:, c + j, v:v + 1]).then_inc(done, 1)

        @block.tensor
        def _(pe):
            for i, (src, dst, N, g, c, v) in enumerate(jobs):
                for j in range(KT):
                    pe.wait_ge(sq_ready, i * KT + j + 1)
                    for a in range(0, N, HALF):
                        n = min(HALF, N - a)
                        mm = pe.matmul(banks(k, 2 * i)[:, a:a + n], k.ones[:], dst[:, j, a:a + n], start=(j == 0), stop=(j == KT - 1))
                mm.then_inc(ss_ready, 1)

        @block.vector
        def _(dve):
            mine = Steps(dve, own)
            dve.wait_ge(ld, 16)
            for i, (src, dst, N, g, c, v) in enumerate(jobs):
                mine.do(dve.tensor_scalar(coef[:, i], k.cond[:, c + KT:c + 2 * KT, v], 1.0, None, ALU.add))
                mine.do(dve.tensor_tensor(coef[:, i], coef[:, i], gain[:, g], ALU.mult))
                dve.wait_ge(rstd_ready, i + 1)
                for j in range(KT):
                    dve.scalar_tensor_tensor(dst[:, j, 0:N], src[:, j, 0:N], coef[:, i, j:j + 1], rstd[:, i, 0:N],
                                             ALU.mult, ALU.mult).then_inc(scaled, 1)


def attention(k, hcT):
    nc, I = k.nc, k.I
    NB = T // P
    SW = CTX + 3 * P
    with Stage(k, "attn") as s:
        w = s.sb("w", [P, KT, P])
        wkv = s.sb("wkv", [P, 2, KT, P])
        cos, sin, rot = s.sb("cos", [P, T]), s.sb("sin", [P, T]), s.sb("rot", [P, P])
        kT, qT, raw = s.sb("kT", [P, CTX + T]), s.sb("qT", [P, T]), s.sb("raw", [P, T])
        vt = s.sb("vt", [P, NKC + NB, P])
        band = s.sb("band", [P, 3 * P])
        sink, scur = s.sb("sink", [P, QH, 2]), s.sb("scur", [P, 2])
        S = s.sb("S", [P, 2, SW])
        PT = s.sb("PT", [P, 2, 5, P])
        st = s.sb("st", [P, 2, 6])
        names = ("ld_c ld_kv ld_q kp_ready k_raw rot_ready kc_taken own vps_ready v_taken "
                 "q_ready q_raw qrot_ready q_done s_ready s_loc s_ctx max_ready e_ready es_ready p_ready pt_ready "
                 "pt_taken o_ready o_taken")
        (ld_c, ld_kv, ld_q, kp_ready, k_raw, rot_ready, kc_taken, own, vps_ready, v_taken,
         q_ready, q_raw, qrot_ready, q_done, s_ready, s_loc, s_ctx, max_ready, e_ready, es_ready, p_ready, pt_ready,
         pt_taken, o_ready, o_taken) = (s.sem(n) for n in names.split())
        block = s.block()
        mix = k.mix

        def width(n):
            a = max(n - 1, 0)
            return a, min(n + 1, NB - 1) - a + 1

        @block.sync
        def _(sp):
            sp.dma_start(wkv[:, 0], I["w_in2"][W2K]).then_inc(ld_kv, 16)
            sp.dma_start(wkv[:, 1], I["w_in2"][W2V]).then_inc(ld_kv, 16)
            sp.dma_start(rot[:], I["rot"]).then_inc(ld_c, 16)
            sp.dma_start(cos[:], I["cos"]).then_inc(ld_c, 16)
            sp.dma_start(sin[:], I["sin"]).then_inc(ld_c, 16)
            sp.dma_start(band[:], I["band"]).then_inc(ld_c, 16)
            sp.dma_start(sink[:], I["sink"]).then_inc(ld_c, 16)
            for j in rounds(sp, QH):
                wait(sp, q_ready, j)
                sp.dma_start(w[:], I["w_in2"][j + W2Q]).then_inc(ld_q, 16)

        @block.scalar
        def _(act):
            act.wait_ge(kp_ready, 1)
            act.activation(raw[:], banks(k, 0), ACT.Copy).then_inc(k_raw, 1)
            act.wait_ge(kp_ready, 2)
            act.activation(kT[:, 0:CTX], k.ps[:, 2, 0:CTX], ACT.Copy).then_inc(kc_taken, 1)
            act.wait_ge(vps_ready, 1)
            act.activation(vt[:, 0:NKC + 2, :].rearrange("p a n -> p (a n)"), k.ps[:, 5, :], ACT.Copy).then_inc(v_taken, 1)
            act.wait_ge(vps_ready, 2)
            act.activation(vt[:, NKC + 2:NKC + 6, :].rearrange("p a n -> p (a n)"), k.ps[:, 6, :], ACT.Copy).then_inc(v_taken, 1)
            act.wait_ge(vps_ready, 3)
            act.activation(vt[:, NKC + 6:NKC + 8, :].rearrange("p a n -> p (a n)"), k.ps[:, 7, 0:2 * P], ACT.Copy).then_inc(v_taken, 1)
            for j in rounds(act, QH):
                if isinstance(j, int):
                    act.wait_ge(own, 1)
                wait(act, q_ready, j + 1)
                act.activation(raw[:], banks(k, 0), ACT.Copy).then_inc(q_raw, 1)
                for n in range(NB):
                    a, nb = width(n)
                    u = j * 2 * NB + 2 * n
                    for e in range(2):
                        wait(act, s_ready, u + (e + 1))
                        wait(act, pt_ready, u + (e - 1))
                        act.activation(S[:, e, 0:CTX], k.ps[:, 2 * e + 1, 0:CTX], ACT.Copy, scale=SCALE2).then_inc(s_ctx, 1)
                    for e in range(2):
                        wait(act, max_ready, u + (e + 1))
                        act.activation(S[:, e, 0:CTX + nb * P], S[:, e, 0:CTX + nb * P], ACT.Exp, bias=st[:, e, 1:2],
                                       accum_out=st[:, e, 2:3]).then_inc(e_ready, 1)
                        act.activation(st[:, e, 3:4], scur[:, e:e + 1], ACT.Exp, bias=st[:, e, 1:2]).then_inc(es_ready, 1)
                    for e in range(2):
                        wait(act, pt_ready, u + (e + 1))
                        wait(act, o_ready, u + (e - 1))
                        act.activation(PT[:, e, 0:4, :].rearrange("p a n -> p (a n)"), k.ps[:, 4 + e, :], ACT.Copy).then_inc(pt_taken, 1)

        @block.vector
        def _(dve):
            mine = Steps(dve, own)

            def rope(dst, rotated):
                mine.do(dve.tensor_tensor(dst, raw[:], cos[:], ALU.mult))
                mine.do(dve.tensor_tensor(raw[:], rotated, sin[:], ALU.mult))
                return dve.tensor_tensor(dst, dst, raw[:], ALU.add)

            dve.wait_ge(ld_c, 80)
            dve.wait_ge(rot_ready, 1)
            dve.tensor_tensor(kT[:, CTX:], raw[:], cos[:], ALU.mult).then_inc(k_raw, 1)
            dve.wait_ge(k_raw, 2)
            dve.tensor_tensor(raw[:], banks(k, 3), sin[:], ALU.mult).then_inc(k_raw, 1)
            dve.wait_ge(k_raw, 3)
            dve.tensor_tensor(kT[:, CTX:], kT[:, CTX:], raw[:], ALU.add).then_inc(own, 1)
            BASE, PER = 1, 3 + NB * 2 * 3
            for j in rounds(dve, QH):
                mine.loop(j * PER + BASE)
                mine.mark(dve.tensor_copy(scur[:].unsqueeze(1), sink[:, bass.ds(j, 1), :]))
                wait(dve, qrot_ready, j + 1)
                rope(qT[:], banks(k, 2)).then_inc(q_done, 1)
                for n in range(NB):
                    a, nb = width(n)
                    u = j * 2 * NB + 2 * n
                    b0 = (a - (n - 1)) * P
                    for e in range(2):
                        wait(dve, s_ready, u + (e + 1))
                        wait(dve, pt_ready, u + (e - 1))
                        dve.scalar_tensor_tensor(S[:, e, CTX:CTX + nb * P], k.ps[:, 2 * e, 0:nb * P], SCALE2,
                                                 band[:, b0:b0 + nb * P], ALU.mult, ALU.add).then_inc(s_loc, 1)
                        wait(dve, s_loc, u + (e + 1))
                        wait(dve, s_ctx, u + (e + 1))
                        mine.do(dve.tensor_reduce(st[:, e, 0:1], S[:, e, 0:CTX + nb * P], AX, ALU.max))
                        dve.tensor_scalar(st[:, e, 1:2], st[:, e, 0:1], scur[:, e:e + 1], -1.0, ALU.max, ALU.mult).then_inc(max_ready, 1)
                    for e in range(2):
                        wait(dve, e_ready, u + (e + 1))
                        wait(dve, es_ready, u + (e + 1))
                        mine.do(dve.tensor_tensor(st[:, e, 4:5], st[:, e, 2:3], st[:, e, 3:4], ALU.add))
                        mine.do(dve.reciprocal(st[:, e, 5:6], st[:, e, 4:5]))
                        dve.tensor_scalar(S[:, e, 0:CTX + nb * P], S[:, e, 0:CTX + nb * P], st[:, e, 5:6], None, ALU.mult)\
                           .then_inc(p_ready, 1)
                    if nb == 3:
                        for e in range(2):
                            wait(dve, pt_ready, u + 2)
                            wait(dve, o_ready, u + (e - 1))
                            dve.tensor_copy(PT[:, e, 4, :], k.ps[:, 6, e * P:(e + 1) * P]).then_inc(pt_taken, 1)
                    wait(dve, o_ready, u + 2)
                    dve.tensor_copy(mix[:, bass.ds(j, 1), n * P:(n + 1) * P], k.ps[:, 7:8, 0:P]).then_inc(o_taken, 1)
                assert mine.n == PER, mine.n

        @block.tensor
        def _(pe):
            pe.wait_ge(ld_kv, 32)
            for half in range(2):
                for t in range(KT):
                    mm = pe.matmul(k.ps[:, half, :], wkv[:, 0, t, :], k.hT2[:, t, half * HALF:(half + 1) * HALF],
                                   start=(t == 0), stop=(t == KT - 1))
            mm.then_inc(kp_ready, 1)
            for t in range(KT):
                mm = pe.matmul(k.ps[:, 2, 0:CTX], wkv[:, 0, t, :], hcT[:, t, :], start=(t == 0), stop=(t == KT - 1))
            mm.then_inc(kp_ready, 1)
            for g, tiles in enumerate(((-2, -1, 0, 1), (2, 3, 4, 5), (6, 7))):
                for i, a in enumerate(tiles):
                    for t in range(KT):
                        lhs = hcT[:, t, (a + 2) * P:(a + 3) * P] if a < 0 else k.hT2[:, t, a * P:(a + 1) * P]
                        mm = pe.matmul(k.ps[:, 5 + g, i * P:(i + 1) * P], lhs, wkv[:, 1, t, :], start=(t == 0), stop=(t == KT - 1))
                mm.then_inc(vps_ready, 1)
            pe.wait_ge(ld_c, 80)
            pe.wait_ge(k_raw, 1)
            for half in range(2):
                mm = pe.matmul(k.ps[:, 3 + half, :], rot[:], raw[:, half * HALF:(half + 1) * HALF], start=True, stop=True)
            mm.then_inc(rot_ready, 1)
            pe.wait_ge(v_taken, 3)
            pe.wait_ge(kc_taken, 1)
            pe.wait_ge(own, 1)
            for j in rounds(pe, QH):
                wait(pe, ld_q, j * 16 + 16, 16)
                wait(pe, e_ready, j * 2 * NB)
                for half in range(2):
                    for t in range(KT):
                        mm = pe.matmul(k.ps[:, half, :], w[:, t, :], k.hT2[:, t, half * HALF:(half + 1) * HALF],
                                       start=(t == 0), stop=(t == KT - 1))
                mm.then_inc(q_ready, 1)
                wait(pe, q_raw, j + 1)
                for half in range(2):
                    mm = pe.matmul(k.ps[:, 2 + half, :], rot[:], raw[:, half * HALF:(half + 1) * HALF], start=True, stop=True)
                mm.then_inc(qrot_ready, 1)

                def scores(n):
                    a, nb = width(n)
                    u = j * 2 * NB + 2 * n
                    for e in range(2):
                        er = slice(e * HD2, (e + 1) * HD2)
                        if n == 0:
                            wait(pe, q_done, j + 1)
                        else:
                            wait(pe, s_loc, u + (e - 1))
                            wait(pe, s_ctx, u + (e - 1))
                        pe.matmul(k.ps[:, 2 * e, 0:nb * P], qT[er, n * P:(n + 1) * P], kT[er, CTX + a * P:CTX + (a + nb) * P],
                                  start=True, stop=True)
                        pe.matmul(k.ps[:, 2 * e + 1, 0:CTX], qT[er, n * P:(n + 1) * P], kT[er, 0:CTX],
                                  start=True, stop=True).then_inc(s_ready, 1)

                scores(0)
                for n in range(NB):
                    a, nb = width(n)
                    u = j * 2 * NB + 2 * n
                    if n + 1 < NB:
                        scores(n + 1)
                    taken = sum(4 if width(m)[1] == 3 else 2 for m in range(n))
                    per = sum(4 if width(m)[1] == 3 else 2 for m in range(NB))
                    for e in range(2):
                        wait(pe, p_ready, u + (e + 1))
                        wait(pe, pt_taken, j * per + taken)
                        for i in range(NKC + nb):
                            out = k.ps[:, 4 + e, i * P:(i + 1) * P] if i < 4 else k.ps[:, 6, e * P:(e + 1) * P]
                            tr = pe.transpose(out, S[:, e, i * P:(i + 1) * P], k.eye[:])
                        tr.then_inc(pt_ready, 1)
                    wait(pe, o_taken, j * NB + n)
                    wait(pe, pt_taken, j * per + (taken + (4 if nb == 3 else 2)))
                    for e in range(2):
                        ec = slice(e * HD2, (e + 1) * HD2)
                        for i in range(NKC + nb):
                            v = vt[:, i if i < NKC else NKC + a + i - NKC, ec]
                            mm = pe.matmul(k.ps[ec, 7, 0:P], v, PT[:, e, i, :], start=(i == 0), stop=(i == NKC + nb - 1))
                        mm.then_inc(o_ready, 1)


def pooling(k):
    nc, I = k.nc, k.I
    NG = len(POOLS)
    with Stage(k, "pool") as s:
        w, pw = s.sb("w", [P, 2, KT, P]), s.sb("pw", [P, NG, P])
        inv, scale = s.sb("inv", [P, NG, T]), s.sb("scale", [P, NG])
        pp = s.sb("pp", [P, 2, T + 2 * PAD])
        ws = s.sb("ws", [P, 2, T + 2 * PAD])
        ld_w, ld_c = [s.sem("ld_w0"), s.sem("ld_w1")], s.sem("ld_c")
        p_ready, p_taken, d_ready, y_ready, y_taken, own = (s.sem(n) for n in "p_ready p_taken d_ready y_ready y_taken own".split())
        block = s.block()

        @block.sync
        def _(sp):
            for g in range(NG):
                if g == 2:
                    sp.dma_start(pw[:], I["pool_w"]).then_inc(ld_c, 16)
                    sp.dma_start(inv[:], I["pool_inv"]).then_inc(ld_c, 16)
                    sp.dma_start(scale[:], I["pool_scale"]).then_inc(ld_c, 16)
                if g >= 2:
                    sp.wait_ge(p_ready, g - 1)
                sp.dma_start(w[:, g % 2], I["w_in2"][W2P + g]).then_inc(ld_w[g % 2], 16)

        @block.tensor
        def _(pe):
            def product(g):
                pe.wait_ge(d_ready, g + 1)
                if g:
                    pe.wait_ge(y_taken, g)
                for half in range(2):
                    mm = pe.matmul(k.ps[:, 4 + half, :], pw[:, g, :], ws[:, 0, half * HALF:(half + 1) * HALF], start=True, stop=True)
                mm.then_inc(y_ready, 1)

            for g in range(NG):
                pe.wait_ge(ld_w[g % 2], 16 * (g // 2 + 1))
                if g >= 2:
                    pe.wait_ge(p_taken, g - 1)
                for half in range(2):
                    for t in range(KT):
                        mm = pe.matmul(k.ps[:, 2 * (g % 2) + half, :], w[:, g % 2, t, :], k.hT2[:, t, half * HALF:(half + 1) * HALF],
                                       start=(t == 0), stop=(t == KT - 1))
                mm.then_inc(p_ready, 1)
                if g:
                    product(g - 1)
            product(NG - 1)

        @block.scalar
        def _(act):
            act.wait_ge(own, 1)
            for g in range(NG):
                act.wait_ge(p_ready, g + 1)
                if g >= 2:
                    act.wait_ge(d_ready, g - 1)
                act.activation(pp[:, g % 2, PAD:PAD + T], banks(k, 2 * (g % 2)), ACT.Copy).then_inc(p_taken, 1)
                if g:
                    act.wait_ge(ld_c, 48)
                    act.wait_ge(y_ready, g)
                    act.activation(k.mix[:, 4 + g - 1, :], banks(k, 4), ACT.Copy, scale=scale[:, g - 1:g]).then_inc(y_taken, 1)
            act.wait_ge(y_ready, NG)
            act.activation(k.mix[:, 3 + NG, :], banks(k, 4), ACT.Copy, scale=scale[:, NG - 1:NG]).then_inc(y_taken, 1)

        @block.vector
        def _(dve):
            mine = Steps(dve, own)
            mine.do(dve.memset(pp[:], 0.0))
            dve.wait_ge(ld_c, 48)
            for g, win in enumerate(POOLS):
                dve.wait_ge(p_taken, g + 1)
                if g:
                    dve.wait_ge(y_ready, g)
                src, n, step = pp[:, g % 2], T + 2 * PAD, 1
                for i in range(g + 1):
                    n -= step
                    dst = ws[:, i % 2]
                    mine.do(dve.tensor_tensor(dst[:, 0:n], src[:, 0:n], src[:, step:step + n], ALU.add))
                    src, step = dst, 2 * step
                first = PAD - win // 2
                mine.do(dve.tensor_tensor(ws[:, (g + 1) % 2, 0:T], src[:, first:first + T], inv[:, g], ALU.mult))
                dve.tensor_tensor(ws[:, 0, 0:T], ws[:, (g + 1) % 2, 0:T], pp[:, g % 2, PAD:PAD + T], ALU.subtract).then_inc(d_ready, 1)
                dve.wait_ge(d_ready, g + 1)


def project_out(k):
    nc, I = k.nc, k.I
    with Stage(k, "out") as s:
        w = s.sb("w", [P, 2, KT, P])
        ld_w = [s.sem("ld_w0"), s.sem("ld_w1")]
        o_ready, taken = s.sem("o_ready"), s.sem("taken")
        block = s.block()

        @block.sync
        def _(sp):
            for j in range(KT):
                if j >= 2:
                    sp.wait_ge(o_ready, j - 1)
                sp.dma_start(w[:, j % 2], I["w_out2"][j]).then_inc(ld_w[j % 2], 16)

        @block.tensor
        def _(pe):
            for j in range(KT):
                pe.wait_ge(ld_w[j % 2], 16 * (j // 2 + 1))
                if j >= 2:
                    pe.wait_ge(taken, j - 1)
                for half in range(2):
                    for t in range(KT):
                        mm = pe.matmul(k.ps[:, 2 * (j % 2) + half, :], w[:, j % 2, t, :], k.mix[:, t, half * HALF:(half + 1) * HALF],
                                       start=(t == 0), stop=(t == KT - 1))
                mm.then_inc(o_ready, 1)

        @block.vector
        def _(dve):
            for j in range(KT):
                dve.wait_ge(o_ready, j + 1)
                dve.scalar_tensor_tensor(k.xT[:, j], banks(k, 2 * (j % 2)), k.cond[:, C2 + 2 * KT + j, 1:2], k.xT[:, j],
                                         ALU.mult, ALU.add).then_inc(taken, 1)

NE = 64
NG = 8
TOPG, TOPK = 4, 8
DE = 256
ROUTED_SCALE = 2.5
NTT = T // P
NBLK = NE + T * TOPK // P
assert NBLK >= NE - 1 + T * TOPK // P and NBLK <= P
NR = NBLK // 2
BIG = 1e30


def used_rounds(eng, k):
    final = eng.snap(eng.value_load(k.nr[0:1, 0:1], min_val=0, max_val=NR - NE // 2) + (NE // 2 - 1))
    yield 0, False
    yield 1, False
    with eng.Fori(2, NR - 1) as i:
        with eng.If(i < final):
            yield i, False
    yield final, True


def route(k):
    nc, I = k.nc, k.I
    acc = k.mix
    with Stage(k, "route") as s:
        wr, bias = s.sb("wr", [P, KT, NE]), s.sb("bias", [P, NE])
        lower = s.sb("lower", [P, NG, NG])
        causal = s.sb("causal", [P, P])
        pidx, tokid = s.sb("pidx", [P, 1]), s.sb("tokid", [P, NTT], I32)
        zero = s.sb("zero", [P, NBLK], I32)
        sc, bi, sel, mask, gate, key = (s.sb(n, [P, NTT, NE]) for n in ("sc", "bi", "sel", "mask", "gate", "key"))
        u1, u2 = s.sb("u1", [P, NTT, NG, 4]), s.sb("u2", [P, NTT, NG, 4])
        v1, v2, v3 = (s.sb(n, [P, NTT, NG, 4]) for n in ("v1", "v2", "v3"))
        cmp = s.sb("cmp", [P, NTT, NG, NG])
        gs, gm, top = s.sb("gs", [P, NTT, NG]), s.sb("gm", [P, NTT, NG]), s.sb("top", [P, NTT, 8])
        tot = s.sb("tot", [P, NTT])
        ri, qi = s.sb("ri", [P, NTT * NE], I32), s.sb("qi", [P, NTT * NE], I32)
        ci, nb, end = s.sb("ci", [P, NE], I32), s.sb("nb", [P, NE]), s.sb("end", [P, NE])
        slotv, ebf, ebi = s.sb("slotv", [P, NTT, 8]), s.sb("ebf", [P, 1]), s.sb("ebi", [P, 1], I32)
        pick = s.sb("pick", [P, 8, NE])
        cmp2 = pick[:].rearrange("p t (g n) -> p t g n", g=NG)
        hrow = s.sb("hrow", [P, 2, D])
        wgu, wd = s.sb("wgu", [P, 2, 2, KT, P]), s.sb("wd", [P, 2, D])
        aT = s.sb("aT", [P, 2, T])
        sg = hrow[:, 0]
        names = ("ld_c z_set st_z ld_s ld_d lg_ready sc_ready own mask_ready rank_ready slots_ready st_slot eb_ready st_eb ld_back "
                 "h_ready h_taken st_h0 st_h1 g_ready u_ready sg_ready act_ready d_ready d_taken tq")
        (ld_c, z_set, st_z, ld_s, ld_d, lg_ready, sc_ready, own, mask_ready, rank_ready, slots_ready, st_slot, eb_ready, st_eb,
         ld_back, h_ready, h_taken, st_h0, st_h1, g_ready, u_ready, sg_ready, act_ready, d_ready, d_taken, tq) = (
            s.sem(n) for n in names.split())
        st_h = [st_h0, st_h1]
        block = s.block()
        rowtok, ebd = k.scratch["rowtok"], k.scratch["ebd"]

        @block.sync
        def _(sp):
            for dst, src in ((wr, "w_router"), (bias, "router_bias"), (lower, "lower_groups"), (causal, "causal"),
                             (pidx, "pidx"), (tokid, "tokid")):
                sp.dma_start(dst[:], I[src]).then_inc(ld_c, 16)
            sp.wait_ge(z_set, 1)
            sp.dma_start(rowtok.rearrange("(p b) o -> p (b o)", p=P), zero[:]).then_inc(st_z, 16)
            sp.dma_start(wgu[:], I["ws_gu"]).then_inc(ld_s, 16)
            sp.dma_start(wd[:], I["ws_down"]).then_inc(ld_d, 16)
            sp.wait_ge(eb_ready, 1)
            sp.dma_start(ebd[:, :], ebi[:]).then_inc(st_eb, 16)
            sp.wait_ge(st_eb, 16)
            sp.dma_start(k.eb[:], ebd.rearrange("p o -> o p")).then_inc(ld_back, 16)
            sp.wait_ge(st_slot, 16 * NTT * TOPK)
            sp.dma_start(k.idx[:], rowtok.rearrange("(p b) o -> p (b o)", p=P)).then_inc(ld_back, 16)
            sp.wait_ge(ld_back, 32)

        @block.gpsimd
        def _(pool):
            pool.memset(zero[:], 0).then_inc(z_set, 1)
            pool.wait_ge(st_z, 16)
            pool.wait_ge(slots_ready, 1)
            for i in range(NTT):
                for j in range(TOPK):
                    pool.indirect_dma_start(rowtok, bass.IndirectOffsetOnAxis(ap=k.slot[:, i, j:j + 1], axis=0),
                                            tokid[:, i:i + 1], None).then_inc(st_slot, 16)
            pool.wait_ge(st_slot, 16 * NTT * TOPK)

        @block.scalar
        def _(act):
            act.wait_ge(lg_ready, 1)
            act.activation(sc[:].rearrange("p a e -> p (a e)"), k.ps[:, 0, :], ACT.Sigmoid).then_inc(sc_ready, 1)
            for i in range(NTT):
                act.wait_ge(h_ready, i + 1)
                if i >= 2:
                    act.wait_ge(st_h[i % 2], 16 * (i // 2))
                act.activation(hrow[:, i % 2, :], banks(k, 2 + 2 * (i % 2)), ACT.Copy).then_inc(h_taken, 1)
                act.wait_ge(h_taken, i + 1)
                act.dma_start(k.scratch["hrow"][i * P:(i + 1) * P, :], hrow[:, i % 2, :]).then_inc(st_h[i % 2], 16)
            for f in range(2):
                act.wait_ge(g_ready, f + 1)
                if f:
                    act.wait_ge(act_ready, f)
                act.wait_ge(st_h[0], 16 * NTT // 2)
                act.activation(sg, banks(k, 2), ACT.Sigmoid).then_inc(sg_ready, 1)
                act.wait_ge(sg_ready, 2 * f + 1)
                act.activation(aT[:, f], banks(k, 2), ACT.Copy).then_inc(sg_ready, 1)
            for i in range(NTT):
                act.wait_ge(d_ready, i + 1)
                act.activation(acc[:, i], banks(k, 2 + 2 * (i % 2)), ACT.Copy).then_inc(d_taken, 1)
            for b in range(2):
                act.wait_ge(st_h[b], 16 * NTT // 2)

        @block.vector
        def _(dve):
            mine = Steps(dve, own)

            def tt(out, a, b, op):
                mine.do(dve.tensor_tensor(out, a, b, op))

            dve.wait_ge(ld_c, 96)
            dve.wait_ge(sc_ready, 1)
            tt(bi[:], sc[:], bias[:].unsqueeze(1).to_broadcast([P, NTT, NE]), ALU.add)
            b8 = bi[:].rearrange("p t (g n) -> p (t g) n", g=NG)
            def f4(x, a, b):
                return x[:].rearrange("p t g n -> p (t g) n")[:, :, a:b]
            tt(f4(u1, 0, 4), b8[:, :, 0:4], b8[:, :, 4:8], ALU.max)
            tt(f4(u2, 0, 4), b8[:, :, 0:4], b8[:, :, 4:8], ALU.min)
            for m in (2, 1):
                tt(f4(v1, 0, m), f4(u1, 0, m), f4(u1, m, 2 * m), ALU.max)
                tt(f4(v2, 0, m), f4(u1, 0, m), f4(u1, m, 2 * m), ALU.min)
                tt(f4(v3, 0, m), f4(u2, 0, m), f4(u2, m, 2 * m), ALU.max)
                tt(f4(u2, 0, m), f4(v2, 0, m), f4(v3, 0, m), ALU.max)
                mine.do(dve.tensor_copy(f4(u1, 0, m), f4(v1, 0, m)))
            tt(gs[:].rearrange("p t g -> p (t g)").unsqueeze(2), f4(u1, 0, 1), f4(u2, 0, 1), ALU.add)
            full = [P, NTT, NG, NG]
            other, self_ = gs[:].unsqueeze(2).to_broadcast(full), gs[:].unsqueeze(3).to_broadcast(full)
            tt(cmp[:], other, self_, ALU.is_equal)
            tt(cmp[:], cmp[:], lower[:].unsqueeze(1).to_broadcast(full), ALU.mult)
            tt(cmp2, other, self_, ALU.is_gt)
            tt(cmp[:], cmp[:], cmp2, ALU.add)
            mine.do(dve.tensor_reduce(gm[:], cmp[:], AX, ALU.add))
            mine.do(dve.tensor_scalar(gm[:], gm[:], float(TOPG), None, ALU.is_lt))
            g64 = gm[:].rearrange("p t g -> p (t g)").unsqueeze(2).to_broadcast([P, NTT * NG, 8])
            flat = lambda x: x[:].rearrange("p t (g n) -> p (t g) n", g=NG)
            tt(flat(sel), flat(bi), g64, ALU.mult)
            mine.do(dve.tensor_scalar(gs[:], gm[:], -1.0, BIG, ALU.add, ALU.mult))
            tt(flat(sel), flat(sel), gs[:].rearrange("p t g -> p (t g)").unsqueeze(2).to_broadcast([P, NTT * NG, 8]), ALU.add)
            for i in range(NTT):
                mine.mark(dve.max(top[:, i], sel[:, i]))
            mine.settle()
            for i in range(NTT):
                mine.mark(dve.match_replace(key[:, i], top[:, i], sel[:, i], -3e38))
            mine.settle()
            dve.tensor_scalar(mask[:], key[:], -3e38, None, ALU.is_equal).then_inc(mask_ready, 1)
            dve.wait_ge(mask_ready, 1)
            tt(gate[:], sc[:], mask[:], ALU.mult)
            mine.do(dve.tensor_reduce(tot[:], gate[:], AX, ALU.add))
            mine.do(dve.reciprocal(tot[:], tot[:]))
            mine.do(dve.tensor_scalar(tot[:], tot[:], ROUTED_SCALE, None, ALU.mult))
            tt(gate[:], gate[:], tot[:].unsqueeze(2).to_broadcast([P, NTT, NE]), ALU.mult)
            dve.wait_ge(rank_ready, 1)
            mine.do(dve.tensor_copy(ci[:], k.ps[:, 7, 0:NE]))
            mine.do(dve.tensor_scalar(ci[:], ci[:], P - 1, None, ALU.add))
            mine.do(dve.tensor_scalar(ci[:], ci[:], 7, None, ALU.arith_shift_right))
            mine.do(dve.tensor_copy(nb[:], ci[:]))
            mine.do(dve.tensor_tensor_scan(end[:], k.ones[:, 0:NE], nb[:], 0.0, ALU.mult, ALU.add))
            tt(nb[:], end[:], nb[:], ALU.subtract)
            mine.do(dve.tensor_scalar(k.nr[:], end[0:1, NE - 1:NE], 1.0, None, ALU.add))
            mine.do(dve.tensor_scalar(k.nr[:], k.nr[:], 1, None, ALU.arith_shift_right))
            mine.do(dve.tensor_scalar(k.nr[:], k.nr[:], -(NE // 2), None, ALU.add))
            mine.do(dve.tensor_copy(ri[:], k.ps[:, 6, :]))
            mine.do(dve.tensor_scalar(qi[:], ri[:], 7, None, ALU.arith_shift_right))
            mine.do(dve.tensor_scalar(ri[:], ri[:], P - 1, None, ALU.bitwise_and))
            fl = lambda x: x[:].rearrange("p t e -> p (t e)")
            mine.do(dve.tensor_copy(fl(key), ri[:]))
            mine.do(dve.tensor_copy(fl(sel), qi[:]))
            mine.do(dve.scalar_tensor_tensor(fl(key), fl(key), float(NBLK), fl(sel), ALU.mult, ALU.add))
            tt(key[:], key[:], nb[:].unsqueeze(1).to_broadcast([P, NTT, NE]), ALU.add)
            tt(key[:], key[:], mask[:], ALU.mult)
            tt(key[:], key[:], mask[:], ALU.add)
            mine.do(dve.tensor_scalar(key[:], key[:], -1.0, None, ALU.add))
            for i in range(NTT):
                mine.mark(dve.max(slotv[:, i], key[:, i]))
            mine.settle()
            dve.tensor_copy(k.slot[:], slotv[:]).then_inc(slots_ready, 1)
            for i in range(NTT):
                tt(pick[:], key[:, i:i + 1, :].to_broadcast([P, 8, NE]), slotv[:, i].unsqueeze(2).to_broadcast([P, 8, NE]), ALU.is_equal)
                tt(pick[:], pick[:], gate[:, i:i + 1, :].to_broadcast([P, 8, NE]), ALU.mult)
                mine.do(dve.tensor_reduce(k.gates[:, i], pick[:], AX, ALU.add))
            mine.do(dve.tensor_scalar(end[:], end[:], pidx[:, 0:1], None, ALU.is_le))
            mine.do(dve.tensor_reduce(ebf[:], end[:], AX, ALU.add))
            mine.do(dve.tensor_scalar(ebf[:], ebf[:], float(NE - 1), None, ALU.min))
            dve.tensor_copy(ebi[:], ebf[:]).then_inc(eb_ready, 1)
            for f in range(2):
                dve.wait_ge(sg_ready, 2 * f + 2)
                tt(aT[:, f], aT[:, f], sg, ALU.mult)
                dve.wait_ge(u_ready, f + 1)
                dve.tensor_tensor(aT[:, f], aT[:, f], banks(k, 4), ALU.mult).then_inc(act_ready, 1)

        @block.tensor
        def _(pe):
            pe.wait_ge(ld_c, 96)
            for i in range(NTT):
                for t in range(KT):
                    mm = pe.matmul(k.ps[:, 0, i * NE:(i + 1) * NE], k.hT2[:, t, i * P:(i + 1) * P], wr[:, t, :],
                                   start=(t == 0), stop=(t == KT - 1))
            mm.then_inc(lg_ready, 1)
            for i in range(NTT):
                if i >= 2:
                    pe.wait_ge(h_taken, i - 1)
                for t in range(KT):
                    tr = pe.transpose(k.ps[:, 2 + 2 * (i % 2) + t // 4, (t % 4) * P:(t % 4 + 1) * P],
                                      k.hT2[:, t, i * P:(i + 1) * P], k.eye[:])
                tr.then_inc(h_ready, 1)
            pe.wait_ge(mask_ready, 1)
            for i in range(NTT):
                for m in range(i):
                    pe.matmul(k.ps[:, 6, i * NE:(i + 1) * NE], k.ones[:], mask[:, m], start=(m == 0), stop=False)
                pe.matmul(k.ps[:, 6, i * NE:(i + 1) * NE], causal[:], mask[:, i], start=(i == 0), stop=True)
            for i in range(NTT):
                mm = pe.matmul(k.ps[:, 7, 0:NE], k.ones[:], mask[:, i], start=(i == 0), stop=(i == NTT - 1))
            mm.then_inc(rank_ready, 1)
            pe.wait_ge(h_taken, NTT)
            pe.wait_ge(ld_s, 16)
            for f in range(2):
                if f:
                    pe.wait_ge(act_ready, f)
                for m in range(2):
                    for half in range(2):
                        for t in range(KT):
                            mm = pe.matmul(k.ps[:, 2 + 2 * m + half, :], wgu[:, m, f, t, :],
                                           k.hT2[:, t, half * HALF:(half + 1) * HALF], start=(t == 0), stop=(t == KT - 1))
                    mm.then_inc((g_ready, u_ready)[m], 1)
            pe.wait_ge(act_ready, 2)
            pe.wait_ge(ld_d, 16)
            for i in range(NTT):
                if i >= 2:
                    pe.wait_ge(d_taken, i - 1)
                for half in range(2):
                    for f in range(2):
                        mm = pe.matmul(k.ps[:, 2 + 2 * (i % 2) + half, :], aT[:, f, i * P:(i + 1) * P],
                                       wd[:, f, half * HALF:(half + 1) * HALF], start=(f == 0), stop=(f == 1))
                mm.then_inc(d_ready, 1)


def experts(k):
    nc, I = k.nc, k.I
    with Stage(k, "exp") as s:
        gu, wd = s.sb("gu", [P, 2, KT, 2 * DE]), s.sb("wd", [P, 2, 2, D])
        x, y = k.hT2[:, 0:2], k.hT2[:, 4:6]
        xT = k.hT2[:, 2:4].rearrange("p u (t n) -> p u t n", t=KT)
        idx = s.sb("idx", [P, 2], I32)
        sg, a = s.sb("sg", [P, 2, DE]), s.sb("a", [P, 2, DE])
        aT = s.sb("aT", [P, 2, P])
        ld_gu, ld_wd, ld_x, st_y = ([s.sem(f"{n}{b}") for b in range(2)] for n in ("ld_gu", "ld_wd", "ld_x", "st_y"))
        names = ("idx_ready xtr_ready xt_act xt_dve gu_ready sg_ready sgg_ready act_ready atr_ready at_taken down_ready y_act y_dve")
        (idx_ready, xtr_ready, xt_act, xt_dve, gu_ready, sg_ready, sgg_ready, act_ready, atr_ready, at_taken, down_ready,
         y_act, y_dve) = (s.sem(n) for n in names.split())
        block = s.block()
        yrow = k.scratch["yrow"].rearrange("(p b) n -> p b n", p=P)
        hrow = k.scratch["hrow"]

        @block.sync
        def _(sp):
            for i, last in used_rounds(sp, k):
                for u in range(2):
                    b = i * 2 + u
                    e = sp.value_load(k.eb[0:1, b:b + 1] if isinstance(b, int) else k.eb[0:1, bass.ds(b, 1)],
                                      min_val=0, max_val=NE - 1)
                    wait(sp, gu_ready, b - 1)
                    sp.dma_start(gu[:, u], I["w_gu"][e]).then_inc(ld_gu[u], 16)
                    wait(sp, down_ready, b - 1)
                    sp.dma_start(wd[:, u], I["w_down"][e]).then_inc(ld_wd[u], 16)

        @block.gpsimd
        def _(pool):
            copied, following = pool.alloc_register("copied"), pool.alloc_register("following")
            pool.reg_mov(following, 1)
            for i, last in used_rounds(pool, k):
                for u in range(2):
                    b = i * 2 + u
                    wait(pool, ld_x[u], i * 16, 16)
                    wait(pool, xtr_ready, b - 1)
                    pool.tensor_copy(idx[:, u:u + 1], k.idx[:, bass.ds(b, 1)]).then_inc(idx_ready, 1)
                    pool.reg_mov(copied, following)
                    pool.wait_ge(idx_ready, copied)
                    pool.reg_add(following, copied, 1)
                    pool.indirect_dma_start(x[:, u, :], None, hrow, bass.IndirectOffsetOnAxis(ap=idx[:, u:u + 1], axis=0))\
                        .then_inc(ld_x[u], 16)
            pool.reg_sub(copied, following, 1)
            pool.wait_ge(idx_ready, copied)
            for u in range(2):
                wait(pool, st_y[u], i * 16 + 16, 16)

        def turned(eng, b, u, half, put, signal):
            wait(eng, xtr_ready, b + 1)
            wait(eng, gu_ready, b - 1)
            put(xT[:, u, 4 * half:4 * half + 4, :].rearrange("p t n -> p (t n)"), k.ps[:, half, :]).then_inc(signal, 1)

        def outputs(eng, i, b, u, half, put, signal):
            wait(eng, down_ready, b + 1)
            wait(eng, st_y[u], i * 16, 16)
            put(y[:, u, half * HALF:(half + 1) * HALF], k.ps[:, 4 + half, :]).then_inc(signal, 1)

        @block.scalar
        def _(act):
            def put(o, i):
                return act.activation(o, i, ACT.Copy)

            def turn_a(b):
                wait(act, atr_ready, b + 1)
                wait(act, down_ready, b)
                put(aT[:].rearrange("p f n -> p (f n)"), k.ps[:, 3, 0:DE]).then_inc(at_taken, 1)

            def store(i, b, u):
                outputs(act, i, b, u, 0, put, y_act)
                wait(act, y_act, b + 1)
                wait(act, y_dve, b + 1)
                act.dma_start(yrow[:, bass.ds(b, 1), :], y[:, u:u + 1, :]).then_inc(st_y[u], 16)

            turned(act, 0, 0, 0, put, xt_act)
            for i, last in used_rounds(act, k):
                for u in range(2):
                    b = i * 2 + u
                    if not (isinstance(b, int) and b == 0):
                        turn_a(b - 1)
                    wait(act, gu_ready, b + 1)
                    wait(act, act_ready, b - 1)
                    act.activation(sg[:, u], k.ps[:, 2 if u == 0 else 6, 0:DE], ACT.Sigmoid).then_inc(sg_ready, 1)
                    if not (last and u):
                        turned(act, b + 1, 1 - u, 0, put, xt_act)
                    if not (isinstance(b, int) and b == 0):
                        store(i if u else i - 1, b - 1, 1 - u)
            turn_a(b)
            store(i, b, 1)

        @block.vector
        def _(dve):
            def put(o, i):
                return dve.tensor_copy(o, i)

            turned(dve, 0, 0, 1, put, xt_dve)
            for i, last in used_rounds(dve, k):
                for u in range(2):
                    b = i * 2 + u
                    g = k.ps[:, 2 if u == 0 else 6, :]
                    wait(dve, sg_ready, b + 1)
                    dve.tensor_tensor(sg[:, u], sg[:, u], g[:, 0:DE], ALU.mult).then_inc(sgg_ready, 1)
                    wait(dve, sgg_ready, b + 1)
                    wait(dve, atr_ready, b - 1)
                    dve.tensor_tensor(a[:, u], sg[:, u], g[:, DE:2 * DE], ALU.mult).then_inc(act_ready, 1)
                    if not (last and u):
                        turned(dve, b + 1, 1 - u, 1, put, xt_dve)
                    if not (isinstance(b, int) and b == 0):
                        outputs(dve, i if u else i - 1, b - 1, 1 - u, 1, put, y_dve)
            outputs(dve, i, b, 1, 1, put, y_dve)

        @block.tensor
        def _(pe):
            def turn_x(i, b, u):
                wait(pe, ld_x[u], i * 16 + 16, 16)
                wait(pe, xt_act, b)
                wait(pe, xt_dve, b)
                for t in range(KT):
                    tr = pe.transpose(k.ps[:, t // 4, (t % 4) * P:(t % 4 + 1) * P], x[:, u, t * P:(t + 1) * P], k.eye[:])
                tr.then_inc(xtr_ready, 1)

            def turn_a(b, u):
                wait(pe, act_ready, b + 1)
                wait(pe, at_taken, b)
                for f in range(2):
                    tr = pe.transpose(k.ps[:, 3, f * P:(f + 1) * P], a[:, u, f * P:(f + 1) * P], k.eye[:])
                tr.then_inc(atr_ready, 1)

            def down(i, b, u):
                wait(pe, at_taken, b + 1)
                wait(pe, ld_wd[u], i * 16 + 16, 16)
                wait(pe, y_act, b)
                wait(pe, y_dve, b)
                for half in range(2):
                    for f in range(2):
                        mm = pe.matmul(k.ps[:, 4 + half, :], aT[:, f, :], wd[:, u, f, half * HALF:(half + 1) * HALF],
                                       start=(f == 0), stop=(f == 1))
                mm.then_inc(down_ready, 1)

            turn_x(0, 0, 0)
            for i, last in used_rounds(pe, k):
                for u in range(2):
                    b = i * 2 + u
                    first = isinstance(b, int) and b == 0
                    if not first:
                        turn_a(b - 1, 1 - u)
                    wait(pe, xt_act, b + 1)
                    wait(pe, xt_dve, b + 1)
                    wait(pe, ld_gu[u], i * 16 + 16, 16)
                    wait(pe, act_ready, b - 1)
                    for t in range(KT):
                        mm = pe.matmul(k.ps[:, 2 if u == 0 else 6, :], xT[:, u, t, :], gu[:, u, t, :],
                                       start=(t == 0), stop=(t == KT - 1))
                    mm.then_inc(gu_ready, 1)
                    if not (last and u):
                        turn_x(i + 1 if u else i, b + 1, 1 - u)
                    if not first:
                        down(i if u else i - 1, b - 1, 1 - u)
            turn_a(b, 1)
            down(i, b, 1)


def combine(k):
    nc, I = k.nc, k.I
    acc = k.mix
    NBUF = 6
    with Stage(k, "comb") as s:
        y = s.sb("y", [P, NBUF, D])
        fg, rstd = s.sb("fg", [P, KT]), s.sb("rstd", [P, T])
        ld_y = [s.sem(f"ld_y{b}") for b in range(NBUF)]
        names = "ld_g summed turned x_ready sq_ready ss_ready own_a rstd_ready o_ready st_o"
        (ld_g, summed, turned, x_ready, sq_ready, ss_ready, own_a, rstd_ready, o_ready, st_o) = (s.sem(n) for n in names.split())
        block = s.block()

        @block.sync
        def _(sp):
            sp.dma_start(fg[:], I["final_g"]).then_inc(ld_g, 16)
            for j in range(KT):
                sp.wait_ge(o_ready, j + 1)
                sp.dma_start(k.out[j], k.hT2[:, j]).then_inc(st_o, 16)
            sp.wait_ge(st_o, 16 * KT)

        @block.gpsimd
        def _(pool):
            for i in range(NTT):
                for j in range(TOPK):
                    n = i * TOPK + j
                    if n >= NBUF:
                        pool.wait_ge(summed, n - NBUF + 1)
                    pool.indirect_dma_start(y[:, n % NBUF, :], None, k.scratch["yrow"],
                                            bass.IndirectOffsetOnAxis(ap=k.slot[:, i, j:j + 1], axis=0)).then_inc(ld_y[n % NBUF], 16)

        @block.vector
        def _(dve):
            def to_residual(i):
                dve.wait_ge(turned, i + 1)
                for t in range(KT):
                    ins = dve.scalar_tensor_tensor(k.xT[:, t, i * P:(i + 1) * P], k.ps[:, 2 * (i % 2) + t // 4, (t % 4) * P:(t % 4 + 1) * P],
                                                   k.cond[:, C2 + 5 * KT + t, 1:2], k.xT[:, t, i * P:(i + 1) * P], ALU.mult, ALU.add)
                ins.then_inc(x_ready, 1)

            for i in range(NTT):
                for j in range(TOPK):
                    n = i * TOPK + j
                    dve.wait_ge(ld_y[n % NBUF], 16 * (n // NBUF + 1))
                    if j:
                        dve.wait_ge(summed, n)
                    dve.scalar_tensor_tensor(acc[:, i], y[:, n % NBUF, :], k.gates[:, i, j:j + 1], acc[:, i],
                                             ALU.mult, ALU.add).then_inc(summed, 1)
                if i:
                    to_residual(i - 1)
            to_residual(NTT - 1)
            dve.wait_ge(ld_g, 16)
            dve.wait_ge(rstd_ready, 1)
            dve.wait_ge(x_ready, NTT)
            for j in range(KT):
                dve.scalar_tensor_tensor(k.hT2[:, j], k.xT[:, j], fg[:, j:j + 1], rstd[:], ALU.mult, ALU.mult).then_inc(o_ready, 1)

        @block.tensor
        def _(pe):
            for i in range(NTT):
                pe.wait_ge(summed, (i + 1) * TOPK)
                if i >= 2:
                    pe.wait_ge(x_ready, i - 1)
                for t in range(KT):
                    tr = pe.transpose(k.ps[:, 2 * (i % 2) + t // 4, (t % 4) * P:(t % 4 + 1) * P], acc[:, i, t * P:(t + 1) * P], k.eye[:])
                tr.then_inc(turned, 1)
            for j in range(KT):
                pe.wait_ge(sq_ready, j + 1)
                for half in range(2):
                    mm = pe.matmul(k.ps[:, 4 + half, :], k.ones[:], k.hT2[:, j, half * HALF:(half + 1) * HALF],
                                   start=(j == 0), stop=(j == KT - 1))
            mm.then_inc(ss_ready, 1)

        @block.scalar
        def _(act):
            act.wait_ge(x_ready, NTT)
            for j in range(KT):
                act.activation(k.hT2[:, j], k.xT[:, j], ACT.Square).then_inc(sq_ready, 1)
            act.wait_ge(ss_ready, 1)
            act.activation(rstd[:], banks(k, 4), ACT.Ln, scale=1.0 / D, bias=EPS).then_inc(own_a, 1)
            act.wait_ge(own_a, 1)
            act.activation(rstd[:], rstd[:], ACT.Exp, scale=-0.5).then_inc(rstd_ready, 1)


def program(nc, I, out):
    with ExitStack() as ctx:
        scratch = {
            "proj": nc.dram_tensor("proj", (NSCAN, P, T), F32).ap(),
            "vfirst": nc.dram_tensor("vfirst", (PAIRS, P, T), F32).ap(),
            "rowtok": nc.dram_tensor("rowtok", (NBLK * P, 1), I32).ap(),
            "ebd": nc.dram_tensor("ebd", (NBLK, 1), I32).ap(),
            "hrow": nc.dram_tensor("hrow", (T, D), F32).ap(),
            "yrow": nc.dram_tensor("yrow", (NBLK * P, D), F32).ap(),
        }
        k = Kernel(nc, I, out, ctx, scratch)
        modulation(k)
        for l in range(L):
            projection(k, l)
            hgrn(k, l)
            rwkv(k, l)
            merge(k, l)
        k.second_block()
        with Stage(k, "ctx") as s:
            ctxT, hcT = s.sb("ctxT", [P, KT, CTX]), s.sb("hcT", [P, KT, CTX])
            ld = s.sem("ld")
            with nc.Block() as block:
                @block.sync
                def _(sp):
                    sp.dma_start(ctxT[:], I["ctxT"]).then_inc(ld, 16)
                    sp.wait_ge(ld, 16)
            rms_modulated(k, "norm1", [(k.xT, k.hT2, T, 0, C2, 1), (ctxT, hcT, CTX, 0, C2, 2)])
            attention(k, hcT)
        pooling(k)
        project_out(k)
        rms_modulated(k, "norm2", [(k.xT, k.hT2, T, 1, C2 + 3 * KT, 1)])
        route(k)
        experts(k)
        combine(k)


def slabs(w):
    kk, n = w.shape
    return np.ascontiguousarray(w.reshape(kk // 128, 128, n // 128, 128).transpose(2, 1, 0, 3))


def cols(v):
    return np.ascontiguousarray(np.swapaxes(v.reshape(v.shape[:-1] + (-1, 128)), -1, -2))


def lay_projection(i):
    o = {}
    o["xT"] = np.ascontiguousarray(i["x"][0].T).reshape(8, 128, 1024)
    o["c3"] = np.ascontiguousarray(np.stack([cols(i["c"][0]), cols(i["c_2"][0]), cols(i["c_ctx_2"])], -1))
    o["w_ada"] = np.concatenate([slabs(i["w_ada"][0]), slabs(i["w_ada"][1]), slabs(i["w_ada_2"][0])])
    o["b_ada"] = np.concatenate([cols(i["b_ada"][0]), cols(i["b_ada"][1]), cols(i["b_ada_2"][0])], -1)
    o["w_in"] = np.stack([slabs(w) for w in i["w_in"]])
    o["v_down"] = np.zeros((128, 8, 128), np.float32)
    o["v_down"][:, :, 0:32] = i["rw_v_down"][0].reshape(8, 128, 32).transpose(1, 0, 2)
    return o


def lay_hgrn(i, o):
    b = cols(i["hg_lower_bounds"])
    g = cols(i["hg_norm_g"])
    o["hg_par"] = np.ascontiguousarray(np.stack([np.stack([b[0], b[1], g[l]], -1) for l in range(2)]))
    s, t = np.meshgrid(np.arange(128), np.arange(128), indexing="ij")
    ms = [((s // (2*m) == t // (2*m)) & ((s // m) % 2 == 0) & ((t // m) % 2 == 1)) for m in (64,32,16,8,4,2,1)] + [s == t]
    o["level_masks"] = np.ascontiguousarray(np.stack(ms, 1).astype(np.int32))
    return o


def lay_rwkv(i, o):
    L = 2
    mu = i["rw_mu"]
    W = 512
    z = np.zeros((W,), np.float32)
    par = []
    for l in range(L):
        c = [mu[l, n * W:(n + 1) * W] for n in range(4)] + [i["rw_w0"][l], i["rw_a0"][l], i["rw_k_k"][l], i["rw_k_a"][l],
             i["rw_r_k"][l].reshape(-1), i["rw_gn_g"][l], i["rw_gn_b"][l], i["rw_v0"][l - 1] if l else z,
             np.tile(mu[l, 4 * W:], 4)]
        par.append(np.stack([cols(v) for v in c], -1))
    o["rw_par"] = np.ascontiguousarray(np.stack(par))
    o["rw_lora"] = np.stack([slabs(np.concatenate([i["rw_w_up"][l], i["rw_a_up"][l]]))[:, :, 0] for l in range(L)])
    o["v_up"] = np.ascontiguousarray(i["rw_v_up"][0].reshape(32, 4, 128).transpose(1, 0, 2))
    s, t = np.meshgrid(np.arange(128), np.arange(128), indexing="ij")
    o["causal_masks"] = np.stack([s < t, s <= t], 1).astype(np.float32)
    pm = [((s // (2*m) == t // (2*m)) & ((s // m) % 2 == 0) & ((t // m) % 2 == 1)) for m in (1,2,4,8,16,32,64)]
    o["pair_masks"] = np.stack(pm, 1).astype(np.float32)
    o["pair_mask_t"] = np.ascontiguousarray(pm[0].T.astype(np.float32))
    return o


def lay_merge(i, o):
    o["w_branch_hg"] = np.stack([slabs(w) for w in i["w_branch_hg"]])
    o["w_branch_rw"] = np.stack([slabs(w) for w in i["w_branch_rw"]])
    o["w_out"] = np.stack([slabs(w) for w in i["w_out"]])
    o["ln_par"] = np.ascontiguousarray(np.stack([cols(i["ln_g"]), cols(i["ln_b"])], 2))
    return o


def lay_attention(i, o):
    perm = np.concatenate([np.r_[j*64:(j+1)*64, (4+j)*64:(5+j)*64] for j in range(4)])
    w = i["w_in_2"][0]
    cp = np.concatenate([perm, np.arange(512, 1280)])
    o["w_in2"] = slabs(w[:, cp])
    rp = np.concatenate([perm, np.arange(512, 1024)])
    o["w_out2"] = slabs(i["w_out_2"][0][rp])
    o["ctxT"] = np.ascontiguousarray(i["ctx_2"][0].T.reshape(8, 128, 256).transpose(1, 0, 2))
    o["norm_g"] = np.ascontiguousarray(np.stack([cols(i["norm1_g_2"][0]), cols(i["norm2_g_2"][0])], 1))
    p = np.arange(128) % 64
    fr = (np.float32(10000.0) ** (-np.arange(16, dtype=np.float32) / np.float32(16)))
    t = np.arange(1024)
    pos = np.where((p < 32)[:, None], (t // 64)[None], (t % 64)[None]).astype(np.float32)
    ang = pos * fr[p % 16][:, None]
    o["cos"], o["sin"] = np.cos(ang), np.sin(ang)
    rot = np.zeros((128, 128), np.float32)
    for m in range(128):
        if m % 32 < 16: rot[m + 16, m] = -1
        else: rot[m - 16, m] = 1
    o["rot"] = rot
    a, b = np.meshgrid(np.arange(128), np.arange(384), indexing="ij")
    o["band"] = np.where(np.abs(a + 128 - b) <= 128, 0, -1e30).astype(np.float32)
    sk = i["attn_sink_2"][0]
    o["sink"] = np.ascontiguousarray(np.tile(np.stack([sk[0:4], sk[4:8]], 1)[None], (128, 1, 1)))
    o["pool_w"] = np.ascontiguousarray(i["pool_w_2"][0].transpose(1, 0, 2))
    inv = np.zeros((4, 1024), np.float32)
    for g, w_ in enumerate((2, 4, 8, 16)):
        lo = np.clip(t - w_ // 2, 0, 1024); hi = np.clip(t - w_ // 2 + w_, 0, 1024)
        inv[g] = 1 / (hi - lo).astype(np.float32)
    o["pool_inv"] = np.ascontiguousarray(np.tile(inv[None], (128, 1, 1)))
    o["pool_scale"] = cols(i["pool_scale_2"][0])
    return o


def lay_experts(i, o):
    o["w_router"] = np.ascontiguousarray(i["w_router_2"][0].reshape(8, 128, 64).transpose(1, 0, 2))
    o["router_bias"] = np.ascontiguousarray(np.tile(i["router_bias_2"][0][None], (128, 1)))
    a, b = np.meshgrid(np.arange(8), np.arange(8), indexing="ij")
    o["lower_groups"] = np.ascontiguousarray(np.tile((b < a).astype(np.float32)[None], (128, 1, 1)))
    s, t = np.meshgrid(np.arange(128), np.arange(128), indexing="ij")
    o["causal"] = (s < t).astype(np.float32)
    o["pidx"] = np.arange(128, dtype=np.float32)[:, None].copy()
    o["tokid"] = np.ascontiguousarray((np.arange(128)[:, None] + 128 * np.arange(8)[None]).astype(np.int32))
    o["ws_gu"] = np.ascontiguousarray(np.stack([slabs(i["ws_gate_2"][0]), slabs(i["ws_up_2"][0])]).transpose(2, 0, 1, 3, 4))
    o["ws_down"] = np.ascontiguousarray(i["ws_down_2"][0].reshape(2, 128, 1024).transpose(1, 0, 2))
    g, u = i["w_gate_2"][0], i["w_up_2"][0]
    o["w_gu"] = np.ascontiguousarray(np.concatenate([g, u], -1).reshape(64, 8, 128, 512).transpose(0, 2, 1, 3))
    o["w_down"] = np.ascontiguousarray(i["w_down_2"][0].reshape(64, 2, 128, 1024).transpose(0, 2, 1, 3))
    o["final_g"] = cols(i["final_g_2"])
    return o


def kernel(**inputs):
    import concourse.bacc as bacc
    from concourse.bass_utils import run_bass_kernel_spmd

    i = {n: np.asarray(a) for n, a in inputs.items()}
    o = lay_projection(i)
    for part in (lay_hgrn, lay_rwkv, lay_merge, lay_attention, lay_experts):
        part(i, o)
    nc = bacc.Bacc("TRN2", target_bir_lowering=False, num_devices=1)
    arrays, aps = {}, {}
    for name, a in o.items():
        arrays[f"in_{name}_dram"] = a = np.ascontiguousarray(a)
        aps[name] = nc.dram_tensor(f"in_{name}_dram", a.shape, mybir.dt.from_np(a.dtype), kind="ExternalInput").ap()
    out = nc.dram_tensor("out_0_dram", (KT, P, T), F32, kind="ExternalOutput").ap()
    program(nc, aps, out)
    r = run_bass_kernel_spmd(nc, [arrays], core_ids=[0])
    return np.ascontiguousarray(r.results[0]["out_0_dram"].reshape(D, T).T)[None]
```
